# Optimizing a Trainium2 kernel written in Bass

```python
import jax, jax.numpy as jnp
from jax import lax
import numpy as np

D_MODEL = 1024
BATCH = 1
SEQ = 1024
DEPTH = 1

MIX_WIDTH = D_MODEL
CONV_WIDTH = MIX_WIDTH // 2
CONV_GROUPS = 8
CONV_K = 3
RET_WIDTH = MIX_WIDTH - CONV_WIDTH
RET_HEADS = 4
RET_HEAD_DIM = RET_WIDTH // RET_HEADS
RET_CHUNK = 128
ROPE_BASE = 10000.0
D_FF = 4 * D_MODEL
NORM_EPS = 1e-6
IN_COLS = 3 * CONV_WIDTH + 4 * RET_WIDTH


def rms_norm(x, g, eps=NORM_EPS):
    xf = x.astype(jnp.float32)
    y = xf * lax.rsqrt(jnp.mean(xf * xf, axis=-1, keepdims=True) + eps)
    return (y * g.astype(jnp.float32)).astype(x.dtype)

def group_rms_norm(x, g, n_groups, eps=NORM_EPS):
    shp = x.shape
    xg = x.reshape(shp[:-1] + (n_groups, shp[-1] // n_groups)).astype(jnp.float32)
    y = xg * lax.rsqrt(jnp.mean(xg * xg, axis=-1, keepdims=True) + eps)
    return (y.reshape(shp) * g.astype(jnp.float32)).astype(x.dtype)

def rotary(x, positions):
    half = x.shape[-1] // 2
    inv_freq = 1.0 / (ROPE_BASE ** (jnp.arange(half, dtype=jnp.float32) / half))
    ang = positions.astype(jnp.float32)[:, None] * inv_freq[None, :]
    cos = jnp.cos(ang)[None, :, None, :].astype(x.dtype)
    sin = jnp.sin(ang)[None, :, None, :].astype(x.dtype)
    x1, x2 = x[..., :half], x[..., half:]
    return jnp.concatenate([x1 * cos - x2 * sin, x2 * cos + x1 * sin], axis=-1)

def causal_dwconv3(u, w):
    up = jnp.pad(u, ((0, 0), (CONV_K - 1, 0), (0, 0)))
    s = u.shape[1]
    return up[:, 0:s] * w[0] + up[:, 1:s + 1] * w[1] + up[:, 2:s + 2] * w[2]

def chunkwise_retention(q, k, v):
    b, s, h, d = q.shape
    nc = s // RET_CHUNK
    dt = q.dtype
    to_chunks = lambda t: t.reshape(b, nc, RET_CHUNK, h, d).transpose(0, 3, 1, 2, 4)
    qc, kc, vc = to_chunks(q), to_chunks(k), to_chunks(v)

    log_gamma = jnp.log(1.0 - 2.0 ** (-5.0 - jnp.arange(h, dtype=jnp.float32)))
    idx = jnp.arange(RET_CHUNK, dtype=jnp.float32)
    diff = idx[:, None] - idx[None, :]
    intra_decay = jnp.where(diff[None] >= 0,
                            jnp.exp(log_gamma[:, None, None] * jnp.maximum(diff, 0.0)[None]),
                            0.0).astype(dt)
    zeta = jnp.exp(log_gamma[:, None] * (RET_CHUNK - 1 - idx)[None]).astype(dt)
    xi = jnp.exp(log_gamma[:, None] * (idx + 1.0)[None]).astype(dt)
    chunk_decay = jnp.exp(log_gamma * RET_CHUNK).astype(dt)

    scores = jnp.einsum('bhncd,bhnmd->bhncm', qc, kc) * intra_decay[None, :, None]
    o_intra = jnp.einsum('bhncm,bhnme->bhnce', scores, vc)

    kv = jnp.einsum('bhnmd,bhnme->nbhde', kc * zeta[None, :, None, :, None], vc)

    def step(state, kv_n):
        new_state = chunk_decay[None, :, None, None] * state + kv_n
        return new_state, state

    _, s_prev = lax.scan(step, jnp.zeros_like(kv[0]), kv)
    o_cross = jnp.einsum('bhncd,nbhde->bhnce', qc * xi[None, :, None, :, None], s_prev)

    o = o_intra + o_cross
    return o.transpose(0, 2, 3, 1, 4).reshape(b, s, h, d)

def hybrid_mixer(u, w_in, conv_w, conv_norm_g, ret_norm_g, w_out):
    b, s, _ = u.shape
    z = u @ w_in
    c0 = 3 * CONV_WIDTH
    cb, cc, ch = jnp.split(z[..., :c0], 3, axis=-1)
    rq, rk, rv, rg = jnp.split(z[..., c0:], 4, axis=-1)

    y_conv = cb * causal_dwconv3(cc * ch, conv_w)
    y_conv = group_rms_norm(y_conv, conv_norm_g, CONV_GROUPS)

    positions = jnp.arange(s)
    q = rotary(rq.reshape(b, s, RET_HEADS, RET_HEAD_DIM), positions)
    k = rotary(rk.reshape(b, s, RET_HEADS, RET_HEAD_DIM), positions) * (RET_HEAD_DIM ** -0.5)
    v = rv.reshape(b, s, RET_HEADS, RET_HEAD_DIM)
    o = chunkwise_retention(q, k, v).reshape(b, s, RET_WIDTH)
    y_ret = group_rms_norm(o, ret_norm_g, RET_HEADS) * jax.nn.silu(rg)

    return jnp.concatenate([y_conv, y_ret], axis=-1) @ w_out

def sq_relu_mlp(u, w_up, w_down):
    hdn = jax.nn.relu(u @ w_up)
    return (hdn * hdn) @ w_down

def first_inputs(seed: int = 0) -> dict:
    key = jax.random.key(seed)
    ks = jax.random.split(key, 11)
    f32 = jnp.float32
    x = jax.random.normal(ks[0], (BATCH, SEQ, D_MODEL), f32)
    norm1_g = 1.0 + 0.05 * jax.random.normal(ks[1], (D_MODEL,), f32)
    w_in = jax.random.normal(ks[2], (D_MODEL, IN_COLS), f32) * D_MODEL ** -0.5
    conv_w = jax.random.normal(ks[3], (CONV_K, CONV_WIDTH), f32) * CONV_K ** -0.5
    conv_norm_g = 1.0 + 0.05 * jax.random.normal(ks[4], (CONV_WIDTH,), f32)
    ret_norm_g = 1.0 + 0.05 * jax.random.normal(ks[5], (RET_WIDTH,), f32)
    w_out = jax.random.normal(ks[6], (MIX_WIDTH, D_MODEL), f32) * MIX_WIDTH ** -0.5
    norm2_g = 1.0 + 0.05 * jax.random.normal(ks[7], (D_MODEL,), f32)
    w_up = jax.random.normal(ks[8], (D_MODEL, D_FF), f32) * D_MODEL ** -0.5
    w_down = jax.random.normal(ks[9], (D_FF, D_MODEL), f32) * D_FF ** -0.5
    final_norm_g = 1.0 + 0.05 * jax.random.normal(ks[10], (D_MODEL,), f32)
    return {"x": x, "norm1_g": norm1_g, "w_in": w_in, "conv_w": conv_w,
            "conv_norm_g": conv_norm_g, "ret_norm_g": ret_norm_g, "w_out": w_out,
            "norm2_g": norm2_g, "w_up": w_up, "w_down": w_down,
            "final_norm_g": final_norm_g}

def first_block(x, norm1_g, w_in, conv_w, conv_norm_g, ret_norm_g, w_out,
              norm2_g, w_up, w_down, final_norm_g):
    h = x
    for _ in range(DEPTH):
        h = h + hybrid_mixer(rms_norm(h, norm1_g), w_in, conv_w, conv_norm_g, ret_norm_g, w_out)
        h = h + sq_relu_mlp(rms_norm(h, norm2_g), w_up, w_down)
    return rms_norm(h, final_norm_g)


DEPTH_2 = 2

N_MIXERS = 2
CONV_K_2 = 4
EPS = 1e-6
M_INNER = 2 * D_MODEL
M_HEADS = 4
M_DV = M_INNER // M_HEADS
M_DK = M_DV // 2
M_CHUNK = 64
R_WIDTH = 3 * D_MODEL // 2
R_BLOCKS = 8
R_BS = R_WIDTH // R_BLOCKS
LRU_C = 8.0

N_A = (DEPTH_2 + 1) // 2
N_B = DEPTH_2 // 2


def rmsnorm(x, g):
    xf = x.astype(jnp.float32)
    y = xf * lax.rsqrt(jnp.mean(xf * xf, axis=-1, keepdims=True) + EPS)
    return (y * g.astype(jnp.float32)).astype(x.dtype)

def causal_dwconv(x, w, b):
    s = x.shape[1]
    xp = jnp.pad(x, ((0, 0), (CONV_K_2 - 1, 0), (0, 0)))
    y = b + xp[:, 0:s] * w[0]
    for j in range(1, CONV_K_2):
        y = y + xp[:, j:j + s] * w[j]
    return y

def mlstm_chunkwise(q, k, v, log_i, log_f):
    b, h, s, dk = q.shape
    dv = v.shape[-1]
    L = M_CHUNK
    nc = s // L

    def to_chunks(t):
        t = t.reshape((b, h, nc, L) + t.shape[3:])
        return jnp.moveaxis(t, 2, 0)

    qc, kc, vc, ic, fc = (to_chunks(t) for t in (q, k, v, log_i, log_f))
    causal = jnp.tril(jnp.ones((L, L), dtype=bool))

    def step(carry, inp):
        C, n, m = carry
        qb, kb, vb, ib, fb = inp
        F = jnp.cumsum(fb, axis=-1)
        D = F[..., :, None] - F[..., None, :] + ib[..., None, :]
        D = jnp.where(causal, D, -jnp.inf)
        m_t = jnp.maximum(F + m[..., None], jnp.max(D, axis=-1))
        decay = jnp.exp(F + m[..., None] - m_t)
        W = jnp.exp(D - m_t[..., None])
        Sm = jnp.einsum('bhtk,bhsk->bhts', qb, kb) * W
        num = (decay[..., None] * jnp.einsum('bhtk,bhkv->bhtv', qb, C)
               + jnp.einsum('bhts,bhsv->bhtv', Sm, vb))
        den = decay * jnp.einsum('bhtk,bhk->bht', qb, n) + jnp.sum(Sm, axis=-1)
        hb = num / jnp.maximum(jnp.abs(den), jnp.exp(-m_t))[..., None]
        w_last = W[..., -1, :]
        d_last = decay[..., -1]
        C_new = d_last[..., None, None] * C + jnp.einsum('bhs,bhsk,bhsv->bhkv', w_last, kb, vb)
        n_new = d_last[..., None] * n + jnp.einsum('bhs,bhsk->bhk', w_last, kb)
        return (C_new, n_new, m_t[..., -1]), hb

    init = (jnp.zeros((b, h, dk, dv), jnp.float32),
            jnp.zeros((b, h, dk), jnp.float32),
            jnp.zeros((b, h), jnp.float32))
    _, hs = lax.scan(step, init, (qc, kc, vc, ic, fc))
    return jnp.moveaxis(hs, 0, 2).reshape(b, h, s, dv)

def mlstm_mixer(u, w_in, conv_w, conv_b, w_q, w_k, w_v, b_i, b_f, norm_w, skip, w_out):
    bsz, s, _ = u.shape
    proj = u @ w_in
    xm, z, o_pre, i_pre, f_pre = jnp.split(
        proj, [M_INNER, 2 * M_INNER, 3 * M_INNER, 3 * M_INNER + M_HEADS], axis=-1)
    xc = jax.nn.silu(causal_dwconv(xm, conv_w, conv_b))
    xch = xc.reshape(bsz, s, M_HEADS, M_DV)
    xmh = xm.reshape(bsz, s, M_HEADS, M_DV)
    q = jnp.einsum('bshd,hde->bhse', xch, w_q).astype(jnp.float32) * (M_DK ** -0.5)
    k = jnp.einsum('bshd,hde->bhse', xch, w_k).astype(jnp.float32)
    v = jnp.einsum('bshd,hde->bhse', xmh, w_v).astype(jnp.float32)
    log_i = jnp.transpose((i_pre + b_i).astype(jnp.float32), (0, 2, 1))
    log_f = jnp.transpose(jax.nn.log_sigmoid((f_pre + b_f).astype(jnp.float32)), (0, 2, 1))
    h_tilde = jnp.transpose(mlstm_chunkwise(q, k, v, log_i, log_f), (0, 2, 1, 3))
    o = jax.nn.sigmoid(o_pre.astype(jnp.float32)).reshape(bsz, s, M_HEADS, M_DV)
    hh = o * h_tilde
    mu = jnp.mean(hh, axis=-1, keepdims=True)
    var = jnp.mean(jnp.square(hh - mu), axis=-1, keepdims=True)
    hn = ((hh - mu) * lax.rsqrt(var + EPS)).reshape(bsz, s, M_INNER)
    hn = (hn * norm_w.astype(jnp.float32)).astype(u.dtype)
    y = (hn + skip * xc) * jax.nn.silu(z)
    return y @ w_out

def linear_scan(a, bt):
    def step(hc, ab):
        a_t, b_t = ab
        hc = a_t * hc + b_t
        return hc, hc
    h0 = jnp.zeros((a.shape[0], a.shape[2]), jnp.float32)
    _, hs = lax.scan(step, h0, (jnp.moveaxis(a, 1, 0), jnp.moveaxis(bt, 1, 0)))
    return jnp.moveaxis(hs, 0, 1)

def rglru_mixer(u, w_in, conv_w, conv_b, w_a, b_a, w_x, b_x, lam, w_out):
    bsz, s, _ = u.shape
    proj = u @ w_in
    xr, g = jnp.split(proj, [R_WIDTH], axis=-1)
    xc = causal_dwconv(xr, conv_w, conv_b)
    xb = xc.reshape(bsz, s, R_BLOCKS, R_BS)
    r = jax.nn.sigmoid(jnp.einsum('bsnc,ncd->bsnd', xb, w_a).reshape(bsz, s, R_WIDTH) + b_a)
    ig = jax.nn.sigmoid(jnp.einsum('bsnc,ncd->bsnd', xb, w_x).reshape(bsz, s, R_WIDTH) + b_x)
    log_a = -LRU_C * r.astype(jnp.float32) * jax.nn.softplus(-lam.astype(jnp.float32))
    a = jnp.exp(log_a)
    bt = jnp.sqrt(-jnp.expm1(2.0 * log_a)) * (ig * xc).astype(jnp.float32)
    hs = linear_scan(a, bt).astype(u.dtype)
    y = hs * jax.nn.silu(g)
    return y @ w_out

def second_inputs(seed: int = 0) -> dict:
    key = jax.random.key(seed)
    ks = iter(jax.random.split(key, 32))
    nrm = lambda shape, scale: jax.random.normal(next(ks), shape, jnp.float32) * scale
    i_w = 3 * M_INNER + 2 * M_HEADS
    lam_u = jax.random.uniform(next(ks), (N_B, R_WIDTH), jnp.float32, 0.9, 0.999)
    sig = lam_u ** (1.0 / LRU_C)
    b_f = jnp.broadcast_to(jnp.linspace(3.0, 6.0, M_HEADS, dtype=jnp.float32), (N_A, M_HEADS))
    return {
        "x": nrm((BATCH, SEQ, D_MODEL), 1.0),
        "ln_g": 1.0 + nrm((DEPTH_2, D_MODEL), 0.05),
        "final_g": 1.0 + nrm((D_MODEL,), 0.05),
        "m_w_in": nrm((N_A, D_MODEL, i_w), D_MODEL ** -0.5),
        "m_conv_w": nrm((N_A, CONV_K_2, M_INNER), CONV_K_2 ** -0.5),
        "m_conv_b": nrm((N_A, M_INNER), 0.02),
        "m_w_q": nrm((N_A, M_HEADS, M_DV, M_DK), M_DV ** -0.5),
        "m_w_k": nrm((N_A, M_HEADS, M_DV, M_DK), M_DV ** -0.5),
        "m_w_v": nrm((N_A, M_HEADS, M_DV, M_DV), M_DV ** -0.5),
        "m_b_i": nrm((N_A, M_HEADS), 0.1),
        "m_b_f": b_f + nrm((N_A, M_HEADS), 0.1),
        "m_norm_w": 1.0 + nrm((N_A, M_INNER), 0.05),
        "m_skip": 1.0 + nrm((N_A, M_INNER), 0.05),
        "m_w_out": nrm((N_A, M_INNER, D_MODEL), M_INNER ** -0.5),
        "r_w_in": nrm((N_B, D_MODEL, 2 * R_WIDTH), D_MODEL ** -0.5),
        "r_conv_w": nrm((N_B, CONV_K_2, R_WIDTH), CONV_K_2 ** -0.5),
        "r_conv_b": nrm((N_B, R_WIDTH), 0.02),
        "r_w_a": nrm((N_B, R_BLOCKS, R_BS, R_BS), R_BS ** -0.5),
        "r_b_a": nrm((N_B, R_WIDTH), 0.02),
        "r_w_x": nrm((N_B, R_BLOCKS, R_BS, R_BS), R_BS ** -0.5),
        "r_b_x": nrm((N_B, R_WIDTH), 0.02),
        "r_lam": jnp.log(sig / (1.0 - sig)),
        "r_w_out": nrm((N_B, R_WIDTH, D_MODEL), R_WIDTH ** -0.5),
    }

def second_block(x, ln_g, final_g, m_w_in, m_conv_w, m_conv_b, m_w_q, m_w_k, m_w_v, m_b_i, m_b_f,
              m_norm_w, m_skip, m_w_out, r_w_in, r_conv_w, r_conv_b, r_w_a, r_b_a, r_w_x, r_b_x,
              r_lam, r_w_out):
    for layer in range(DEPTH_2):
        u = rmsnorm(x, ln_g[layer])
        j = layer // N_MIXERS
        if layer % N_MIXERS == 0:
            y = mlstm_mixer(u, m_w_in[j], m_conv_w[j], m_conv_b[j], m_w_q[j], m_w_k[j], m_w_v[j],
                            m_b_i[j], m_b_f[j], m_norm_w[j], m_skip[j], m_w_out[j])
        else:
            y = rglru_mixer(u, r_w_in[j], r_conv_w[j], r_conv_b[j], r_w_a[j], r_b_a[j],
                            r_w_x[j], r_b_x[j], r_lam[j], r_w_out[j])
        x = x + y
    return rmsnorm(x, final_g)


def setup_inputs(seed=0):
    out = dict(first_inputs(seed))
    for name, value in second_inputs(seed + 1).items():
        if name != "x":
            out[name + "_2"] = value
    return out


def reference(
    x, norm1_g, w_in, conv_w, conv_norm_g, ret_norm_g, w_out, norm2_g, w_up, w_down,
    final_norm_g, ln_g_2, final_g_2, m_w_in_2, m_conv_w_2, m_conv_b_2, m_w_q_2, m_w_k_2,
    m_w_v_2, m_b_i_2, m_b_f_2, m_norm_w_2, m_skip_2, m_w_out_2, r_w_in_2, r_conv_w_2,
    r_conv_b_2, r_w_a_2, r_b_a_2, r_w_x_2, r_b_x_2, r_lam_2, r_w_out_2,
):
    x = first_block(
        x, norm1_g, w_in, conv_w, conv_norm_g, ret_norm_g, w_out, norm2_g, w_up, w_down,
        final_norm_g,
    )
    return second_block(
        x, ln_g_2, final_g_2, m_w_in_2, m_conv_w_2, m_conv_b_2, m_w_q_2, m_w_k_2, m_w_v_2,
        m_b_i_2, m_b_f_2, m_norm_w_2, m_skip_2, m_w_out_2, r_w_in_2, r_conv_w_2, r_conv_b_2,
        r_w_a_2, r_b_a_2, r_w_x_2, r_b_x_2, r_lam_2, r_w_out_2,
    )


_drawn_inputs = setup_inputs


def setup_inputs(seed=0):
    import zlib

    import numpy as np

    out = dict(_drawn_inputs(seed))
    spreads = {}
    factors = {'m_b_i_2': 64.0,
     'm_skip_2': 3.599,
     'r_b_a_2': 39.77,
     'r_b_x_2': 23.819,
     'm_norm_w_2': 3.074}
    for name, (base, spread) in spreads.items():
        noise = np.random.default_rng([zlib.crc32(name.encode()), seed]).standard_normal(out[name].shape)
        drawn = base * np.exp(spread * noise) if base else spread * noise
        out[name] = __import__('jax').numpy.asarray(drawn.astype(out[name].dtype))
    for name, factor in factors.items():
        out[name] = (out[name] * factor).astype(out[name].dtype)
    return out
```

```python
from contextlib import ExitStack

import concourse.bass as bass
from concourse import mybir

F32 = mybir.dt.float32
F32R = mybir.dt.float32r
ACT = mybir.ActivationFunctionType
ALU = mybir.AluOpType
ds = bass.ds

P = 128
D = 1024
S = 1024
KT = D // P
HALF = 512
EPS = 1e-6

RET_HEADS = 4
CONV_TILES = 4
CHUNK = 128
CONSTS = 9 * 16
NCH = S // CHUNK
RET_COL = 1536

FF_BLOCKS = 8

M_HEADS = 4
M_INNER = 2048
MT = M_INNER // P
DV = 512
DK = 256
VT = DV // P
KK = DK // P
ROWS = M_HEADS * NCH

R_WIDTH = 1536
R_TILES = R_WIDTH // P
R_PAIRS = 4
RT = 3
GATE_TILES = [(0, 0), (1, 0), (0, 1), (1, 1), (2, 1), (1, 2), (2, 2)]

PHASES = [
    ("read", 1, 0, 8, 0),
    ("norm1", 1, 0, 0, 2),
    ("ret", RET_HEADS, 4, 4, 6),
    ("ret_down", 1, 4, 8, 0),
    ("conv", 2, 6, 6, 2),
    ("conv_down", 1, 4, 8, 0),
    ("norm2", 1, 0, 0, 2),
    ("ffn", FF_BLOCKS, 8, 12, 0),
    ("norm3", 1, 0, 0, 2),
    ("norm4", 1, 0, 0, 2),
    ("gate", 1, 2, 2, 2),
    ("inner", MT // 2, 6, 6, 0),
    ("mlstm", M_HEADS, 8, 16, 4),
    ("norm5", 1, 0, 0, 2),
    ("lru", R_PAIRS, 12, 20, 0),
    ("norm6", 1, 0, 0, 2),
    ("write", 1, 0, 8, 0),
]


def first_of(column):
    at, out = 0, {}
    for row in PHASES:
        out[row[0]] = at
        at += row[1] * row[column]
    return out, at


UNIT0, UNITS = first_of(2)
PROJ0, _ = first_of(3)
AUX0, _ = first_of(4)
UNITS_OF = {row[0]: row[2] for row in PHASES}
PROJ_OF = {row[0]: row[3] for row in PHASES}
AUX_OF = {row[0]: row[4] for row in PHASES}


def slot_uses(first, per, i, k):
    return first // 2 + (per // 2) * i + k // 2


VEC = [("n1g", KT), ("n2g", KT), ("n3g", KT), ("n4g", KT), ("n5g", KT), ("n6g", KT),
       ("cnw", 3 * CONV_TILES), ("cng", CONV_TILES), ("rng", RET_HEADS), ("zeta", RET_HEADS),
       ("chunk_decay", RET_HEADS), ("mcw", 4 * MT), ("mcb", MT), ("mnw", MT), ("msk", MT),
       ("rcw", 4 * R_TILES), ("rcb", R_TILES), ("rba", R_TILES), ("rbx", R_TILES),
       ("lam", R_TILES)]
VEC_AT = {}
VEC_N = 0
for _name, _n in VEC:
    VEC_AT[_name] = VEC_N
    VEC_N += _n


START1 = {
    "pool": ["w_split0", "w_split1", "h_y", "h_done"],
    "pe": ["w_used0", "h_qc", "h_oT", "h_hnT"],
    "act": ["g_rounded", "h_t1", "h_yhi", "m_xc"],
    "dve": ["g_ready", "c_y", "c_n", "m_conv", "m_zs", "m_zn", "h_hh", "h_y1", "h_den",
            "h_num", "l_xc", "l_h", "l_ix", "l_xclo"],
}
START16 = {"act": ["st_xm", "st_xc", "st_zn", "st_zs", "st_o"]}


def from1(n):
    return n + 1


def from16(n):
    return n + 16


def build(nc, d):
    ctx = ExitStack()
    with ctx:
        def dram(name, shape):
            return nc.dram_tensor(name, shape, F32, kind="Internal").ap()

        by_name = {}

        def sem(name):
            by_name[name] = ctx.enter_context(nc.semaphore(name))
            return by_name[name]

        def raise_starts(engine, who):
            for name in START1.get(who, []):
                engine.sem_inc(by_name[name], 1)
            for name in START16.get(who, []):
                engine.sem_inc(by_name[name], 16)

        x_kept = dram("x_kept", (P, KT, S))
        xm_kept = dram("xm_kept", (MT, P, S))
        xc_kept = dram("xc_kept", (MT, P, S))
        o_kept = dram("o_kept", (MT, P, S))
        zn_kept = dram("zn_kept", (MT, P, S))
        zs_kept = dram("zs_kept", (MT, P, S))
        gate_kept = dram("gate_kept", (2, M_HEADS, S))
        last_kept = dram("last_kept", (3, ROWS))

        base = nc.sbuf_base
        end = nc.sbuf_usable_end
        top = [(base + 31) // 32 * 32]

        def place(name, shape, dt=F32, at=None):
            size = 4
            for n in shape[1:]:
                size *= n
            size = (size + 31) // 32 * 32
            where = top[0] if at is None else at
            t = nc.alloc_sbuf_tensor_at(name, list(shape), dt, offset=where)
            assert where + size <= end, (name, where + size - end)
            if at is None:
                top[0] += size
            return t, where + size

        def keep(name, shape, dt=F32):
            return place(name, shape, dt)[0]

        X_AT = top[0]
        X = keep("x_res", [P, KT, S])
        X_END = top[0]
        raw = keep("w_raw", [P, 2, 1024])
        wh = keep("w_hi", [P, 2, 1024], F32R)
        wl = keep("w_lo", [P, 2, 1024], F32R)
        ident = keep("ident", [P, P])
        identr = keep("identr", [P, P], F32R)
        ones = keep("ones", [P, P])
        eps = keep("eps", [P, 1])
        zero = keep("zero", [P, 1])
        onesr = keep("onesr", [P, 4], F32R)
        group64 = keep("group64", [P, P])
        mbif = keep("mbif", [M_HEADS, 2])
        vec = keep("vec", [P, VEC_N])
        lra = keep("lru_rate", [P, R_TILES])
        ltmp = keep("lru_tmp", [P, 4, R_TILES])

        def v(name, k=0, n=1):
            return vec[:, ds(VEC_AT[name] + k, n)]

        Ap = keep("tile_a", [P, 8 + S])
        A = Ap[:, 8:8 + S]
        B = keep("tile_b", [P, S])
        C = keep("tile_c", [P, S])
        Dt = keep("tile_d", [P, S])
        U_AT = top[0]
        Uh = keep("u_hi", [P, KT, S], F32R)
        Ul = keep("u_lo", [P, KT, S], F32R)
        V_AT = top[0]
        Gh = keep("g_hi", [P, VT, S], F32R)
        Gl = keep("g_lo", [P, VT, S], F32R)
        G_END = top[0]

        def area(at, limit):
            cur = [at]

            def put(name, shape, dt=F32):
                t, cur[0] = place(name, shape, dt, at=cur[0])
                assert cur[0] <= limit, (name, cur[0] - limit)
                return t
            return put

        put = area(X_AT, X_END)
        Qh, Ql = put("q_hi", [P, S], F32R), put("q_lo", [P, S], F32R)
        Kh, Kl = put("k_hi", [P, S], F32R), put("k_lo", [P, S], F32R)
        QXh, QXl = put("qx_hi", [P, S], F32R), put("qx_lo", [P, S], F32R)
        Kth, Ktl = put("kt_hi", [P, S], F32R), put("kt_lo", [P, S], F32R)
        put = area(G_END, end)
        Vth, Vtl = put("vt_hi", [P, S], F32R), put("vt_lo", [P, S], F32R)
        SMh, SMl = put("sm_hi", [P, S], F32R), put("sm_lo", [P, S], F32R)
        cos = put("cos", [P, S])
        sin = put("sin", [P, S])
        decay = put("decay", [P, RET_HEADS, P])
        xi = put("xi", [P, RET_HEADS, P])

        put = area(G_END, end)
        Cp = put("conv_in", [P, 8 + S])

        put = area(V_AT, end)
        E = put("inner_e", [P, S])
        Fx = put("inner_xc", [P, S])
        H = put("inner_z", [P, S])
        Q = put("inner_q", [P, S])
        O = put("inner_o", [P, S])
        GR = put("gate_rows", [M_HEADS, 2, S])

        put = area(U_AT, end)
        GXh = put("m_x_hi", [P, VT, S], F32R)
        GXl = put("m_x_lo", [P, VT, S], F32R)
        Vh = put("m_v_hi", [P, NCH, DV], F32R)
        Vl = put("m_v_lo", [P, NCH, DV], F32R)
        Mqh = put("m_q_hi", [P, KK, S], F32R)
        Mql = put("m_q_lo", [P, KK, S], F32R)
        Mkh = put("m_k_hi", [P, KK, S], F32R)
        Mkl = put("m_k_lo", [P, KK, S], F32R)
        Cf = put("m_c", [P, KK, 514])
        Ch = put("m_c_hi", [P, KK, 514], F32R)
        Cl = put("m_c_lo", [P, KK, 514], F32R)
        negmask = put("negmask", [P, P])
        cols = put("cols", [P, 5, ROWS])
        hc = put("head_cols", [P, 6, NCH])
        dlb = put("dlb", [P, ROWS])
        num = put("m_num", [P, DV])
        dcol = put("m_dcol", [P, 8])
        bst = put("m_bst", [P, 8])
        mst = put("m_mst", [P, 4])
        c_at = [U_AT - 2 * 4 * S, U_AT - 4 * S]
        Msh = place("m_s_hi", [P, S], F32R, at=c_at[0])[0]
        Msl = place("m_s_lo", [P, S], F32R, at=c_at[1])[0]
        ab_at = U_AT - 4 * 4 * S
        t1 = place("m_t1", [P, DV], F32, at=ab_at)[0]
        hh = place("m_hh", [P, DV], F32, at=ab_at + 2048)[0]
        yy = place("m_y", [P, DV], F32, at=ab_at + 4096)[0]
        och = put("m_och", [P, VT, CHUNK])
        znc = put("m_znc", [P, VT, CHUNK])
        zsc = put("m_zsc", [P, VT, CHUNK])
        put = area(U_AT, V_AT)
        gi = put("gi", [ROWS, P])
        gf = put("gf", [ROWS, P])
        ga = put("ga", [ROWS, P])
        gb = put("gb", [ROWS, P])
        gc_ = put("gc", [ROWS, P])
        gF = put("gF", [ROWS, P])
        gA = put("gA", [ROWS, P])
        gM = put("gM", [ROWS, P])
        gone = put("gone", [ROWS, P])
        gzero = put("gzero", [ROWS, P])
        g5 = put("g5", [ROWS, 5, P])
        gcol = put("gcol", [ROWS, 8])
        gdiag = put("gdiag", [ROWS, ROWS])
        sc4 = put("sc4", [M_HEADS, 3, NCH + 1])

        put = area(V_AT, end)
        G3h = put("g3_hi", [P, RT, S], F32R)
        G3l = put("g3_lo", [P, RT, S], F32R)
        XCh = put("xc_hi", [P, RT, S], F32R)
        XCl = put("xc_lo", [P, RT, S], F32R)
        R3 = put("lru_r", [P, RT, S])


        PJ = ctx.enter_context(nc.psum_tensor("proj", [P, 2, 1024], F32))
        AX = ctx.enter_context(nc.psum_tensor("aux", [P, 2, 1024], F32))

        consts = sem("consts")
        consts_r = sem("consts_r")
        w_loaded = [sem("w_loaded0"), sem("w_loaded1")]
        w_rounded = sem("w_rounded")
        w_split = [sem("w_split0"), sem("w_split1")]
        w_used = [sem("w_used0"), sem("w_used1")]
        pj_full = [sem("pj_full0"), sem("pj_full1")]
        pj_free = [sem("pj_free0"), sem("pj_free1")]
        ax_full = [sem("ax_full0"), sem("ax_full1")]
        ax_free = [sem("ax_free0"), sem("ax_free1")]
        xt_loaded = [sem("xt_loaded0"), sem("xt_loaded1")]
        x_spilled = sem("x_spilled")
        x_back = sem("x_back")
        out_stored = [sem("out_stored0"), sem("out_stored1")]
        sq_ready = sem("sq_ready")
        sq_used = sem("sq_used")
        rstd_ready = sem("rstd_ready")
        y_ready = sem("y_ready")
        u_rounded = sem("u_rounded")
        u_ready = sem("u_ready")
        g_rounded = sem("g_rounded")
        g_ready = sem("g_ready")
        x_scaled = sem("x_scaled")

        def use(phase, i, k):
            return slot_uses(UNIT0[phase], UNITS_OF[phase], i, k)

        def tile(phase, i, k):
            return slot_uses(PROJ0[phase], PROJ_OF[phase], i, k)

        def aux(phase, i, k):
            return slot_uses(AUX0[phase], AUX_OF[phase], i, k)

        NORMS = ["norm1", "norm2", "norm3", "norm4", "norm5", "norm6"]
        GAINS = dict(norm1="n1g", norm2="n2g", norm3="n3g", norm4="n4g", norm5="n5g", norm6="n6g")
        SOURCE = dict(norm1=("read", 0, 0), norm2=("conv_down", 0, 0), norm3=("ffn", FF_BLOCKS - 1, 4),
                      norm5=("mlstm", M_HEADS - 1, 8), norm6=("lru", R_PAIRS - 1, 12))
        UREADY = dict(norm1=0, norm2=8, norm4=16, norm5=24)
        GREADY = dict(ret=1, conv=5, ffn=9, lru=41)

        block = ctx.enter_context(nc.Block())

        w_in = d["w_in"].rearrange("(t p) n -> p t n", p=P)
        w_out = d["w_out"].rearrange("(t p) n -> p t n", p=P)
        w_up = d["w_up"].rearrange("(t p) n -> p t n", p=P)
        w_down = d["w_down"].rearrange("(t p) n -> p t n", p=P)
        m_in = d["m_w_in"].rearrange("(t p) n -> p t n", p=P)
        m_q = d["m_w_q"].rearrange("(t p) n -> p t n", p=P)
        m_k = d["m_w_k"].rearrange("(t p) n -> p t n", p=P)
        m_v = d["m_w_v"].rearrange("(t p) n -> p t n", p=P)
        m_out = d["m_w_out"].rearrange("(t p) n -> p t n", p=P)
        r_in = d["r_w_in"].rearrange("(t p) n -> p t n", p=P)
        r_out = d["r_w_out"].rearrange("(t p) n -> p t n", p=P)

        def sems(names):
            return {n: sem(n) for n in names.split()}

        r = sems("r_swapped r_sin r_rotated r_qhi r_qlo r_qx r_qxhi r_qxlo r_khi r_klo "
                 "r_kthi r_vthi r_smhi r_smlo r_state r_shi r_slo r_rstd r_y1 r_y")
        c = sems("c_pad c_0 c_1 c_2 c_y c_sq c_rstd c_n")
        f_sq = sem("f_sq")
        m = sems("m_pad m_c0 m_c1 m_c2 m_conv m_xc m_zn m_zs st_xm st_xc st_zn st_zs st_o "
                 "g_stored g_back ga_exp ga_abs ga_step ga_last ga_lastback ga_m ga_mback ga_rows ga_exps "
                 "ga_dl lam_abs lam_exp")
        h = sems("h_x0 h_x1 h_xround h_xsplit h_vhi h_qhi h_khi h_hc h_diag h_w "
                 "h_smhi h_smlo h_kthi h_ktlo h_c h_chi h_clo h_den h_och h_znc h_zsc "
                 "h_qc h_sv h_cu h_t1 h_num h_d0 h_d1 h_d2 h_oT h_hh h_st h_st2 h_std h_rs h_hn h_hnT "
                 "h_y1 h_y h_yhi h_done")
        l = sems("l_pad l_c0 l_c1 l_c2 l_xc l_xchi l_xclo l_rate l_th l_aa l_e l_sqrt l_x l_ix l_bt "
                 "l_h l_y")

        @block.sync
        def _(sp):
            for t in range(8):
                if t >= 2:
                    sp.wait_ge(pj_full[t % 2], t // 2)
                sp.dma_start((B, C)[t % 2][:, :], d["x"][t * P:(t + 1) * P, :]) \
                    .then_inc(xt_loaded[t % 2], 16)

            def load(phase, i, k, src, width):
                n = use(phase, i, k)
                sp.wait_ge(w_split[k % 2], from1(n))
                dst = raw[:, k % 2, :].rearrange("p (t n) -> p t n", n=width)[:, 0:src.shape[1], 0:src.shape[2]]
                sp.dma_start(dst, src).then_inc(w_loaded[k % 2], 16)

            def load_down(phase, i, k0, w, row, tiles):
                for k in range(4):
                    load(phase, i, k0 + k, w[:, ds(row, tiles), k * 256:(k + 1) * 256], 256)

            with sp.Fori(0, RET_HEADS) as i:
                for k in range(4):
                    load("ret", i, k, w_in[:, :, ds(i * P + (RET_COL + k * 512), P)], P)
            sp.wait_ge(x_spilled, 16)
            sp.wait_ge(g_ready, GREADY["ret"] + RET_HEADS)
            sp.dma_start(X[:, :, :], x_kept).then_inc(x_back, 16)
            load_down("ret_down", 0, 0, w_out, 4, 4)
            with sp.Fori(0, 2) as i:
                for cc in range(2):
                    for k in range(3):
                        load("conv", i, cc * 3 + k, w_in[:, :, ds(i * 256 + (k * 512 + cc * P), P)], P)
            load_down("conv_down", 0, 0, w_out, 0, 4)
            with sp.Fori(0, FF_BLOCKS) as i:
                for k in range(4):
                    load("ffn", i, k, w_up[:, :, ds(i * 512 + k * P, P)], P)
                load_down("ffn", i, 4, w_down, i * 4, 4)
            for k in range(2):
                load("gate", 0, k, m_in[:, :, 3 * M_INNER + 4 * k:3 * M_INNER + 4 * k + 4], P)
            with sp.Fori(0, MT // 2) as i:
                for jj in range(2):
                    for k in range(3):
                        load("inner", i, jj * 3 + k, m_in[:, :, ds(i * 256 + (k * M_INNER + jj * P), P)], P)
            with sp.Fori(0, M_HEADS) as i:
                for k in range(2):
                    load("mlstm", i, k, m_v[:, ds(i * VT + 2 * k, 2), :], DV)
                for kept, q in ((xm_kept, 0), (xc_kept, 1)):
                    for t in range(VT):
                        u = 4 * q + t
                        if u >= 2:
                            sp.wait_ge(h["h_xsplit"], 8 * i + u - 1)
                        elif u == 0:
                            for s in ("st_xm", "st_xc", "st_zn", "st_zs", "st_o"):
                                sp.wait_ge(m[s], from16(16 * MT))
                            sp.wait_ge(h["h_done"], from1(NCH * i))
                        sp.dma_start((A, B)[t % 2][:, :], kept[ds(i * VT + t, 1), :, :].rearrange("a p s -> (a p) s")) \
                            .then_inc(h["h_x%d" % (t % 2)], 16)
                load("mlstm", i, 2, m_q[:, ds(i * VT, VT), :], DK)
                load("mlstm", i, 3, m_k[:, ds(i * VT, VT), :], DK)
                for k in range(2):
                    load("mlstm", i, 4 + k, m_out[:, ds(i * VT, VT), k * 256:(k + 1) * 256], 256)
                def stage_chunk(kept, dst, got, gone, n):
                    sp.wait_ge(h[gone], from1(NCH * i + n))
                    sp.dma_start(dst[:, :, :], kept[ds(i * VT, VT), :, n * CHUNK:(n + 1) * CHUNK]
                                 .rearrange("t p s -> p t s")).then_inc(h[got], 16)

                for n in range(NCH + 1):
                    if n < NCH:
                        stage_chunk(o_kept, och, "h_och", "h_oT", n)
                    if n >= 1:
                        stage_chunk(zn_kept, znc, "h_znc", "h_y1", n - 1)
                        stage_chunk(zs_kept, zsc, "h_zsc", "h_y", n - 1)
                for k in range(2, 4):
                    load("mlstm", i, 4 + k, m_out[:, ds(i * VT, VT), k * 256:(k + 1) * 256], 256)
            with sp.Fori(0, R_PAIRS) as i:
                for k in range(3):
                    load("lru", i, k, r_in[:, :, ds(i * 384 + k * P, P)], P)
                for k, w in ((3, d["gate_a"]), (4, d["gate_x"])):
                    load("lru", i, k, w[ds(i, 1), :, :].rearrange("a p (t n) -> (a p) t n", n=P), P)
                for k in range(3):
                    load("lru", i, 5 + k, r_in[:, :, ds(i * 384 + (R_WIDTH + k * P), P)], P)
                load_down("lru", i, 8, r_out, i * RT, RT)
            for t in range(8):
                sp.wait_ge(pj_free[t % 2], tile("write", 0, t) + 1)
                sp.dma_start(d["out"][t * P:(t + 1) * P, :], (B, C)[t % 2][:, :]).then_inc(out_stored[t % 2], 16)
            for s in out_stored:
                sp.wait_ge(s, 64)

        @block.gpsimd
        def _(pool):
            raise_starts(pool, "pool")
            pool.wait_ge(consts_r, 4)

            def split_unit(s, n):
                pool.wait_ge(w_loaded[s], 16 * n + 16)
                pool.wait_ge(w_used[s], n + 1)
                nc.gpsimd.tensor_tensor(wh[:, s, :], raw[:, s, :], zero[:, 0:1].broadcast_to([P, 1024]),
                                        ALU.add).then_inc(w_rounded, 1)
                pool.wait_ge(w_rounded, 2 * n + (s + 1))
                nc.gpsimd.tensor_tensor(wl[:, s, :], raw[:, s, :], wh[:, s, :].bitcast(F32),
                                        ALU.subtract).then_inc(w_split[s], 1)

            with pool.Fori(0, UNIT0["mlstm"] // 2) as i:
                for s in range(2):
                    split_unit(s, i)
            with pool.Fori(0, M_HEADS) as i:
                for k in range(6):
                    split_unit(k % 2, use("mlstm", i, k))
                for n in range(NCH):
                    g = NCH * i + n
                    pool.wait_ge(h["h_y1"], from1(g + 1))
                    pool.wait_ge(h["h_zsc"], 16 * g + 16)
                    nc.gpsimd.tensor_tensor(yy[:, :], yy[:, :], zsc[:, :, :].rearrange("p t s -> p (t s)"),
                                            ALU.add).then_inc(h["h_y"], 1)
                    pool.wait_ge(h["h_yhi"], from1(g + 1))
                    nc.gpsimd.tensor_tensor(GXl[:, :, n * P:(n + 1) * P],
                                            yy[:, :].rearrange("p (t s) -> p t s", t=VT),
                                            GXh[:, :, n * P:(n + 1) * P].bitcast(F32),
                                            ALU.subtract).then_inc(h["h_done"], 1)
                for k in range(6, 8):
                    split_unit(k % 2, use("mlstm", i, k))
            with pool.Fori(0, (UNITS - UNIT0["norm5"]) // 2) as i:
                for s in range(2):
                    split_unit(s, i + UNIT0["norm5"] // 2)

        @block.tensor
        def _(pe):
            raise_starts(pe, "pe")
            mm = nc.tensor.matmul

            def mm3(out, lh, ll, rh, rl, start, stop, closes=None):
                first = mm(out, lh, rh, start=start, stop=False)
                if closes is not None:
                    first.then_inc(w_used[closes], 1)
                mm(out, lh, rl, start=False, stop=False)
                return mm(out, ll, rh, start=False, stop=stop)

            def start_unit(phase, i, k):
                pe.wait_ge(w_split[k % 2], from1(use(phase, i, k) + 1))

            def start_tile(phase, i, k):
                pe.wait_ge(pj_free[k % 2], tile(phase, i, k))

            def start_aux(phase, i, k):
                pe.wait_ge(ax_free[k % 2], aux(phase, i, k))

            def project(phase, i, k, p, xh, xl, kts, width, col, waits=None, closes=True):
                s = k % 2
                start_tile(phase, i, p)
                for kt in range(kts):
                    if waits is not None:
                        pe.wait_ge(*waits(kt))
                    at = kt * width + col
                    for j in range(2):
                        tok = slice(j * HALF, (j + 1) * HALF)
                        ins = mm3(PJ[:, p % 2, tok], wh[:, s, at:at + P], wl[:, s, at:at + P],
                                  xh[:, kt, tok], xl[:, kt, tok], kt == 0, kt == kts - 1,
                                  1 - s if closes and kt == 0 and j == 0 else None)
                ins.then_inc(pj_full[p % 2], 1)

            def up(phase, i, k, p, waits=None):
                start_unit(phase, i, k)
                project(phase, i, k, p, Uh, Ul, KT, P, 0, waits)

            def down(phase, i, k0, p0, gh, gl, kts, ready=None, closes_first=True):
                for k in range(4):
                    start_unit(phase, i, k0 + k)
                    for j in range(2):
                        first = k == 0 and j == 0 and ready is not None
                        project(phase, i, k0 + k, p0 + 2 * k + j, gh, gl, kts, 256, j * P,
                                (lambda kt: (g_ready, ready + kt + 1)) if first else None,
                                j == 0 and (k > 0 or closes_first))

            def norm_sums(phase):
                first = 8 * NORMS.index(phase)
                for j in range(2):
                    start_aux(phase, 0, j)
                for t in range(KT):
                    pe.wait_ge(sq_ready, first + t + 1)
                    for j in range(2):
                        ins = mm(AX[:, j, 0:HALF], ones[:, :], (A, B)[t % 2][:, j * HALF:(j + 1) * HALF],
                                 start=t == 0, stop=t == KT - 1)
                        if t == KT - 1:
                            ins.then_inc(ax_full[j], 1)
                        elif j == 1:
                            ins.then_inc(sq_used, 1)

            u_wait = lambda phase: (lambda kt: (u_ready, UREADY[phase] + kt + 1))

            pe.wait_ge(consts, CONSTS)
            pe.wait_ge(consts_r, 4)
            for t in range(8):
                pe.wait_ge(xt_loaded[t % 2], 16 * (t // 2 + 1))
                start_tile("read", 0, t)
                for kt in range(KT):
                    ins = nc.tensor.transpose(PJ[:, t % 2, kt * P:(kt + 1) * P],
                                              (B, C)[t % 2][:, kt * P:(kt + 1) * P], ident[:, :])
                ins.then_inc(pj_full[t % 2], 1)
            norm_sums("norm1")

            with pe.Fori(0, RET_HEADS) as i:
                up("ret", i, 0, 0, u_wait("norm1"))
                up("ret", i, 1, 1)
                up("ret", i, 2, 2)
                start_aux("ret", i, 0)
                pe.wait_ge(r["r_rotated"], 2 * i + 2)
                for n in range(NCH):
                    at = slice(n * P, (n + 1) * P)
                    ins = nc.tensor.transpose(AX[:, 0, at], B[:, at], ident[:, :])
                ins.then_inc(ax_full[0], 1)
                up("ret", i, 3, 3)
                start_aux("ret", i, 1)
                pe.wait_ge(pj_free[0], tile("ret", i, 2) + 1)
                for n in range(NCH):
                    at = slice(n * P, (n + 1) * P)
                    ins = nc.tensor.transpose(AX[:, 1, at], C[:, at], ident[:, :])
                ins.then_inc(ax_full[1], 1)
                start_aux("ret", i, 2)
                pe.wait_ge(r["r_qlo"], i + 1)
                pe.wait_ge(r["r_klo"], i + 1)
                for n in range(NCH):
                    at = slice(n * P, (n + 1) * P)
                    ins = mm3(AX[:, 0, at], Kh[:, at], Kl[:, at], Qh[:, at], Ql[:, at], True, True)
                ins.then_inc(ax_full[0], 1)
                start_aux("ret", i, 3)
                pe.wait_ge(ax_free[0], aux("ret", i, 0) + 1)
                for n in range(NCH):
                    at = slice(n * P, (n + 1) * P)
                    ins = mm3(AX[:, 1, at], Kth[:, at], Ktl[:, at], Vth[:, at], Vtl[:, at], True, True)
                ins.then_inc(ax_full[1], 1)
                start_aux("ret", i, 4)
                pe.wait_ge(r["r_smlo"], i + 1)
                pe.wait_ge(r["r_slo"], i + 1)
                pe.wait_ge(r["r_qxlo"], i + 1)
                for n in range(NCH):
                    at = slice(n * P, (n + 1) * P)
                    mm3(AX[:, 0, at], Vth[:, at], Vtl[:, at], SMh[:, at], SMl[:, at], True, False)
                    ins = mm3(AX[:, 0, at], Kh[:, at], Kl[:, at], QXh[:, at], QXl[:, at], False, True)
                ins.then_inc(ax_full[0], 1)
                start_aux("ret", i, 5)
                pe.wait_ge(ax_free[0], aux("ret", i, 4) + 1)
                for j in range(2):
                    ins = mm(AX[:, 1, j * HALF:(j + 1) * HALF], ones[:, :], A[:, j * HALF:(j + 1) * HALF],
                             start=True, stop=True)
                ins.then_inc(ax_full[1], 1)
            down("ret_down", 0, 0, 0, Gh, Gl, 4, GREADY["ret"])

            with pe.Fori(0, 2) as i:
                for cc in range(2):
                    for k in range(3):
                        up("conv", i, 3 * cc + k, 3 * cc + k)
                    start_aux("conv", i, cc)
                    pe.wait_ge(c["c_sq"], 2 * i + cc + 1)
                    for j in range(2):
                        ins = mm(AX[:, cc, j * HALF:(j + 1) * HALF], group64[:, :],
                                 B[:, j * HALF:(j + 1) * HALF], start=True, stop=True)
                    ins.then_inc(ax_full[cc], 1)
            down("conv_down", 0, 0, 0, Gh, Gl, 4, GREADY["conv"])
            norm_sums("norm2")

            with pe.Fori(0, FF_BLOCKS) as i:
                for k in range(4):
                    up("ffn", i, k, k, u_wait("norm2") if k == 0 else None)
                down("ffn", i, 4, 4, Gh, Gl, 4, GREADY["ffn"] + 4 * i)
            norm_sums("norm3")
            norm_sums("norm4")

            for k in range(2):
                up("gate", 0, k, k, u_wait("norm4") if k == 0 else None)
            with pe.Fori(0, MT // 2) as i:
                for k in range(6):
                    up("inner", i, k, k)
            start_aux("gate", 0, 0)
            pe.wait_ge(m["ga_rows"], 2)
            pe.wait_ge(m["ga_exps"], 3)
            for q in range(5):
                ins = nc.tensor.transpose(AX[:, 0, q * ROWS:(q + 1) * ROWS], g5[:, q, :], ident[0:ROWS, 0:ROWS])
            ins.then_inc(ax_full[0], 1)
            start_aux("gate", 0, 1)
            pe.wait_ge(m["ga_dl"], 1)
            mm(AX[:, 1, 0:ROWS], ones[0:ROWS, :], gdiag[:, :], start=True, stop=True).then_inc(ax_full[1], 1)

            with pe.Fori(0, M_HEADS) as i:
                start_unit("mlstm", i, 0)
                pe.wait_ge(h["h_xsplit"], 8 * i + 4)
                for p in range(4):
                    start_tile("mlstm", i, p)
                    for j in range(2):
                        at = slice((2 * p + j) * P, (2 * p + j + 1) * P)
                        for kt in range(VT):
                            w = slice((kt % 2) * DV, (kt % 2 + 1) * DV)
                            if p == 0 and j == 0 and kt == 2:
                                start_unit("mlstm", i, 1)
                            ins = mm3(PJ[:, p % 2, j * HALF:(j + 1) * HALF], GXh[:, kt, at], GXl[:, kt, at],
                                      wh[:, kt // 2, w], wl[:, kt // 2, w], kt == 0, kt == VT - 1,
                                      1 if p == 0 and j == 0 and kt == 0 else None)
                    ins.then_inc(pj_full[p % 2], 1)
                start_aux("mlstm", i, 0)
                pe.wait_ge(h["h_diag"], i + 1)
                for j in range(2):
                    tok = slice(j * HALF, (j + 1) * HALF)
                    mm(AX[:, 0, tok], ones[:, :], Dt[:, tok], start=True, stop=False).then_inc(w_used[j], 1)
                for j in range(2):
                    ins = mm(AX[:, 0, j * HALF:(j + 1) * HALF], ident[:, :],
                             negmask[:, :].unsqueeze(1).broadcast_to([P, 4, P]), start=False, stop=True)
                ins.then_inc(ax_full[0], 1)
                pe.wait_ge(h["h_xsplit"], 8 * i + 8)
                for k in range(2):
                    start_unit("mlstm", i, 2 + k)
                    for j in range(2):
                        project("mlstm", i, 2 + k, 4 + 2 * k + j, GXh, GXl, VT, DK, j * P,
                                closes=k == 1 and j == 0)
                start_aux("mlstm", i, 1)
                for kk in range(KK):
                    pe.wait_ge(pj_free[kk], tile("mlstm", i, 6 + kk) + 1)
                for n in range(NCH):
                    at = slice(n * P, (n + 1) * P)
                    for kk in range(KK):
                        ins = mm3(AX[:, 1, at], Mkh[:, kk, at], Mkl[:, kk, at], Mqh[:, kk, at], Mql[:, kk, at],
                                  kk == 0, kk == KK - 1, 1 if n == 0 and kk == 0 else None)
                ins.then_inc(ax_full[1], 1)
                for kk in range(KK):
                    start_aux("mlstm", i, 2 + kk)
                    for n in range(NCH):
                        at = slice(n * P, (n + 1) * P)
                        mm(AX[:, kk, at], Mkh[:, kk, at], identr[:, :], start=True, stop=False)
                        ins = mm(AX[:, kk, at], Mkl[:, kk, at], identr[:, :], start=False, stop=True)
                    ins.then_inc(ax_full[kk], 1)
                for s in range(2):
                    pe.wait_ge(pj_free[s], tile("mlstm", i, 6 + s) + 1)
                    pe.wait_ge(ax_free[s], aux("mlstm", i, 2 + s) + 1)
                pe.wait_ge(h["h_smlo"], i + 1)
                pe.wait_ge(h["h_ktlo"], 2 * i + 2)
                for step in range(NCH + 1):
                    if step < NCH:
                        n = step
                        g = NCH * i + n
                        at = slice(n * P, (n + 1) * P)
                        if n < NCH - 1:
                            pe.wait_ge(h["h_c"], g + 1)
                            for kk in range(KK):
                                mm3(AX[:, 0, kk * DV:(kk + 1) * DV], Mkh[:, kk, at], Mkl[:, kk, at],
                                    Vh[:, n, :], Vl[:, n, :], True, True)
                            for kk in range(KK):
                                add = AX[:, 1, HALF + 2 * kk:HALF + 2 * kk + 2]
                                mm(add, Mkh[:, kk, at], onesr[:, 0:2], start=True, stop=False)
                                ins = mm(add, Mkl[:, kk, at], onesr[:, 0:2], start=False, stop=True)
                            ins.then_inc(h["h_cu"], 1)
                        pe.wait_ge(h["h_och"], 16 * (g + 1))
                        pe.wait_ge(h["h_hh"], from1(g))
                        for t in range(VT):
                            ins = nc.tensor.transpose(PJ[:, 1, t * P:(t + 1) * P], och[:, t, :], ident[:, :])
                        ins.then_inc(h["h_oT"], 1)
                        pe.wait_ge(h["h_num"], from1(g))
                        mm3(PJ[:, 0, DV:2 * DV], Msh[:, at], Msl[:, at], Vh[:, n, :], Vl[:, n, :], True, True) \
                            .then_inc(h["h_sv"], 1)
                        pe.wait_ge(h["h_clo"], g + 1)
                        pe.wait_ge(h["h_t1"], from1(g))
                        pe.wait_ge(h["h_den"], from1(g))
                        for kk in range(KK):
                            mm3(PJ[:, 0, 0:DV], Mqh[:, kk, at], Mql[:, kk, at], Ch[:, kk, 0:DV],
                                Cl[:, kk, 0:DV], kk == 0, kk == KK - 1)
                        for kk in range(KK):
                            mm3(AX[:, 1, 0:2], Mqh[:, kk, at], Mql[:, kk, at], Ch[:, kk, DV:DV + 2],
                                Cl[:, kk, DV:DV + 2], kk == 0, kk == KK - 1)
                        mm(AX[:, 1, 2:4], Msh[:, at], onesr[:, 0:2], start=True, stop=False)
                        mm(AX[:, 1, 2:4], Msl[:, at], onesr[:, 0:2], start=False, stop=True) \
                            .then_inc(h["h_qc"], 1)
                    if step >= 1:
                        g = NCH * i + (step - 1)
                        pe.wait_ge(h["h_hn"], g + 1)
                        pe.wait_ge(h["h_y1"], from1(g))
                        for t in range(VT):
                            ins = nc.tensor.transpose(PJ[:, 1, HALF + t * P:HALF + (t + 1) * P],
                                                      hh[:, t * P:(t + 1) * P], ident[:, :])
                        ins.then_inc(h["h_hnT"], 1)
                pe.wait_ge(h["h_done"], from1(NCH * i + NCH))
                down("mlstm", i, 4, 8, GXh, GXl, VT, closes_first=False)
            norm_sums("norm5")

            with pe.Fori(0, R_PAIRS) as i:
                for k in range(3):
                    up("lru", i, k, k, u_wait("norm5") if k == 0 else None)
                pe.wait_ge(l["l_xclo"], from1(3 * i + 3))
                for k in range(2):
                    s = (3 + k) % 2
                    start_unit("lru", i, 3 + k)
                    for t in range(RT):
                        qs = [q for q, (_, b) in enumerate(GATE_TILES) if b == t]
                        p = 3 + 3 * k + t
                        start_tile("lru", i, p)
                        for q in qs:
                            for j in range(2):
                                tok = slice(j * HALF, (j + 1) * HALF)
                                ins = mm3(PJ[:, p % 2, tok], wh[:, s, q * P:(q + 1) * P],
                                          wl[:, s, q * P:(q + 1) * P], XCh[:, GATE_TILES[q][0], tok],
                                          XCl[:, GATE_TILES[q][0], tok], q == qs[0], q == qs[-1],
                                          1 - s if t == 0 and q == qs[0] and j == 0 else None)
                        ins.then_inc(pj_full[p % 2], 1)
                for k in range(3):
                    up("lru", i, 5 + k, 9 + k)
                down("lru", i, 8, 12, G3h, G3l, RT, GREADY["lru"] + 3 * i)
            norm_sums("norm6")
            pe.wait_ge(x_scaled, 16)
            for t in range(8):
                start_tile("write", 0, t)
                for kt in range(KT):
                    ins = nc.tensor.transpose(PJ[:, t % 2, kt * P:(kt + 1) * P], X[:, kt, t * P:(t + 1) * P],
                                              ident[:, :])
                ins.then_inc(pj_full[t % 2], 1)

        @block.scalar
        def _(act):
            raise_starts(act, "act")
            def fn(out, in_, func, scale=1.0, bias=0.0):
                return nc.scalar.activation(out, in_, func, bias=bias, scale=scale)

            def norm(phase):
                first = 8 * NORMS.index(phase)
                used0 = 7 * NORMS.index(phase)
                for t in range(KT):
                    if phase == "norm4":
                        act.wait_ge(x_scaled, t + 1)
                    elif phase == "norm1":
                        for s in range(2):
                            act.wait_ge(pj_free[s], tile("read", 0, 6) + 1)
                    else:
                        ph, i, p = SOURCE[phase]
                        act.wait_ge(pj_free[t % 2], tile(ph, i, p + t) + 1)
                    if t >= 2:
                        act.wait_ge(sq_used, used0 + t - 1)
                    fn((A, B)[t % 2][:, :], X[:, t, :], ACT.Square).then_inc(sq_ready, 1)
                for j in range(2):
                    at = slice(j * HALF, (j + 1) * HALF)
                    act.wait_ge(ax_full[j], aux(phase, 0, j) + 1)
                    fn(C[:, at], AX[:, j, 0:HALF], ACT.Ln, 1.0 / D, eps[:, 0:1]).then_inc(ax_free[j], 1)
                    act.wait_ge(ax_free[j], aux(phase, 0, j) + 1)
                    fn(Dt[:, at], C[:, at], ACT.Exp, -0.5).then_inc(rstd_ready, 1)
                if phase in UREADY:
                    for t in range(KT):
                        act.wait_ge(y_ready, UREADY[phase] + t + 1)
                        fn(Uh[:, t, :], (A, B)[t % 2][:, :], ACT.Copy).then_inc(u_rounded, 1)

            for dst, name in ((ident, "ident"), (ones, "ones"), (group64, "group64"), (vec, "vec"),
                              (mbif, "mbif"), (cos, "cos"), (sin, "sin"), (decay, "decay"), (xi, "xi")):
                act.dma_start(dst[tuple(slice(None) for _ in dst.shape)], d[name]).then_inc(consts, 16)
            act.wait_ge(consts, CONSTS)
            act.wait_ge(consts_r, 4)
            for s in range(2):
                act.wait_ge(pj_free[s], tile("read", 0, 6) + 1)
            act.dma_start(x_kept, X[:, :, :]).then_inc(x_spilled, 16)
            norm("norm1")

            act.wait_ge(x_spilled, 16)
            act.wait_ge(u_ready, UREADY["norm1"] + 8)
            with act.Fori(0, RET_HEADS) as i:
                for q in range(2):
                    act.wait_ge(pj_full[q], tile("ret", i, q) + 1)
                    if q:
                        act.wait_ge(r["r_qxlo"], i + 1)
                    fn(A[64:128, :], PJ[0:64, q, :], ACT.Copy)
                    fn(A[0:64, :], PJ[64:128, q, :], ACT.Copy).then_inc(r["r_swapped"], 1)
                    act.wait_ge(r["r_rotated"], 2 * i + (q + 1))
                    if q == 0:
                        fn(Qh[:, :], B[:, :], ACT.Copy).then_inc(r["r_qhi"], 1)
                        act.wait_ge(r["r_qx"], i + 1)
                        fn(QXh[:, :], A[:, :], ACT.Copy).then_inc(r["r_qxhi"], 1)
                    else:
                        fn(Kh[:, :], B[:, :], ACT.Copy).then_inc(r["r_khi"], 1)
                act.wait_ge(pj_full[0], tile("ret", i, 2) + 1)
                act.wait_ge(g_ready, GREADY["ret"] + i)
                fn(C[:, :], PJ[:, 0, :], ACT.Copy).then_inc(pj_free[0], 1)
                act.wait_ge(ax_full[0], aux("ret", i, 0) + 1)
                fn(Kth[:, :], AX[:, 0, :], ACT.Copy, v("zeta", i)).then_inc(r["r_kthi"], 1)
                act.wait_ge(pj_full[1], tile("ret", i, 3) + 1)
                fn(Dt[:, :], PJ[:, 1, :], ACT.Silu).then_inc(pj_free[1], 1)
                act.wait_ge(ax_full[1], aux("ret", i, 1) + 1)
                fn(Vth[:, :], AX[:, 1, :], ACT.Copy).then_inc(r["r_vthi"], 1)
                act.wait_ge(ax_free[0], aux("ret", i, 2) + 1)
                fn(SMh[:, :], A[:, :], ACT.Copy).then_inc(r["r_smhi"], 1)
                act.wait_ge(ax_free[1], aux("ret", i, 3) + 1)
                fn(Kh[:, :], B[:, :], ACT.Copy).then_inc(r["r_shi"], 1)
                act.wait_ge(ax_full[0], aux("ret", i, 4) + 1)
                fn(C[:, :], AX[:, 0, :], ACT.Copy)
                act.wait_ge(r["r_smlo"], i + 1)
                fn(A[:, :], AX[:, 0, :], ACT.Square).then_inc(ax_free[0], 1)
                act.wait_ge(ax_full[1], aux("ret", i, 5) + 1)
                act.wait_ge(r["r_slo"], i + 1)
                fn(B[:, :], AX[:, 1, :], ACT.Ln, 1.0 / P, eps[:, 0:1]).then_inc(ax_free[1], 1)
                act.wait_ge(ax_free[1], aux("ret", i, 5) + 1)
                fn(B[:, :], B[:, :], ACT.Exp, -0.5).then_inc(r["r_rstd"], 1)
                act.wait_ge(r["r_y"], i + 1)
                fn(Gh[:, ds(i, 1), :].rearrange("p a s -> p (a s)"), C[:, :], ACT.Copy).then_inc(g_rounded, 1)

            with act.Fori(0, 2) as i:
                for cc in range(2):
                    p = 3 * cc
                    act.wait_ge(pj_full[p % 2], tile("conv", i, p) + 1)
                    act.wait_ge(c["c_y"], from1(2 * i + cc))
                    fn(A[:, :], PJ[:, p % 2, :], ACT.Copy).then_inc(pj_free[p % 2], 1)
                    p += 1
                    act.wait_ge(pj_full[p % 2], tile("conv", i, p) + 1)
                    act.wait_ge(c["c_n"], from1(2 * i + cc))
                    fn(B[:, :], PJ[:, p % 2, :], ACT.Copy).then_inc(pj_free[p % 2], 1)
                    act.wait_ge(c["c_y"], from1(2 * i + (cc + 1)))
                    fn(B[:, :], Dt[:, :], ACT.Square).then_inc(c["c_sq"], 1)
                    act.wait_ge(ax_full[cc], aux("conv", i, cc) + 1)
                    fn(B[:, :], AX[:, cc, :], ACT.Ln, 1.0 / 64, eps[:, 0:1]).then_inc(ax_free[cc], 1)
                    act.wait_ge(ax_free[cc], aux("conv", i, cc) + 1)
                    fn(B[:, :], B[:, :], ACT.Exp, -0.5).then_inc(c["c_rstd"], 1)
                    act.wait_ge(pj_full[1], tile("conv", i, 0))
                    act.wait_ge(c["c_n"], from1(2 * i + (cc + 1)))
                    fn(Gh[:, ds(2 * i + cc, 1), :].rearrange("p a s -> p (a s)"), Dt[:, :], ACT.Copy) \
                        .then_inc(g_rounded, 1)
            norm("norm2")

            with act.Fori(0, FF_BLOCKS) as i:
                def split(k):
                    act.wait_ge(f_sq, 4 * i + (k + 1))
                    fn(Gh[:, k, :], (A, B)[k % 2][:, :], ACT.Copy).then_inc(g_rounded, 1)

                for k in range(4):
                    act.wait_ge(pj_full[k % 2], tile("ffn", i, k) + 1)
                    act.wait_ge(g_ready, 4 * i + (GREADY["ffn"] + k - 1))
                    fn((A, B)[k % 2][:, :], PJ[:, k % 2, :], ACT.Relu).then_inc(pj_free[k % 2], 1)
                    if k == 0:
                        act.wait_ge(pj_full[1], tile("ffn", i, 0))
                    if k >= 1:
                        split(k - 1)
                split(3)
            norm("norm3")
            norm("norm4")

            for k in range(2):
                act.wait_ge(pj_full[k], tile("gate", 0, k) + 1)
                fn(GR[:, k, :], PJ[0:M_HEADS, k, :], ACT.Identity, 1.0, mbif[:, k:k + 1]).then_inc(pj_free[k], 1)
            for k in range(2):
                act.wait_ge(pj_free[k], tile("gate", 0, k) + 1)
            act.dma_start(gate_kept.rearrange("g h s -> h g s"), GR[:, :, :]).then_inc(m["g_stored"], 16)
            with act.Fori(0, MT // 2) as i:
                for jj in range(2):
                    j = 2 * i + jj
                    p = 3 * jj
                    s = p % 2
                    act.wait_ge(pj_full[s], tile("inner", i, p) + 1)
                    act.wait_ge(m["st_xm"], from16(32 * i + 16 * jj))
                    act.wait_ge(m["m_conv"], from1(2 * i + jj))
                    fn(A[:, :], PJ[:, s, :], ACT.Copy).then_inc(pj_free[s], 1)
                    act.wait_ge(pj_free[s], tile("inner", i, p) + 1)
                    act.dma_start(xm_kept[ds(j, 1), :, :].rearrange("a p s -> (a p) s"), A[:, :]) \
                        .then_inc(m["st_xm"], 16)
                    act.wait_ge(m["m_conv"], from1(2 * i + (jj + 1)))
                    act.wait_ge(m["st_xc"], from16(32 * i + 16 * jj))
                    act.wait_ge(m["m_zs"], from1(2 * i + jj))
                    fn(Fx[:, :], E[:, :], ACT.Silu).then_inc(m["m_xc"], 1)
                    act.wait_ge(m["m_xc"], from1(2 * i + (jj + 1)))
                    act.dma_start(xc_kept[ds(j, 1), :, :].rearrange("a p s -> (a p) s"), Fx[:, :]) \
                        .then_inc(m["st_xc"], 16)
                    s = 1 - s
                    act.wait_ge(pj_full[s], tile("inner", i, p + 1) + 1)
                    act.wait_ge(m["m_zn"], from1(2 * i + jj))
                    fn(H[:, :], PJ[:, s, :], ACT.Silu).then_inc(pj_free[s], 1)
                    s = 1 - s
                    act.wait_ge(pj_full[s], tile("inner", i, p + 2) + 1)
                    act.wait_ge(m["st_o"], from16(32 * i + 16 * jj))
                    fn(O[:, :], PJ[:, s, :], ACT.Sigmoid).then_inc(pj_free[s], 1)
                    act.wait_ge(pj_free[s], tile("inner", i, p + 2) + 1)
                    act.dma_start(o_kept[ds(j, 1), :, :].rearrange("a p s -> (a p) s"), O[:, :]) \
                        .then_inc(m["st_o"], 16)
                    act.wait_ge(m["m_zs"], from1(2 * i + (jj + 1)))
                    act.dma_start(zs_kept[ds(j, 1), :, :].rearrange("a p s -> (a p) s"), Q[:, :]) \
                        .then_inc(m["st_zs"], 16)
                    act.wait_ge(m["m_zn"], from1(2 * i + (jj + 1)))
                    act.dma_start(zn_kept[ds(j, 1), :, :].rearrange("a p s -> (a p) s"), B[:, :]) \
                        .then_inc(m["st_zn"], 16)

            act.wait_ge(m["g_stored"], 16)
            for s in range(2):
                act.wait_ge(pj_full[s], tile("mlstm", 0, 0))
            act.dma_start(gi[:, :], gate_kept[0].rearrange("h (c t) -> (h c) t", t=CHUNK)).then_inc(m["g_back"], 16)
            act.dma_start(gf[:, :], gate_kept[1].rearrange("h (c t) -> (h c) t", t=CHUNK)).then_inc(m["g_back"], 16)
            for s in ("st_xm", "st_xc", "st_o", "st_zn", "st_zs"):
                act.wait_ge(m[s], from16(16 * MT))
            act.dma_start(negmask[:, :], d["negmask"]).then_inc(m["g_back"], 16)
            act.wait_ge(m["g_back"], 48)
            fn(ga[:, :], gf[:, :], ACT.Abs).then_inc(m["ga_abs"], 1)
            fn(ltmp[:, 0, :], v("lam", 0, R_TILES), ACT.Abs).then_inc(m["lam_abs"], 1)
            act.wait_ge(m["ga_abs"], 1)
            fn(ga[:, :], ga[:, :], ACT.Exp, -1.0).then_inc(m["ga_exp"], 1)
            act.wait_ge(m["lam_abs"], 1)
            fn(ltmp[:, 0, :], ltmp[:, 0, :], ACT.Exp, -1.0).then_inc(m["lam_exp"], 1)
            act.wait_ge(m["ga_last"], 2)
            for k in range(2):
                act.dma_start(last_kept[k].rearrange("(r a) -> r a", a=1), gcol[:, k:k + 1]).then_inc(m["ga_lastback"], 16)
            act.wait_ge(m["ga_lastback"], 32)
            act.dma_start(sc4[:, 0:2, 0:NCH], last_kept[0:2].rearrange("k (h c) -> h k c", c=NCH)) \
                .then_inc(m["ga_lastback"], 16)
            act.wait_ge(m["ga_m"], 2)
            act.dma_start(last_kept[2].rearrange("(h c) -> h c", c=NCH), sc4[:, 2, 0:NCH]).then_inc(m["ga_mback"], 16)
            act.wait_ge(m["ga_mback"], 16)
            act.dma_start(gcol[:, 2:3], last_kept[2].rearrange("(r a) -> r a", a=1)).then_inc(m["ga_mback"], 16)
            act.wait_ge(m["ga_rows"], 2)
            fn(g5[:, 2, :], g5[:, 1, :], ACT.Exp, 1.0, gcol[:, 2:3]).then_inc(m["ga_exps"], 1)
            fn(g5[:, 3, :], gb[:, :], ACT.Exp, -1.0).then_inc(m["ga_exps"], 1)
            fn(g5[:, 4, :], g5[:, 0, :], ACT.Exp, 1.0, gcol[:, 3:4]).then_inc(m["ga_exps"], 1)
            act.wait_ge(ax_full[0], aux("gate", 0, 0) + 1)
            fn(cols[:, :, :].rearrange("p q r -> p (q r)"), AX[:, 0, 0:5 * ROWS], ACT.Copy).then_inc(ax_free[0], 1)
            act.wait_ge(ax_full[1], aux("gate", 0, 1) + 1)
            fn(dlb[:, :], AX[:, 1, 0:ROWS], ACT.Copy).then_inc(ax_free[1], 1)

            with act.Fori(0, M_HEADS) as i:
                def stage(u):
                    act.wait_ge(h["h_x%d" % (u % 2)], 64 * i + 16 * (u // 2 + 1))
                    fn(GXh[:, u % 4, :], (A, B)[u % 2][:, :], ACT.Copy).then_inc(h["h_xround"], 1)

                act.wait_ge(pj_full[1], tile("mlstm", i, 0))
                for u in range(4):
                    stage(u)
                for p in range(4):
                    act.wait_ge(pj_full[p % 2], tile("mlstm", i, p) + 1)
                    fn(Vh[:, 2 * p:2 * p + 2, :].rearrange("p a s -> p (a s)"), PJ[:, p % 2, :], ACT.Copy) \
                        .then_inc(h["h_vhi"], 1)
                for u in range(4, 8):
                    stage(u)
                for kk in range(KK):
                    act.wait_ge(pj_full[kk], tile("mlstm", i, 4 + kk) + 1)
                    fn(Mqh[:, kk, :], PJ[:, kk, :], ACT.Copy, DK ** -0.5).then_inc(h["h_qhi"], 1)
                for kk in range(KK):
                    act.wait_ge(pj_full[kk], tile("mlstm", i, 6 + kk) + 1)
                    fn(Mkh[:, kk, :], PJ[:, kk, :], ACT.Copy).then_inc(h["h_khi"], 1)
                act.wait_ge(ax_free[0], aux("mlstm", i, 0) + 1)
                fn(Dt[:, :], Dt[:, :], ACT.Exp).then_inc(h["h_w"], 1)
                act.wait_ge(ax_free[1], aux("mlstm", i, 1) + 1)
                fn(Msh[:, :], B[:, :], ACT.Copy).then_inc(h["h_smhi"], 1)
                for kk in range(KK):
                    act.wait_ge(ax_free[kk], aux("mlstm", i, 2 + kk) + 1)
                    fn(Mkh[:, kk, :], (A, B)[kk][:, :], ACT.Copy).then_inc(h["h_kthi"], 1)
                for step in range(NCH + 2):
                    if step < NCH:
                        g = NCH * i + step
                        act.wait_ge(h["h_c"], g + 1)
                        act.wait_ge(h["h_qc"], from1(g))
                        fn(Ch[:, :, :], Cf[:, :, :], ACT.Copy).then_inc(h["h_chi"], 1)
                    if 1 <= step <= NCH:
                        act.wait_ge(h["h_st2"], NCH * i + step)
                        fn(mst[:, 2:3], mst[:, 1:2], ACT.Sqrt, 1.0, eps[:, 0:1]).then_inc(h["h_std"], 1)
                    if step < NCH:
                        act.wait_ge(h["h_qc"], from1(g + 1))
                        act.wait_ge(h["h_num"], from1(g))
                        if step == 0:
                            act.wait_ge(h["h_ktlo"], 2 * i + 2)
                        fn(t1[:, :], PJ[:, 0, 0:DV], ACT.Copy, hc[:, 2, step:step + 1]).then_inc(h["h_t1"], 1)
                    if step >= 2:
                        n = step - 2
                        act.wait_ge(h["h_y"], from1(NCH * i + (n + 1)))
                        fn(GXh[:, :, n * P:(n + 1) * P], yy[:, :].rearrange("p (t s) -> p t s", t=VT),
                           ACT.Copy).then_inc(h["h_yhi"], 1)
            norm("norm5")

            with act.Fori(0, R_PAIRS) as i:
                for t in range(RT):
                    s = t % 2
                    act.wait_ge(pj_full[s], tile("lru", i, t) + 1)
                    act.wait_ge(l["l_xc"], from1(3 * i + t))
                    if t == 0:
                        act.wait_ge(g_ready, 3 * i + GREADY["lru"])
                    fn(A[:, :], PJ[:, s, :], ACT.Copy).then_inc(pj_free[s], 1)
                    act.wait_ge(l["l_xc"], from1(3 * i + (t + 1)))
                    fn(XCh[:, t, :], B[:, :], ACT.Copy).then_inc(l["l_xchi"], 1)
                for t in range(RT):
                    s = (3 + t) % 2
                    act.wait_ge(pj_full[s], tile("lru", i, 3 + t) + 1)
                    fn(R3[:, t, :], PJ[:, s, :], ACT.Sigmoid, 1.0, v("rba", 3 * i + t)).then_inc(pj_free[s], 1)
                for t in range(RT):
                    s = (6 + t) % 2
                    act.wait_ge(pj_full[s], tile("lru", i, 6 + t) + 1)
                    act.wait_ge(l["l_h"], from1(3 * i + t))
                    fn(B[:, :], PJ[:, s, :], ACT.Sigmoid, 1.0, v("rbx", 3 * i + t)).then_inc(pj_free[s], 1)
                    act.wait_ge(l["l_rate"], 3 * i + (t + 1))
                    fn(C[:, :], R3[:, t, :], ACT.Exp)
                    fn(Dt[:, :], R3[:, t, :], ACT.Tanh).then_inc(l["l_th"], 1)
                    act.wait_ge(l["l_e"], 3 * i + (t + 1))
                    fn(Dt[:, :], R3[:, t, :], ACT.Sqrt, -1.0).then_inc(l["l_sqrt"], 1)
                act.wait_ge(pj_full[1], tile("lru", i, 0))
                for t in range(RT):
                    s = (9 + t) % 2
                    act.wait_ge(pj_full[s], tile("lru", i, 9 + t) + 1)
                    act.wait_ge(l["l_x"], 3 * i + 3)
                    act.wait_ge(g_ready, 3 * i + (GREADY["lru"] + t))
                    fn(A[:, :], PJ[:, s, :], ACT.Silu).then_inc(pj_free[s], 1)
                    act.wait_ge(l["l_y"], 3 * i + (t + 1))
                    fn(G3h[:, t, :], A[:, :], ACT.Copy).then_inc(g_rounded, 1)
            norm("norm6")

        @block.vector
        def _(dve):
            raise_starts(dve, "dve")
            V = nc.vector

            def tt(out, a, b, op=ALU.mult):
                return V.tensor_tensor(out, a, b, op)

            def stt(out, a, s, b, op0=ALU.mult, op1=ALU.add):
                return V.scalar_tensor_tensor(out=out, in0=a, scalar=s, in1=b, op0=op0, op1=op1)

            def lo(out, whole, hi):
                return V.tensor_tensor(out, whole, hi.bitcast(F32), ALU.subtract)

            def norm(phase):
                dve.wait_ge(rstd_ready, 2 * NORMS.index(phase) + 2)
                g = GAINS[phase]
                if phase not in UREADY:
                    for t in range(KT):
                        stt(X[:, t, :], X[:, t, :], v(g, t), Dt[:, :], ALU.mult, ALU.mult).then_inc(x_scaled, 1)
                    return
                for t in range(KT + 1):
                    if t < KT:
                        if t >= 2:
                            dve.wait_ge(u_ready, UREADY[phase] + t - 1)
                        stt((A, B)[t % 2][:, :], X[:, t, :], v(g, t), Dt[:, :], ALU.mult, ALU.mult) \
                            .then_inc(y_ready, 1)
                    if t >= 1:
                        dve.wait_ge(u_rounded, UREADY[phase] + t)
                        lo(Ul[:, t - 1, :], (A, B)[(t - 1) % 2][:, :], Uh[:, t - 1, :]).then_inc(u_ready, 1)

            def add_down(phase, i, p0):
                for t in range(KT):
                    s = (p0 + t) % 2
                    dve.wait_ge(pj_full[s], tile(phase, i, p0 + t) + 1)
                    tt(X[:, t, :], PJ[:, s, :], X[:, t, :], ALU.add).then_inc(pj_free[s], 1)

            V.memset(eps[:, :], EPS).then_inc(consts_r, 1)
            V.memset(zero[:, :], 0.0).then_inc(consts_r, 1)
            dve.wait_ge(consts, CONSTS)
            V.tensor_copy(identr[:, :], ident[:, :]).then_inc(consts_r, 1)
            V.tensor_copy(onesr[:, :], ones[:, 0:4]).then_inc(consts_r, 1)
            for t in range(8):
                dve.wait_ge(pj_full[t % 2], tile("read", 0, t) + 1)
                V.tensor_copy(X[:, :, t * P:(t + 1) * P], PJ[:, t % 2, :].rearrange("p (k s) -> p k s", k=KT)) \
                    .then_inc(pj_free[t % 2], 1)
            norm("norm1")

            dve.wait_ge(x_spilled, 16)
            by_chunk = lambda a: a[:, :].rearrange("p (n s) -> p n s", n=NCH)
            with dve.Fori(0, RET_HEADS) as i:
                for q in range(2):
                    scale = 1.0 if q == 0 else float(P) ** -0.5
                    dve.wait_ge(pj_full[q], tile("ret", i, q) + 1)
                    dve.wait_ge(r["r_swapped"], 2 * i + (q + 1))
                    stt(B[:, :], PJ[:, q, :], scale, cos[:, :], ALU.mult, ALU.mult).then_inc(pj_free[q], 1)
                    stt(A[:, :], A[:, :], scale, sin[:, :], ALU.mult, ALU.mult).then_inc(r["r_sin"], 1)
                    dve.wait_ge(pj_free[q], tile("ret", i, q) + 1)
                    dve.wait_ge(r["r_sin"], 2 * i + (q + 1))
                    tt(B[:, :], B[:, :], A[:, :], ALU.add).then_inc(r["r_rotated"], 1)
                    dve.wait_ge(r["r_rotated"], 2 * i + (q + 1))
                    if q == 0:
                        tt(by_chunk(A), by_chunk(B), xi[:, ds(i, 1), :].broadcast_to([P, NCH, P])) \
                            .then_inc(r["r_qx"], 1)
                        dve.wait_ge(r["r_qhi"], i + 1)
                        lo(Ql[:, :], B[:, :], Qh[:, :]).then_inc(r["r_qlo"], 1)
                        dve.wait_ge(r["r_qxhi"], i + 1)
                        lo(QXl[:, :], A[:, :], QXh[:, :]).then_inc(r["r_qxlo"], 1)
                    else:
                        dve.wait_ge(r["r_khi"], i + 1)
                        lo(Kl[:, :], B[:, :], Kh[:, :]).then_inc(r["r_klo"], 1)
                dve.wait_ge(r["r_kthi"], i + 1)
                stt(Ktl[:, :], AX[:, 0, :], v("zeta", i), Kth[:, :].bitcast(F32), ALU.mult, ALU.subtract) \
                    .then_inc(ax_free[0], 1)
                dve.wait_ge(r["r_vthi"], i + 1)
                lo(Vtl[:, :], AX[:, 1, :], Vth[:, :]).then_inc(ax_free[1], 1)
                dve.wait_ge(ax_full[0], aux("ret", i, 2) + 1)
                tt(by_chunk(A), by_chunk(AX[:, 0, :]), decay[:, ds(i, 1), :].broadcast_to([P, NCH, P])) \
                    .then_inc(ax_free[0], 1)
                V.memset(B[:, 0:P], 0.0).then_inc(r["r_state"], 1)
                dve.wait_ge(ax_full[1], aux("ret", i, 3) + 1)
                for n in range(NCH - 1):
                    dve.wait_ge(r["r_state"], 7 * i + (n + 1))
                    ins = stt(B[:, (n + 1) * P:(n + 2) * P], B[:, n * P:(n + 1) * P], v("chunk_decay", i),
                              AX[:, 1, n * P:(n + 1) * P])
                    if n < NCH - 2:
                        ins.then_inc(r["r_state"], 1)
                    else:
                        ins.then_inc(ax_free[1], 1)
                dve.wait_ge(r["r_smhi"], i + 1)
                lo(SMl[:, :], A[:, :], SMh[:, :]).then_inc(r["r_smlo"], 1)
                dve.wait_ge(r["r_shi"], i + 1)
                lo(Kl[:, :], B[:, :], Kh[:, :]).then_inc(r["r_slo"], 1)
                dve.wait_ge(r["r_rstd"], i + 1)
                stt(C[:, :], C[:, :], v("rng", i), B[:, :], ALU.mult, ALU.mult).then_inc(r["r_y1"], 1)
                dve.wait_ge(r["r_y1"], i + 1)
                dve.wait_ge(pj_free[1], tile("ret", i, 3) + 1)
                tt(C[:, :], C[:, :], Dt[:, :]).then_inc(r["r_y"], 1)
                dve.wait_ge(g_rounded, i + (GREADY["ret"] + 1))
                tt(Gl[:, ds(i, 1), :].rearrange("p a s -> p (a s)"), C[:, :],
                   Gh[:, ds(i, 1), :].rearrange("p a s -> p (a s)").bitcast(F32), ALU.subtract).then_inc(g_ready, 1)
            dve.wait_ge(x_back, 16)
            add_down("ret_down", 0, 0)

            V.memset(Cp[:, 0:8], 0.0).then_inc(c["c_pad"], 1)
            dve.wait_ge(c["c_pad"], 1)
            with dve.Fori(0, 2) as i:
                for cc in range(2):
                    q = 2 * i + cc
                    p = 3 * cc + 2
                    dve.wait_ge(pj_full[p % 2], tile("conv", i, p) + 1)
                    dve.wait_ge(pj_free[(p - 1) % 2], tile("conv", i, p - 1) + 1)
                    tt(Cp[:, 8:8 + S], PJ[:, p % 2, :], B[:, :]).then_inc(pj_free[p % 2], 1)
                    dve.wait_ge(pj_free[p % 2], tile("conv", i, p) + 1)
                    V.tensor_scalar(Dt[:, :], Cp[:, 6:6 + S], v("cnw", q), None, ALU.mult).then_inc(c["c_0"], 1)
                    dve.wait_ge(c["c_0"], 2 * i + (cc + 1))
                    stt(Dt[:, :], Cp[:, 7:7 + S], v("cnw", CONV_TILES + q), Dt[:, :]).then_inc(c["c_1"], 1)
                    dve.wait_ge(c["c_1"], 2 * i + (cc + 1))
                    stt(Dt[:, :], Cp[:, 8:8 + S], v("cnw", 2 * CONV_TILES + q), Dt[:, :]).then_inc(c["c_2"], 1)
                    dve.wait_ge(c["c_2"], 2 * i + (cc + 1))
                    dve.wait_ge(pj_free[(p - 2) % 2], tile("conv", i, p - 2) + 1)
                    tt(Dt[:, :], Dt[:, :], A[:, :]).then_inc(c["c_y"], 1)
                    dve.wait_ge(c["c_rstd"], 2 * i + (cc + 1))
                    stt(Dt[:, :], Dt[:, :], v("cng", q), B[:, :], ALU.mult, ALU.mult).then_inc(c["c_n"], 1)
                    dve.wait_ge(g_rounded, 2 * i + (GREADY["conv"] + cc + 1))
                    tt(Gl[:, ds(q, 1), :].rearrange("p a s -> p (a s)"), Dt[:, :],
                       Gh[:, ds(q, 1), :].rearrange("p a s -> p (a s)").bitcast(F32), ALU.subtract) \
                        .then_inc(g_ready, 1)
            add_down("conv_down", 0, 0)
            norm("norm2")

            with dve.Fori(0, FF_BLOCKS) as i:
                for k in range(5):
                    if k < 4:
                        T = (A, B)[k % 2]
                        dve.wait_ge(pj_free[k % 2], tile("ffn", i, k) + 1)
                        tt(T[:, :], T[:, :], T[:, :]).then_inc(f_sq, 1)
                    if k >= 1:
                        dve.wait_ge(g_rounded, 4 * i + (GREADY["ffn"] + k))
                        lo(Gl[:, k - 1, :], (A, B)[(k - 1) % 2][:, :], Gh[:, k - 1, :]).then_inc(g_ready, 1)
                add_down("ffn", i, 4)
            norm("norm3")
            dve.wait_ge(x_scaled, 8)
            norm("norm4")

            V.memset(Ap[:, 0:8], 0.0).then_inc(m["m_pad"], 1)
            dve.wait_ge(m["m_pad"], 1)
            with dve.Fori(0, MT // 2) as i:
                for jj in range(2):
                    j = 2 * i + jj
                    p = 3 * jj
                    dve.wait_ge(pj_free[p % 2], tile("inner", i, p) + 1)
                    dve.wait_ge(m["m_xc"], from1(2 * i + jj))
                    V.tensor_scalar(E[:, :], Ap[:, 5:5 + S], v("mcw", j), v("mcb", j), ALU.mult, ALU.add) \
                        .then_inc(m["m_c0"], 1)
                    dve.wait_ge(m["m_c0"], 2 * i + (jj + 1))
                    stt(E[:, :], Ap[:, 6:6 + S], v("mcw", MT + j), E[:, :]).then_inc(m["m_c1"], 1)
                    dve.wait_ge(m["m_c1"], 2 * i + (jj + 1))
                    stt(E[:, :], Ap[:, 7:7 + S], v("mcw", 2 * MT + j), E[:, :]).then_inc(m["m_c2"], 1)
                    dve.wait_ge(m["m_c2"], 2 * i + (jj + 1))
                    stt(E[:, :], Ap[:, 8:8 + S], v("mcw", 3 * MT + j), E[:, :]).then_inc(m["m_conv"], 1)
                    dve.wait_ge(pj_free[(p + 1) % 2], tile("inner", i, p + 1) + 1)
                    dve.wait_ge(m["m_xc"], from1(2 * i + (jj + 1)))
                    dve.wait_ge(m["st_zs"], from16(32 * i + 16 * jj))
                    stt(Q[:, :], Fx[:, :], v("msk", j), H[:, :], ALU.mult, ALU.mult).then_inc(m["m_zs"], 1)
                    dve.wait_ge(m["st_zn"], from16(32 * i + 16 * jj))
                    V.tensor_scalar(B[:, :], H[:, :], v("mnw", j), None, ALU.mult).then_inc(m["m_zn"], 1)

            steps = [0]

            def step(ins):
                steps[0] += 1
                ins.then_inc(m["ga_step"], 1)
                dve.wait_ge(m["ga_step"], steps[0])

            def half_log1p(e, z, zz, out):
                step(V.tensor_scalar(z, e, 2.0, None, ALU.add))
                step(V.reciprocal(z, z))
                step(tt(z, e, z))
                step(tt(zz, z, z))
                step(V.tensor_scalar(out, zz, 1.0 / 15, None, ALU.mult))
                for n in (13, 11, 9, 7, 5, 3):
                    step(stt(out, out, 1.0 / n, zz, ALU.add, ALU.mult))
                step(stt(out, out, 1.0, z, ALU.add, ALU.mult))

            dve.wait_ge(m["lam_exp"], 1)
            half_log1p(ltmp[:, 0, :], ltmp[:, 1, :], ltmp[:, 2, :], ltmp[:, 3, :])
            step(V.tensor_scalar(ltmp[:, 1, :], v("lam", 0, R_TILES), -1.0, 0.0, ALU.mult, ALU.max))
            step(stt(ltmp[:, 2, :], ltmp[:, 3, :], 2.0, ltmp[:, 1, :]))
            step(V.tensor_scalar(lra[:, :], ltmp[:, 2, :], -8.0, None, ALU.mult))
            dve.wait_ge(m["ga_exp"], 1)
            half_log1p(ga[:, :], gb[:, :], gc_[:, :], gF[:, :])
            step(V.tensor_scalar(gb[:, :], gf[:, :], 0.0, None, ALU.min))
            step(stt(gc_[:, :], gF[:, :], -2.0, gb[:, :]))
            step(V.memset(gone[:, :], 1.0))
            step(V.memset(gzero[:, :], 0.0))
            step(V.tensor_tensor_scan(gF[:, :], gone[:, :], gc_[:, :], 0.0, ALU.mult, ALU.add))
            step(tt(g5[:, 0, :], gi[:, :], gF[:, :], ALU.subtract))
            step(V.tensor_tensor_scan(gA[:, :], g5[:, 0, :], gzero[:, :], -3.0e38, ALU.max, ALU.add))
            V.tensor_copy(gcol[:, 0:1], gF[:, CHUNK - 1:CHUNK]).then_inc(m["ga_last"], 1)
            V.tensor_copy(gcol[:, 1:2], gA[:, CHUNK - 1:CHUNK]).then_inc(m["ga_last"], 1)
            dve.wait_ge(m["ga_lastback"], 48)
            V.memset(sc4[:, 2, 0:1], 0.0).then_inc(m["ga_m"], 1)
            V.tensor_tensor_scan(sc4[:, 2, 1:NCH + 1], sc4[:, 1, 0:NCH], sc4[:, 0, 0:NCH], 0.0,
                                 ALU.max, ALU.add).then_inc(m["ga_m"], 1)
            dve.wait_ge(m["ga_mback"], 32)
            step(V.tensor_scalar(gM[:, :], gA[:, :], gcol[:, 2:3], None, ALU.max))
            step(tt(gb[:, :], gF[:, :], gM[:, :], ALU.add))
            V.tensor_scalar(gcol[:, 3:4], gM[:, CHUNK - 1:CHUNK], -1.0, None, ALU.mult).then_inc(m["ga_rows"], 1)
            V.tensor_scalar(g5[:, 1, :], gM[:, :], -1.0, None, ALU.mult).then_inc(m["ga_rows"], 1)
            dve.wait_ge(m["ga_exps"], 1)
            V.tensor_scalar(gdiag[:, :], ident[0:ROWS, 0:ROWS], g5[:, 2, CHUNK - 1:CHUNK], None, ALU.mult) \
                .then_inc(m["ga_dl"], 1)
            for s in range(2):
                dve.wait_ge(ax_free[s], aux("gate", 0, s) + 1)

            with dve.Fori(0, M_HEADS) as i:
                V.tensor_copy(hc[:, 0:5, :], cols[:, :, ds(NCH * i, NCH)])
                V.tensor_copy(hc[:, 5, :], dlb[:, ds(NCH * i, NCH)]).then_inc(h["h_hc"], 1)
                dve.wait_ge(h["h_hc"], i + 1)
                tt(by_chunk(Dt), ident[:, :].unsqueeze(1).broadcast_to([P, NCH, P]),
                   hc[:, 1, :].unsqueeze(2).broadcast_to([P, NCH, P])).then_inc(h["h_diag"], 1)

                def stage(u):
                    dve.wait_ge(h["h_xround"], 8 * i + (u + 1))
                    lo(GXl[:, u % 4, :], (A, B)[u % 2][:, :], GXh[:, u % 4, :]).then_inc(h["h_xsplit"], 1)

                for u in range(4):
                    stage(u)
                for p in range(4):
                    dve.wait_ge(h["h_vhi"], 4 * i + (p + 1))
                    lo(Vl[:, 2 * p:2 * p + 2, :].rearrange("p a s -> p (a s)"), PJ[:, p % 2, :],
                       Vh[:, 2 * p:2 * p + 2, :].rearrange("p a s -> p (a s)")).then_inc(pj_free[p % 2], 1)
                dve.wait_ge(ax_full[0], aux("mlstm", i, 0) + 1)
                tt(by_chunk(Dt), by_chunk(AX[:, 0, :]), hc[:, 0, :].unsqueeze(2).broadcast_to([P, NCH, P]),
                   ALU.add).then_inc(ax_free[0], 1)
                for u in range(4, 8):
                    stage(u)
                for kk in range(KK):
                    dve.wait_ge(h["h_qhi"], 2 * i + (kk + 1))
                    stt(Mql[:, kk, :], PJ[:, kk, :], DK ** -0.5, Mqh[:, kk, :].bitcast(F32), ALU.mult,
                        ALU.subtract).then_inc(pj_free[kk], 1)
                for kk in range(KK):
                    dve.wait_ge(h["h_khi"], 2 * i + (kk + 1))
                    lo(Mkl[:, kk, :], PJ[:, kk, :], Mkh[:, kk, :]).then_inc(pj_free[kk], 1)
                dve.wait_ge(h["h_w"], i + 1)
                dve.wait_ge(ax_full[1], aux("mlstm", i, 1) + 1)
                tt(B[:, :], AX[:, 1, :], Dt[:, :]).then_inc(ax_free[1], 1)
                dve.wait_ge(h["h_smhi"], i + 1)
                lo(Msl[:, :], B[:, :], Msh[:, :]).then_inc(h["h_smlo"], 1)
                dve.wait_ge(h["h_smlo"], i + 1)
                for kk in range(KK):
                    dve.wait_ge(ax_full[kk], aux("mlstm", i, 2 + kk) + 1)
                    tt(by_chunk((A, B)[kk]), by_chunk(AX[:, kk, :]),
                       hc[:, 4, :].unsqueeze(2).broadcast_to([P, NCH, P])).then_inc(ax_free[kk], 1)
                for kk in range(KK):
                    dve.wait_ge(h["h_kthi"], 2 * i + (kk + 1))
                    lo(Mkl[:, kk, :], (A, B)[kk][:, :], Mkh[:, kk, :]).then_inc(h["h_ktlo"], 1)
                V.memset(Cf[:, :, :], 0.0).then_inc(h["h_c"], 1)
                for step in range(NCH + 2):
                    if 1 <= step < NCH:
                        n = step - 1
                        dve.wait_ge(h["h_cu"], 7 * i + step)
                        dve.wait_ge(h["h_clo"], NCH * i + step)
                        stt(Cf[:, :, 0:DV], Cf[:, :, 0:DV], hc[:, 5, n:n + 1],
                            AX[:, 0, :].rearrange("p (k a) -> p k a", k=KK))
                        stt(Cf[:, :, DV:DV + 2], Cf[:, :, DV:DV + 2], hc[:, 5, n:n + 1],
                            AX[:, 1, HALF:HALF + 4].rearrange("p (k a) -> p k a", k=KK)).then_inc(h["h_c"], 1)
                    if 1 <= step <= NCH:
                        n = step - 1
                        g = NCH * i + n
                        dve.wait_ge(h["h_qc"], from1(g + 1))
                        V.tensor_scalar(dcol[:, 0:1], AX[:, 1, 0:1], hc[:, 2, n:n + 1], AX[:, 1, 2:3], ALU.mult,
                                        ALU.add).then_inc(h["h_den"], 1)
                        dve.wait_ge(h["h_den"], from1(g + 1))
                        V.tensor_scalar(dcol[:, 3:4], dcol[:, 0:1], -1.0, hc[:, 3, n:n + 1], ALU.mult,
                                        ALU.max).then_inc(h["h_d0"], 1)
                        dve.wait_ge(h["h_t1"], from1(g + 1))
                        dve.wait_ge(h["h_sv"], g + 1)
                        tt(num[:, :], PJ[:, 0, DV:2 * DV], t1[:, :], ALU.add).then_inc(h["h_num"], 1)
                        dve.wait_ge(h["h_d0"], g + 1)
                        tt(dcol[:, 1:2], dcol[:, 0:1], dcol[:, 3:4], ALU.max).then_inc(h["h_d1"], 1)
                        dve.wait_ge(h["h_d1"], g + 1)
                        V.reciprocal(dcol[:, 2:3], dcol[:, 1:2]).then_inc(h["h_d2"], 1)
                        dve.wait_ge(h["h_oT"], from1(g + 1))
                        dve.wait_ge(h["h_num"], from1(g + 1))
                        dve.wait_ge(h["h_d2"], g + 1)
                        dve.wait_ge(h["h_hnT"], from1(g))
                        stt(hh[:, :], num[:, :], dcol[:, 2:3], PJ[:, 1, 0:DV], ALU.mult, ALU.mult) \
                            .then_inc(h["h_hh"], 1)
                        dve.wait_ge(h["h_hh"], from1(g + 1))
                        V.bn_stats(bst[:, 0:6], hh[:, :]).then_inc(h["h_st"], 1)
                        dve.wait_ge(h["h_st"], g + 1)
                        V.memset(dcol[:, 7:8], 0.0)
                        V.bn_aggr(mst[:, 0:2], bst[:, 0:6]).then_inc(h["h_st2"], 1)
                    if step < NCH:
                        g = NCH * i + step
                        dve.wait_ge(h["h_chi"], g + 1)
                        lo(Cl[:, :, :], Cf[:, :, :], Ch[:, :, :]).then_inc(h["h_clo"], 1)
                    if step >= 2:
                        g = NCH * i + (step - 2)
                        dve.wait_ge(h["h_hnT"], from1(g + 1))
                        dve.wait_ge(h["h_znc"], 16 * g + 16)
                        dve.wait_ge(h["h_done"], from1(g))
                        tt(yy[:, :], PJ[:, 1, DV:2 * DV], znc[:, :, :].rearrange("p t s -> p (t s)")) \
                            .then_inc(h["h_y1"], 1)
                    if 1 <= step <= NCH:
                        g = NCH * i + (step - 1)
                        dve.wait_ge(h["h_std"], g + 1)
                        V.reciprocal(mst[:, 3:4], mst[:, 2:3]).then_inc(h["h_rs"], 1)
                        dve.wait_ge(h["h_rs"], g + 1)
                        V.tensor_scalar(hh[:, :], hh[:, :], mst[:, 0:1], mst[:, 3:4], ALU.subtract, ALU.mult) \
                            .then_inc(h["h_hn"], 1)
                add_down("mlstm", i, 8)
            norm("norm5")

            V.memset(Ap[:, 0:8], 0.0).then_inc(l["l_pad"], 1)
            dve.wait_ge(l["l_pad"], 1)
            with dve.Fori(0, R_PAIRS) as i:
                for t in range(RT):
                    j = 3 * i + t
                    dve.wait_ge(pj_free[t % 2], tile("lru", i, t) + 1)
                    dve.wait_ge(l["l_xclo"], from1(3 * i + t))
                    V.tensor_scalar(B[:, :], Ap[:, 5:5 + S], v("rcw", j), v("rcb", j), ALU.mult, ALU.add) \
                        .then_inc(l["l_c0"], 1)
                    dve.wait_ge(l["l_c0"], 3 * i + (t + 1))
                    stt(B[:, :], Ap[:, 6:6 + S], v("rcw", R_TILES + j), B[:, :]).then_inc(l["l_c1"], 1)
                    dve.wait_ge(l["l_c1"], 3 * i + (t + 1))
                    stt(B[:, :], Ap[:, 7:7 + S], v("rcw", 2 * R_TILES + j), B[:, :]).then_inc(l["l_c2"], 1)
                    dve.wait_ge(l["l_c2"], 3 * i + (t + 1))
                    stt(B[:, :], Ap[:, 8:8 + S], v("rcw", 3 * R_TILES + j), B[:, :]).then_inc(l["l_xc"], 1)
                    dve.wait_ge(l["l_xchi"], 3 * i + (t + 1))
                    lo(XCl[:, t, :], B[:, :], XCh[:, t, :]).then_inc(l["l_xclo"], 1)
                for t in range(RT):
                    j = 3 * i + t
                    dve.wait_ge(pj_free[(3 + t) % 2], tile("lru", i, 3 + t) + 1)
                    V.tensor_scalar(R3[:, t, :], R3[:, t, :], lra[:, ds(j, 1)], None, ALU.mult) \
                        .then_inc(l["l_rate"], 1)
                for t in range(RT):
                    dve.wait_ge(l["l_ix"], from1(3 * i + t))
                    tt(A[:, :], XCh[:, t, :].bitcast(F32), XCl[:, t, :].bitcast(F32), ALU.add).then_inc(l["l_x"], 1)
                    dve.wait_ge(l["l_x"], 3 * i + (t + 1))
                    dve.wait_ge(pj_free[(6 + t) % 2], tile("lru", i, 6 + t) + 1)
                    tt(B[:, :], B[:, :], A[:, :]).then_inc(l["l_ix"], 1)
                    dve.wait_ge(l["l_th"], 3 * i + (t + 1))
                    tt(R3[:, t, :], C[:, :], C[:, :]).then_inc(l["l_aa"], 1)
                    dve.wait_ge(l["l_aa"], 3 * i + (t + 1))
                    stt(R3[:, t, :], R3[:, t, :], 1.0, Dt[:, :], ALU.add, ALU.mult).then_inc(l["l_e"], 1)
                    dve.wait_ge(l["l_sqrt"], 3 * i + (t + 1))
                    dve.wait_ge(l["l_ix"], from1(3 * i + (t + 1)))
                    tt(B[:, :], B[:, :], Dt[:, :]).then_inc(l["l_bt"], 1)
                    dve.wait_ge(l["l_bt"], 3 * i + (t + 1))
                    V.tensor_tensor_scan(R3[:, t, :], C[:, :], B[:, :], 0.0, ALU.mult, ALU.add) \
                        .then_inc(l["l_h"], 1)
                for t in range(RT):
                    dve.wait_ge(pj_free[(9 + t) % 2], tile("lru", i, 9 + t) + 1)
                    dve.wait_ge(l["l_h"], from1(3 * i + (t + 1)))
                    tt(A[:, :], A[:, :], R3[:, t, :]).then_inc(l["l_y"], 1)
                    dve.wait_ge(g_rounded, 3 * i + (GREADY["lru"] + t + 1))
                    lo(G3l[:, t, :], A[:, :], G3h[:, t, :]).then_inc(g_ready, 1)
                add_down("lru", i, 12)
            norm("norm6")
            for t in range(8):
                T = (B, C)[t % 2]
                dve.wait_ge(pj_full[t % 2], tile("write", 0, t) + 1)
                if t >= 2:
                    dve.wait_ge(out_stored[t % 2], 16 * (t // 2))
                V.tensor_copy(T[:, :], PJ[:, t % 2, :]).then_inc(pj_free[t % 2], 1)


def kernel(**inputs):
    import numpy as np
    import concourse.bacc as bacc
    from concourse.bass_utils import run_bass_kernel_spmd

    arrays = {k: np.asarray(v) for k, v in inputs.items()}
    f32 = np.float32

    def columns(a):
        a = np.asarray(a)
        n = a.shape[-1] // P
        return a.reshape(-1, n, P).transpose(2, 0, 1).reshape(P, -1)

    def gate_weight(w):
        full = np.zeros((R_PAIRS, RT * P, RT * P), f32)
        n = w.shape[-1]
        for b in range(2):
            full[:, b * n:(b + 1) * n, b * n:(b + 1) * n] = w[b::2]
        out = np.zeros((R_PAIRS, P, 8, P), f32)
        for q, (k, m) in enumerate(GATE_TILES):
            out[:, :, q, :] = full[:, k * P:(k + 1) * P, m * P:(m + 1) * P]
        return out.reshape(R_PAIRS, P, 8 * P)

    idx = np.arange(CHUNK, dtype=f32)
    log_gamma = np.log(f32(1.0) - f32(2.0) ** (f32(-5.0) - np.arange(RET_HEADS, dtype=f32))).astype(f32)
    diff = idx[None, :] - idx[:, None]
    decay = np.where(diff[None] >= 0, np.exp(log_gamma[:, None, None] * np.maximum(diff, 0)[None]), 0)
    zeta = np.exp(log_gamma[:, None] * (CHUNK - 1 - idx)[None])
    xi = np.exp(log_gamma[:, None] * (idx + 1)[None])
    half = P // 2
    inv_freq = (f32(1.0) / (f32(10000.0) ** (np.arange(half, dtype=f32) / f32(half)))).astype(f32)
    ang = inv_freq[:, None] * np.arange(S, dtype=f32)[None]
    cos, sin = np.cos(ang), np.sin(ang)
    const = {
        "ident": np.eye(P),
        "ones": np.ones((P, P)),
        "group64": np.kron(np.eye(2), np.ones((64, 64))),
        "cos": np.concatenate([cos, cos]),
        "sin": np.concatenate([-sin, sin]),
        "decay": decay.transpose(1, 0, 2),
        "xi": np.broadcast_to(xi[None], (P, RET_HEADS, P)),
        "negmask": np.where(diff >= 0, 0.0, -1e30),
    }
    vectors = {
        "n1g": arrays["norm1_g"], "n2g": arrays["norm2_g"], "n3g": arrays["final_norm_g"],
        "n4g": arrays["ln_g_2"][0], "n5g": arrays["ln_g_2"][1], "n6g": arrays["final_g_2"],
        "cnw": arrays["conv_w"], "cng": arrays["conv_norm_g"], "rng": arrays["ret_norm_g"],
        "mcw": arrays["m_conv_w_2"][0], "mcb": arrays["m_conv_b_2"][0], "mnw": arrays["m_norm_w_2"][0],
        "msk": arrays["m_skip_2"][0], "rcw": arrays["r_conv_w_2"][0], "rcb": arrays["r_conv_b_2"][0],
        "rba": arrays["r_b_a_2"][0], "rbx": arrays["r_b_x_2"][0], "lam": arrays["r_lam_2"][0],
    }
    packed = {k: columns(a) for k, a in vectors.items()}
    packed["zeta"] = zeta.T
    packed["chunk_decay"] = np.broadcast_to(np.exp(log_gamma * CHUNK)[None], (P, RET_HEADS))
    feeds = {k: np.ascontiguousarray(a, dtype=f32) for k, a in const.items()}
    feeds |= {
        "x": arrays["x"][0], "w_in": arrays["w_in"], "w_out": arrays["w_out"], "w_up": arrays["w_up"],
        "w_down": arrays["w_down"], "m_w_in": arrays["m_w_in_2"][0],
        "m_w_q": arrays["m_w_q_2"][0].reshape(M_INNER, DK), "m_w_k": arrays["m_w_k_2"][0].reshape(M_INNER, DK),
        "m_w_v": arrays["m_w_v_2"][0].reshape(M_INNER, DV), "m_w_out": arrays["m_w_out_2"][0],
        "r_w_in": arrays["r_w_in_2"][0], "r_w_out": arrays["r_w_out_2"][0],
        "gate_a": gate_weight(arrays["r_w_a_2"][0]), "gate_x": gate_weight(arrays["r_w_x_2"][0]),
        "mbif": np.stack([arrays["m_b_i_2"][0], arrays["m_b_f_2"][0]], 1),
        "vec": np.concatenate([packed[k] for k, _ in VEC], 1),
    }
    feeds = {k: np.ascontiguousarray(a) for k, a in feeds.items()}
    nc = bacc.Bacc("TRN2", target_bir_lowering=False, num_devices=1)
    d = {k: nc.dram_tensor(k, a.shape, mybir.dt.from_np(a.dtype), kind="ExternalInput").ap()
         for k, a in feeds.items()}
    d["out"] = nc.dram_tensor("out", (S, D), F32, kind="ExternalOutput").ap()
    build(nc, d)
    got = run_bass_kernel_spmd(nc, [feeds], core_ids=[0])
    return np.asarray(got.results[0]["out"]).reshape(1, S, D)
```

```python
from contextlib import ExitStack

import concourse.bass as bass
from concourse import mybir

F32 = mybir.dt.float32
F32R = mybir.dt.float32r
ACT = mybir.ActivationFunctionType
ALU = mybir.AluOpType
ds = bass.ds

P = 128
D = 1024
S = 1024
KT = D // P
HALF = 512
EPS = 1e-6

RET_HEADS = 4
CONV_TILES = 4
CHUNK = 128
CONSTS = 9 * 16
NCH = S // CHUNK
RET_COL = 1536

FF_BLOCKS = 8

M_HEADS = 4
M_INNER = 2048
MT = M_INNER // P
DV = 512
DK = 256
VT = DV // P
KK = DK // P
ROWS = M_HEADS * NCH

R_WIDTH = 1536
R_TILES = R_WIDTH // P
R_PAIRS = 4
RT = 3
GATE_TILES = [(0, 0), (1, 0), (0, 1), (1, 1), (2, 1), (1, 2), (2, 2)]

PHASES = [
    ("read", 1, 0, 8, 0),
    ("norm1", 1, 0, 0, 2),
    ("ret", RET_HEADS, 4, 4, 6),
    ("ret_down", 1, 4, 8, 0),
    ("conv", 2, 6, 6, 2),
    ("conv_down", 1, 4, 8, 0),
    ("norm2", 1, 0, 0, 2),
    ("ffn", FF_BLOCKS, 8, 12, 0),
    ("norm3", 1, 0, 0, 2),
    ("norm4", 1, 0, 0, 2),
    ("gate", 1, 2, 2, 2),
    ("inner", MT // 2, 6, 6, 0),
    ("mlstm", M_HEADS, 8, 16, 4),
    ("norm5", 1, 0, 0, 2),
    ("lru", R_PAIRS, 12, 20, 0),
    ("norm6", 1, 0, 0, 2),
    ("write", 1, 0, 8, 0),
]


def first_of(column):
    at, out = 0, {}
    for row in PHASES:
        out[row[0]] = at
        at += row[1] * row[column]
    return out, at


UNIT0, UNITS = first_of(2)
PROJ0, _ = first_of(3)
AUX0, _ = first_of(4)
UNITS_OF = {row[0]: row[2] for row in PHASES}
PROJ_OF = {row[0]: row[3] for row in PHASES}
AUX_OF = {row[0]: row[4] for row in PHASES}


def slot_uses(first, per, i, k):
    return first // 2 + (per // 2) * i + k // 2


VEC = [("n1g", KT), ("n2g", KT), ("n3g", KT), ("n4g", KT), ("n5g", KT), ("n6g", KT),
       ("cnw", 3 * CONV_TILES), ("cng", CONV_TILES), ("rng", RET_HEADS), ("zeta", RET_HEADS),
       ("chunk_decay", RET_HEADS), ("mcw", 4 * MT), ("mcb", MT), ("mnw", MT), ("msk", MT),
       ("rcw", 4 * R_TILES), ("rcb", R_TILES), ("rba", R_TILES), ("rbx", R_TILES),
       ("lam", R_TILES)]
VEC_AT = {}
VEC_N = 0
for _name, _n in VEC:
    VEC_AT[_name] = VEC_N
    VEC_N += _n


START1 = {
    "pool": ["w_split0", "w_split1", "h_y", "h_done"],
    "pe": ["w_used0", "h_qc", "h_oT", "h_hnT"],
    "act": ["g_rounded", "h_t1", "h_yhi", "m_xc"],
    "dve": ["g_ready", "c_y", "c_n", "m_conv", "m_zs", "m_zn", "h_hh", "h_y1", "h_den",
            "h_num", "l_xc", "l_h", "l_ix", "l_xclo"],
}
START16 = {"act": ["st_xm", "st_xc", "st_zn", "st_zs", "st_o"]}


def from1(n):
    return n + 1


def from16(n):
    return n + 16


def build(nc, d):
    ctx = ExitStack()
    with ctx:
        def dram(name, shape):
            return nc.dram_tensor(name, shape, F32, kind="Internal").ap()

        by_name = {}

        def sem(name):
            by_name[name] = ctx.enter_context(nc.semaphore(name))
            return by_name[name]

        def raise_starts(engine, who):
            for name in START1.get(who, []):
                engine.sem_inc(by_name[name], 1)
            for name in START16.get(who, []):
                engine.sem_inc(by_name[name], 16)

        x_kept = dram("x_kept", (P, KT, S))
        xm_kept = dram("xm_kept", (MT, P, S))
        xc_kept = dram("xc_kept", (MT, P, S))
        o_kept = dram("o_kept", (MT, P, S))
        zn_kept = dram("zn_kept", (MT, P, S))
        zs_kept = dram("zs_kept", (MT, P, S))
        gate_kept = dram("gate_kept", (2, M_HEADS, S))
        last_kept = dram("last_kept", (3, ROWS))

        base = nc.sbuf_base
        end = nc.sbuf_usable_end
        top = [(base + 31) // 32 * 32]

        def place(name, shape, dt=F32, at=None):
            size = 4
            for n in shape[1:]:
                size *= n
            size = (size + 31) // 32 * 32
            where = top[0] if at is None else at
            t = nc.alloc_sbuf_tensor_at(name, list(shape), dt, offset=where)
            assert where + size <= end, (name, where + size - end)
            if at is None:
                top[0] += size
            return t, where + size

        def keep(name, shape, dt=F32):
            return place(name, shape, dt)[0]

        X_AT = top[0]
        X = keep("x_res", [P, KT, S])
        X_END = top[0]
        raw = keep("w_raw", [P, 2, 1024])
        wh = keep("w_hi", [P, 2, 1024], F32R)
        wl = keep("w_lo", [P, 2, 1024], F32R)
        ident = keep("ident", [P, P])
        identr = keep("identr", [P, P], F32R)
        ones = keep("ones", [P, P])
        eps = keep("eps", [P, 1])
        zero = keep("zero", [P, 1])
        onesr = keep("onesr", [P, 4], F32R)
        group64 = keep("group64", [P, P])
        mbif = keep("mbif", [M_HEADS, 2])
        vec = keep("vec", [P, VEC_N])
        lra = keep("lru_rate", [P, R_TILES])
        ltmp = keep("lru_tmp", [P, 4, R_TILES])

        def v(name, k=0, n=1):
            return vec[:, ds(VEC_AT[name] + k, n)]

        Ap = keep("tile_a", [P, 8 + S])
        A = Ap[:, 8:8 + S]
        B = keep("tile_b", [P, S])
        C = keep("tile_c", [P, S])
        Dt = keep("tile_d", [P, S])
        U_AT = top[0]
        Uh = keep("u_hi", [P, KT, S], F32R)
        Ul = keep("u_lo", [P, KT, S], F32R)
        V_AT = top[0]
        Gh = keep("g_hi", [P, VT, S], F32R)
        Gl = keep("g_lo", [P, VT, S], F32R)
        G_END = top[0]

        def area(at, limit):
            cur = [at]

            def put(name, shape, dt=F32):
                t, cur[0] = place(name, shape, dt, at=cur[0])
                assert cur[0] <= limit, (name, cur[0] - limit)
                return t
            return put

        put = area(X_AT, X_END)
        Qh, Ql = put("q_hi", [P, S], F32R), put("q_lo", [P, S], F32R)
        Kh, Kl = put("k_hi", [P, S], F32R), put("k_lo", [P, S], F32R)
        QXh, QXl = put("qx_hi", [P, S], F32R), put("qx_lo", [P, S], F32R)
        Kth, Ktl = put("kt_hi", [P, S], F32R), put("kt_lo", [P, S], F32R)
        put = area(G_END, end)
        Vth, Vtl = put("vt_hi", [P, S], F32R), put("vt_lo", [P, S], F32R)
        SMh, SMl = put("sm_hi", [P, S], F32R), put("sm_lo", [P, S], F32R)
        cos = put("cos", [P, S])
        sin = put("sin", [P, S])
        decay = put("decay", [P, RET_HEADS, P])
        xi = put("xi", [P, RET_HEADS, P])

        put = area(G_END, end)
        Cp = put("conv_in", [P, 8 + S])

        put = area(V_AT, end)
        E = put("inner_e", [P, S])
        Fx = put("inner_xc", [P, S])
        H = put("inner_z", [P, S])
        Q = put("inner_q", [P, S])
        O = put("inner_o", [P, S])
        GR = put("gate_rows", [M_HEADS, 2, S])

        put = area(U_AT, end)
        GXh = put("m_x_hi", [P, VT, S], F32R)
        GXl = put("m_x_lo", [P, VT, S], F32R)
        Vh = put("m_v_hi", [P, NCH, DV], F32R)
        Vl = put("m_v_lo", [P, NCH, DV], F32R)
        Mqh = put("m_q_hi", [P, KK, S], F32R)
        Mql = put("m_q_lo", [P, KK, S], F32R)
        Mkh = put("m_k_hi", [P, KK, S], F32R)
        Mkl = put("m_k_lo", [P, KK, S], F32R)
        XMh = place("m_xm_hi", [P, VT, S], F32R, at=U_AT + 64 * S)[0]
        XMl = place("m_xm_lo", [P, VT, S], F32R, at=U_AT + 80 * S)[0]
        C_AT = U_AT + 96 * S
        Cf = put("m_c", [P, KK, 514])
        Ch = put("m_c_hi", [P, KK, 514], F32R)
        Cl = put("m_c_lo", [P, KK, 514], F32R)
        negmask = put("negmask", [P, P])
        cols = put("cols", [P, 5, ROWS])
        hc = put("head_cols", [P, 6, NCH])
        dlb = put("dlb", [P, ROWS])
        num = put("m_num", [P, DV])
        dcol = put("m_dcol", [P, 8])
        bst = put("m_bst", [P, 8])
        mst = put("m_mst", [P, 4])
        c_at = [U_AT - 2 * 4 * S, U_AT - 4 * S]
        Msh = place("m_s_hi", [P, S], F32R, at=c_at[0])[0]
        Msl = place("m_s_lo", [P, S], F32R, at=c_at[1])[0]
        ab_at = U_AT - 4 * 4 * S
        t1 = place("m_t1", [P, DV], F32, at=ab_at)[0]
        hh = place("m_hh", [P, DV], F32, at=ab_at + 2048)[0]
        yy = place("m_y", [P, DV], F32, at=ab_at + 4096)[0]
        och = put("m_och", [P, VT, CHUNK])
        znc = put("m_znc", [P, VT, CHUNK])
        zsc = put("m_zsc", [P, VT, CHUNK])
        Sw = place("m_scores", [P, S], F32, at=U_AT)[0]
        put = area(C_AT, C_AT + 3 * 4 * KK * 514)
        gi = put("gi", [ROWS, P])
        gf = put("gf", [ROWS, P])
        ga = put("ga", [ROWS, P])
        gb = put("gb", [ROWS, P])
        gc_ = put("gc", [ROWS, P])
        gF = put("gF", [ROWS, P])
        gA = put("gA", [ROWS, P])
        gM = put("gM", [ROWS, P])
        gone = put("gone", [ROWS, P])
        gzero = put("gzero", [ROWS, P])
        g5 = put("g5", [ROWS, 5, P])
        gcol = put("gcol", [ROWS, 8])
        gdiag = put("gdiag", [ROWS, ROWS])
        sc4 = put("sc4", [M_HEADS, 3, NCH + 1])

        put = area(V_AT, end)
        G3h = put("g3_hi", [P, RT, S], F32R)
        G3l = put("g3_lo", [P, RT, S], F32R)
        XCh = put("xc_hi", [P, RT, S], F32R)
        XCl = put("xc_lo", [P, RT, S], F32R)
        R3 = put("lru_r", [P, RT, S])


        PJ = ctx.enter_context(nc.psum_tensor("proj", [P, 2, 1024], F32))
        AX = ctx.enter_context(nc.psum_tensor("aux", [P, 2, 1024], F32))

        consts = sem("consts")
        consts_r = sem("consts_r")
        w_loaded = [sem("w_loaded0"), sem("w_loaded1")]
        w_rounded = sem("w_rounded")
        w_split = [sem("w_split0"), sem("w_split1")]
        w_used = [sem("w_used0"), sem("w_used1")]
        pj_full = [sem("pj_full0"), sem("pj_full1")]
        pj_free = [sem("pj_free0"), sem("pj_free1")]
        ax_full = [sem("ax_full0"), sem("ax_full1")]
        ax_free = [sem("ax_free0"), sem("ax_free1")]
        xt_loaded = [sem("xt_loaded0"), sem("xt_loaded1")]
        x_spilled = sem("x_spilled")
        x_back = sem("x_back")
        out_stored = [sem("out_stored0"), sem("out_stored1")]
        sq_ready = sem("sq_ready")
        sq_used = sem("sq_used")
        sq_added = sem("sq_added")
        rstd_ready = sem("rstd_ready")
        y_ready = sem("y_ready")
        u_rounded = sem("u_rounded")
        u_ready = [sem("u_ready0"), sem("u_ready1")]
        g_rounded = sem("g_rounded")
        g_ready = sem("g_ready")
        x_scaled = sem("x_scaled")

        def use(phase, i, k):
            return slot_uses(UNIT0[phase], UNITS_OF[phase], i, k)

        def tile(phase, i, k):
            return slot_uses(PROJ0[phase], PROJ_OF[phase], i, k)

        def aux(phase, i, k):
            return slot_uses(AUX0[phase], AUX_OF[phase], i, k)

        NORMS = ["norm1", "norm2", "norm3", "norm4", "norm5", "norm6"]
        GAINS = dict(norm1="n1g", norm2="n2g", norm3="n3g", norm4="n4g", norm5="n5g", norm6="n6g")
        SOURCE = dict(norm1=("read", 0, 0), norm2=("conv_down", 0, 0), norm3=("ffn", FF_BLOCKS - 1, 4),
                      norm5=("mlstm", M_HEADS - 1, 8), norm6=("lru", R_PAIRS - 1, 12))
        UREADY = dict(norm1=0, norm2=8, norm4=16, norm5=24)
        PE_SUMS = {p: (1, 3, 5, 7) if p in ("norm1", "norm4") else (7,) for p in NORMS}

        def sums_before(phase, t, by_pe):
            n = 0
            for p in NORMS:
                for u in range(1, 7):
                    if p == phase and u >= t:
                        return n
                    n += (u in PE_SUMS[p]) == by_pe
                if p == phase:
                    return n
        GREADY = dict(ret=1, conv=5, ffn=9, lru=41)

        block = ctx.enter_context(nc.Block())

        w_in = d["w_in"].rearrange("(t p) n -> p t n", p=P)
        w_out = d["w_out"].rearrange("(t p) n -> p t n", p=P)
        w_up = d["w_up"].rearrange("(t p) n -> p t n", p=P)
        w_down = d["w_down"].rearrange("(t p) n -> p t n", p=P)
        m_in = d["m_w_in"].rearrange("(t p) n -> p t n", p=P)
        m_q = d["m_w_q"].rearrange("(t p) n -> p t n", p=P)
        m_k = d["m_w_k"].rearrange("(t p) n -> p t n", p=P)
        m_v = d["m_w_v"].rearrange("(t p) n -> p t n", p=P)
        m_out = d["m_w_out"].rearrange("(t p) n -> p t n", p=P)
        r_in = d["r_w_in"].rearrange("(t p) n -> p t n", p=P)
        r_out = d["r_w_out"].rearrange("(t p) n -> p t n", p=P)

        def sems(names):
            return {n: sem(n) for n in names.split()}

        r = sems("r_swapped r_sin r_rotated r_qhi r_qlo r_qx r_qxhi r_qxlo r_khi r_klo "
                 "r_kthi r_vthi r_smhi r_smlo r_state r_shi r_slo r_rstd r_y1 r_y")
        c = sems("c_pad c_0 c_1 c_2 c_y c_sq c_rstd c_n")
        f_sq = sem("f_sq")
        m = sems("m_pad m_c0 m_c1 m_c2 m_conv m_xc m_zn m_zs st_xm st_xc st_zn st_zs st_o "
                 "g_stored g_back ga_exp ga_abs ga_step ga_last ga_lastback ga_m ga_mback ga_rows ga_exps "
                 "ga_dl lam_abs lam_exp")
        h = sems("h_x0 h_x1 h_xround h_xsplit h_vhi h_qhi h_khi h_hc h_diag h_w "
                 "h_smhi h_smlo h_c h_chi h_clo0 h_clo1 h_den h_och h_znc h_zsc "
                 "h_s0 h_sw h_kt0hi h_kt1hi h_kt0lo h_kt1lo h_qc h_sv h_cu h_t1 h_num h_d0 h_d1 h_d2 h_oT h_hh h_st h_st2 h_std h_rs h_hn h_hnT "
                 "h_y1 h_y h_yhi h_done")
        l = sems("l_pad l_c0 l_c1 l_c2 l_xc l_xchi l_xclo l_rate l_th l_aa l_e l_sqrt l_x l_ix l_bt "
                 "l_h l_y")

        @block.sync
        def _(sp):
            for t in range(8):
                if t >= 2:
                    sp.wait_ge(pj_full[t % 2], t // 2)
                sp.dma_start((B, C)[t % 2][:, :], d["x"][t * P:(t + 1) * P, :]) \
                    .then_inc(xt_loaded[t % 2], 16)

            def load(phase, i, k, src, width):
                n = use(phase, i, k)
                sp.wait_ge(w_split[k % 2], from1(n))
                dst = raw[:, k % 2, :].rearrange("p (t n) -> p t n", n=width)[:, 0:src.shape[1], 0:src.shape[2]]
                sp.dma_start(dst, src).then_inc(w_loaded[k % 2], 16)

            def load_down(phase, i, k0, w, row, tiles):
                for k in range(4):
                    load(phase, i, k0 + k, w[:, ds(row, tiles), k * 256:(k + 1) * 256], 256)

            with sp.Fori(0, RET_HEADS) as i:
                for k in range(4):
                    load("ret", i, k, w_in[:, :, ds(i * P + (RET_COL + k * 512), P)], P)
            sp.wait_ge(x_spilled, 16)
            sp.wait_ge(g_ready, GREADY["ret"] + RET_HEADS)
            sp.dma_start(X[:, :, :], x_kept).then_inc(x_back, 16)
            load_down("ret_down", 0, 0, w_out, 4, 4)
            with sp.Fori(0, 2) as i:
                for cc in range(2):
                    for k in range(3):
                        load("conv", i, cc * 3 + k, w_in[:, :, ds(i * 256 + (k * 512 + cc * P), P)], P)
            load_down("conv_down", 0, 0, w_out, 0, 4)
            with sp.Fori(0, FF_BLOCKS) as i:
                for k in range(4):
                    load("ffn", i, k, w_up[:, :, ds(i * 512 + k * P, P)], P)
                load_down("ffn", i, 4, w_down, i * 4, 4)
            for k in range(2):
                load("gate", 0, k, m_in[:, :, 3 * M_INNER + 4 * k:3 * M_INNER + 4 * k + 4], P)
            with sp.Fori(0, MT // 2) as i:
                for jj in range(2):
                    for k in range(3):
                        load("inner", i, jj * 3 + k, m_in[:, :, ds(i * 256 + (k * M_INNER + jj * P), P)], P)

            def stage_x(i, kept, u0):
                for t in range(VT):
                    u = u0 + t
                    if u >= 2:
                        sp.wait_ge(h["h_xsplit"], 8 * i + (u - 1))
                    sp.dma_start((A, B)[t % 2][:, :], kept[ds(i * VT + t, 1), :, :].rearrange("a p s -> (a p) s")) \
                        .then_inc(h["h_x%d" % (t % 2)], 16)

            def stage_chunk(i, kept, dst, got, gone, n):
                sp.wait_ge(h[gone], from1(NCH * i + n))
                sp.dma_start(dst[:, :, :], kept[ds(i * VT, VT), :, n * CHUNK:(n + 1) * CHUNK]
                             .rearrange("t p s -> p t s")).then_inc(h[got], 16)

            def head(i, last):
                for k in range(2):
                    load("mlstm", i, k, m_v[:, ds(i * VT + 2 * k, 2), :], DV)
                stage_x(i, xc_kept, VT)
                load("mlstm", i, 2, m_q[:, ds(i * VT, VT), :], DK)
                load("mlstm", i, 3, m_k[:, ds(i * VT, VT), :], DK)
                for k in range(2):
                    load("mlstm", i, 4 + k, m_out[:, ds(i * VT, VT), k * 256:(k + 1) * 256], 256)
                for n in range(NCH + 1):
                    if n < NCH:
                        stage_chunk(i, o_kept, och, "h_och", "h_oT", n)
                    if n >= 1:
                        stage_chunk(i, zn_kept, znc, "h_znc", "h_y1", n - 1)
                        stage_chunk(i, zs_kept, zsc, "h_zsc", "h_y", n - 1)
                for k in range(2, 4):
                    load("mlstm", i, 4 + k, m_out[:, ds(i * VT, VT), k * 256:(k + 1) * 256], 256)
                if not last:
                    sp.wait_ge(h["h_done"], from1(NCH * i + NCH))
                    stage_x(i + 1, xm_kept, 0)

            for name in ("st_xm", "st_xc", "st_zn", "st_zs", "st_o"):
                sp.wait_ge(m[name], from16(16 * MT))
            stage_x(0, xm_kept, 0)
            with sp.Fori(0, M_HEADS - 1) as i:
                head(i, False)
            head(M_HEADS - 1, True)
            with sp.Fori(0, R_PAIRS) as i:
                for k in range(3):
                    load("lru", i, k, r_in[:, :, ds(i * 384 + k * P, P)], P)
                for k, w in ((3, d["gate_a"]), (4, d["gate_x"])):
                    load("lru", i, k, w[ds(i, 1), :, :].rearrange("a p (t n) -> (a p) t n", n=P), P)
                for k in range(3):
                    load("lru", i, 5 + k, r_in[:, :, ds(i * 384 + (R_WIDTH + k * P), P)], P)
                load_down("lru", i, 8, r_out, i * RT, RT)
            for t in range(8):
                sp.wait_ge(pj_free[t % 2], tile("write", 0, t) + 1)
                sp.dma_start(d["out"][t * P:(t + 1) * P, :], (B, C)[t % 2][:, :]).then_inc(out_stored[t % 2], 16)
            for s in out_stored:
                sp.wait_ge(s, 64)

        @block.gpsimd
        def _(pool):
            raise_starts(pool, "pool")
            pool.wait_ge(consts_r, 4)

            def split_unit(s, n):
                pool.wait_ge(w_loaded[s], 16 * n + 16)
                pool.wait_ge(w_used[s], n + 1)
                nc.gpsimd.tensor_tensor(wh[:, s, :], raw[:, s, :], zero[:, 0:1].broadcast_to([P, 1024]),
                                        ALU.add).then_inc(w_rounded, 1)
                pool.wait_ge(w_rounded, 2 * n + (s + 1))
                nc.gpsimd.tensor_tensor(wl[:, s, :], raw[:, s, :], wh[:, s, :].bitcast(F32),
                                        ALU.subtract).then_inc(w_split[s], 1)

            def norm(phase, unit=None):
                first = 8 * NORMS.index(phase)
                for t in range(1, 7):
                    if t not in PE_SUMS[phase]:
                        pool.wait_ge(sq_ready, first + t + 1)
                        nc.gpsimd.tensor_tensor(C[:, :], C[:, :], (A, B)[t % 2][:, :], ALU.add) \
                            .then_inc(sq_added, 1)
                        pool.wait_ge(sq_added, sums_before(phase, t + 1, False))
                if unit is not None:
                    split_unit(0, unit // 2)
                if phase in UREADY:
                    for t in range(1, KT, 2):
                        pool.wait_ge(u_rounded, UREADY[phase] + t + 1)
                        nc.gpsimd.tensor_tensor(Ul[:, t, :], (A, B, C)[t % 3][:, :], Uh[:, t, :].bitcast(F32),
                                                ALU.subtract).then_inc(u_ready[1], 1)

            def split_units(first, after):
                with pool.Fori(0, (after - first) // 2 - 1) as i:
                    split_unit(1, i + first // 2)
                    split_unit(0, i + (first // 2 + 1))
                split_unit(1, after // 2 - 1)

            norm("norm1", 0)
            split_units(0, UNIT0["norm2"])
            norm("norm2", UNIT0["ffn"])
            split_units(UNIT0["ffn"], UNIT0["norm3"])
            norm("norm3")
            norm("norm4", UNIT0["gate"])
            split_units(UNIT0["gate"], UNIT0["mlstm"])
            with pool.Fori(0, M_HEADS) as i:
                for k in range(6):
                    split_unit(k % 2, use("mlstm", i, k))
                for hf in range(2):
                    tok = slice(hf * HALF, (hf + 1) * HALF)
                    pool.wait_ge(h["h_kt0hi"], 2 * i + (hf + 1))
                    nc.gpsimd.tensor_tensor(Mkl[:, 0, tok], A[:, tok], Mkh[:, 0, tok].bitcast(F32),
                                            ALU.subtract).then_inc(h["h_kt0lo"], 1)
                for step in range(NCH + 2):
                    if step < NCH:
                        pool.wait_ge(h["h_chi"], NCH * i + (step + 1))
                        nc.gpsimd.tensor_tensor(Cl[:, 1, :], Cf[:, 1, :], Ch[:, 1, :].bitcast(F32),
                                                ALU.subtract).then_inc(h["h_clo1"], 1)
                    if step < 2:
                        continue
                    n = step - 2
                    g = NCH * i + n
                    pool.wait_ge(h["h_y1"], from1(g + 1))
                    pool.wait_ge(h["h_zsc"], 16 * g + 16)
                    nc.gpsimd.tensor_tensor(yy[:, :], yy[:, :], zsc[:, :, :].rearrange("p t s -> p (t s)"),
                                            ALU.add).then_inc(h["h_y"], 1)
                    pool.wait_ge(h["h_yhi"], from1(g + 1))
                    nc.gpsimd.tensor_tensor(GXl[:, :, n * P:(n + 1) * P],
                                            yy[:, :].rearrange("p (t s) -> p t s", t=VT),
                                            GXh[:, :, n * P:(n + 1) * P].bitcast(F32),
                                            ALU.subtract).then_inc(h["h_done"], 1)
                for k in range(6, 8):
                    split_unit(k % 2, use("mlstm", i, k))
            norm("norm5", UNIT0["lru"])
            split_units(UNIT0["lru"], UNITS)
            norm("norm6")

        @block.tensor
        def _(pe):
            raise_starts(pe, "pe")
            mm = nc.tensor.matmul

            def mm3(out, lh, ll, rh, rl, start, stop, closes=None):
                first = mm(out, lh, rh, start=start, stop=False)
                if closes is not None:
                    first.then_inc(w_used[closes], 1)
                mm(out, lh, rl, start=False, stop=False)
                return mm(out, ll, rh, start=False, stop=stop)

            def start_unit(phase, i, k):
                pe.wait_ge(w_split[k % 2], from1(use(phase, i, k) + 1))

            def start_tile(phase, i, k):
                pe.wait_ge(pj_free[k % 2], tile(phase, i, k))

            def start_aux(phase, i, k):
                pe.wait_ge(ax_free[k % 2], aux(phase, i, k))

            def project(phase, i, k, p, xh, xl, kts, width, col, waits=None, closes=True):
                s = k % 2
                start_tile(phase, i, p)
                for kt in range(kts):
                    if waits is not None:
                        pe.wait_ge(*waits(kt))
                    at = kt * width + col
                    for j in range(2):
                        tok = slice(j * HALF, (j + 1) * HALF)
                        ins = mm3(PJ[:, p % 2, tok], wh[:, s, at:at + P], wl[:, s, at:at + P],
                                  xh[:, kt, tok], xl[:, kt, tok], kt == 0, kt == kts - 1,
                                  1 - s if closes and kt == 0 and j == 0 else None)
                ins.then_inc(pj_full[p % 2], 1)

            def up(phase, i, k, p, waits=None):
                start_unit(phase, i, k)
                project(phase, i, k, p, Uh, Ul, KT, P, 0, waits)

            def down(phase, i, k0, p0, gh, gl, kts, ready=None, closes_first=True):
                for k in range(4):
                    start_unit(phase, i, k0 + k)
                    for j in range(2):
                        first = k == 0 and j == 0 and ready is not None
                        project(phase, i, k0 + k, p0 + 2 * k + j, gh, gl, kts, 256, j * P,
                                (lambda kt: (g_ready, ready + kt + 1)) if first else None,
                                j == 0 and (k > 0 or closes_first))

            def norm_sums(phase):
                first = 8 * NORMS.index(phase)
                for j in range(2):
                    start_aux(phase, 0, j)
                own = PE_SUMS[phase]
                for t in own[:-1] + ("C",) + own[-1:]:
                    if t == "C":
                        pe.wait_ge(sq_added, sums_before(phase, 8, False))
                    else:
                        pe.wait_ge(sq_ready, first + t + 1)
                    for j in range(2):
                        ins = mm(AX[:, j, 0:HALF], ones[:, :], (C if t == "C" else B)[:, j * HALF:(j + 1) * HALF],
                                 start=t == (own[:-1] + ("C",))[0], stop=t == 7)
                        if t == 7:
                            ins.then_inc(ax_full[j], 1)
                        elif j == 1 and t != "C":
                            ins.then_inc(sq_used, 1)

            u_wait = lambda phase: (lambda kt: (u_ready[kt % 2], UREADY[phase] // 2 + kt // 2 + 1))

            pe.wait_ge(consts, CONSTS)
            pe.wait_ge(consts_r, 4)
            for t in range(8):
                pe.wait_ge(xt_loaded[t % 2], 16 * (t // 2 + 1))
                start_tile("read", 0, t)
                for kt in range(KT):
                    ins = nc.tensor.transpose(PJ[:, t % 2, kt * P:(kt + 1) * P],
                                              (B, C)[t % 2][:, kt * P:(kt + 1) * P], ident[:, :])
                ins.then_inc(pj_full[t % 2], 1)
            norm_sums("norm1")

            with pe.Fori(0, RET_HEADS) as i:
                up("ret", i, 0, 0, u_wait("norm1"))
                up("ret", i, 1, 1)
                up("ret", i, 2, 2)
                start_aux("ret", i, 0)
                pe.wait_ge(r["r_rotated"], 2 * i + 2)
                for n in range(NCH):
                    at = slice(n * P, (n + 1) * P)
                    ins = nc.tensor.transpose(AX[:, 0, at], B[:, at], ident[:, :])
                ins.then_inc(ax_full[0], 1)
                up("ret", i, 3, 3)
                start_aux("ret", i, 1)
                pe.wait_ge(pj_free[0], tile("ret", i, 2) + 1)
                for n in range(NCH):
                    at = slice(n * P, (n + 1) * P)
                    ins = nc.tensor.transpose(AX[:, 1, at], C[:, at], ident[:, :])
                ins.then_inc(ax_full[1], 1)
                start_aux("ret", i, 2)
                pe.wait_ge(r["r_qlo"], i + 1)
                pe.wait_ge(r["r_klo"], i + 1)
                for n in range(NCH):
                    at = slice(n * P, (n + 1) * P)
                    ins = mm3(AX[:, 0, at], Kh[:, at], Kl[:, at], Qh[:, at], Ql[:, at], True, True)
                ins.then_inc(ax_full[0], 1)
                start_aux("ret", i, 3)
                pe.wait_ge(ax_free[0], aux("ret", i, 0) + 1)
                for n in range(NCH):
                    at = slice(n * P, (n + 1) * P)
                    ins = mm3(AX[:, 1, at], Kth[:, at], Ktl[:, at], Vth[:, at], Vtl[:, at], True, True)
                ins.then_inc(ax_full[1], 1)
                start_aux("ret", i, 4)
                pe.wait_ge(r["r_smlo"], i + 1)
                pe.wait_ge(r["r_slo"], i + 1)
                pe.wait_ge(r["r_qxlo"], i + 1)
                for n in range(NCH):
                    at = slice(n * P, (n + 1) * P)
                    mm3(AX[:, 0, at], Vth[:, at], Vtl[:, at], SMh[:, at], SMl[:, at], True, False)
                    ins = mm3(AX[:, 0, at], Kh[:, at], Kl[:, at], QXh[:, at], QXl[:, at], False, True)
                ins.then_inc(ax_full[0], 1)
                start_aux("ret", i, 5)
                pe.wait_ge(ax_free[0], aux("ret", i, 4) + 1)
                for j in range(2):
                    ins = mm(AX[:, 1, j * HALF:(j + 1) * HALF], ones[:, :], A[:, j * HALF:(j + 1) * HALF],
                             start=True, stop=True)
                ins.then_inc(ax_full[1], 1)
            down("ret_down", 0, 0, 0, Gh, Gl, 4, GREADY["ret"])

            with pe.Fori(0, 2) as i:
                for cc in range(2):
                    for k in range(3):
                        up("conv", i, 3 * cc + k, 3 * cc + k)
                    start_aux("conv", i, cc)
                    pe.wait_ge(c["c_sq"], 2 * i + cc + 1)
                    for j in range(2):
                        ins = mm(AX[:, cc, j * HALF:(j + 1) * HALF], group64[:, :],
                                 B[:, j * HALF:(j + 1) * HALF], start=True, stop=True)
                    ins.then_inc(ax_full[cc], 1)
            down("conv_down", 0, 0, 0, Gh, Gl, 4, GREADY["conv"])
            norm_sums("norm2")

            with pe.Fori(0, FF_BLOCKS) as i:
                for k in range(4):
                    up("ffn", i, k, k, u_wait("norm2") if k == 0 else None)
                down("ffn", i, 4, 4, Gh, Gl, 4, GREADY["ffn"] + 4 * i)
            norm_sums("norm3")
            norm_sums("norm4")

            for k in range(2):
                up("gate", 0, k, k, u_wait("norm4") if k == 0 else None)
            with pe.Fori(0, MT // 2) as i:
                for k in range(6):
                    up("inner", i, k, k)
            start_aux("gate", 0, 0)
            pe.wait_ge(m["ga_rows"], 2)
            pe.wait_ge(m["ga_exps"], 3)
            for q in range(5):
                ins = nc.tensor.transpose(AX[:, 0, q * ROWS:(q + 1) * ROWS], g5[:, q, :], ident[0:ROWS, 0:ROWS])
            ins.then_inc(ax_full[0], 1)
            start_aux("gate", 0, 1)
            pe.wait_ge(m["ga_dl"], 1)
            mm(AX[:, 1, 0:ROWS], ones[0:ROWS, :], gdiag[:, :], start=True, stop=True).then_inc(ax_full[1], 1)

            def head(i):
                start_unit("mlstm", i, 0)
                for p in range(4):
                    start_tile("mlstm", i, p)
                    for j in range(2):
                        at = slice((2 * p + j) * P, (2 * p + j + 1) * P)
                        for kt in range(VT):
                            w = slice((kt % 2) * DV, (kt % 2 + 1) * DV)
                            closes = None
                            if p == 0 and j == 0:
                                pe.wait_ge(h["h_xsplit"], 8 * i + (kt + 1))
                                if kt == 0:
                                    closes = 1
                                if kt == 2:
                                    start_unit("mlstm", i, 1)
                            elif p == 3 and j == 1 and kt == 2:
                                closes = 0
                            ins = mm3(PJ[:, p % 2, j * HALF:(j + 1) * HALF], XMh[:, kt, at], XMl[:, kt, at],
                                      wh[:, kt // 2, w], wl[:, kt // 2, w], kt == 0, kt == VT - 1, closes)
                    ins.then_inc(pj_full[p % 2], 1)
                pe.wait_ge(h["h_xsplit"], 8 * i + 8)
                for k in range(2):
                    start_unit("mlstm", i, 2 + k)
                    for j in range(2):
                        project("mlstm", i, 2 + k, 4 + 2 * k + j, GXh, GXl, VT, DK, j * P, closes=j == 0)
                    if k == 1:
                        break
                    start_aux("mlstm", i, 0)
                    pe.wait_ge(h["h_diag"], i + 1)
                    for j in range(2):
                        tok = slice(j * HALF, (j + 1) * HALF)
                        mm(AX[:, 0, tok], ones[:, :], Dt[:, tok], start=True, stop=False)
                        ins = mm(AX[:, 0, tok], ident[:, :], negmask[:, :].unsqueeze(1).broadcast_to([P, 4, P]),
                                 start=False, stop=True)
                    ins.then_inc(ax_full[0], 1)
                for kk in range(KK):
                    pe.wait_ge(ax_free[1 - kk], aux("mlstm", i, 1 + kk))
                    pe.wait_ge(pj_free[kk], tile("mlstm", i, 6 + kk) + 1)
                    for n in range(NCH):
                        at = slice(n * P, (n + 1) * P)
                        ins = mm(AX[:, 1 - kk, at], Mkh[:, kk, at], identr[:, :], start=True, stop=False)
                        if kk == 0 and n == 0:
                            ins.then_inc(w_used[1], 1)
                        ins = mm(AX[:, 1 - kk, at], Mkl[:, kk, at], identr[:, :], start=False, stop=True)
                    ins.then_inc(ax_full[1 - kk], 1)
                start_aux("mlstm", i, 3)
                for n in range(NCH):
                    at = slice(n * P, (n + 1) * P)
                    for kk in range(KK):
                        ins = mm3(AX[:, 1, at], Mkh[:, kk, at], Mkl[:, kk, at], Mqh[:, kk, at], Mql[:, kk, at],
                                  kk == 0, kk == KK - 1)
                    if n == 3:
                        ins.then_inc(h["h_s0"], 1)
                ins.then_inc(ax_full[1], 1)
                for s in range(2):
                    pe.wait_ge(pj_free[s], tile("mlstm", i, 6 + s) + 1)
                    if s == 0:
                        pe.wait_ge(ax_free[0], aux("mlstm", i, 2) + 1)
                for step in range(NCH + 1):
                    if step < NCH:
                        n = step
                        g = NCH * i + n
                        at = slice(n * P, (n + 1) * P)
                        if n % 4 == 0:
                            for name in ("h_smlo", "h_kt0lo", "h_kt1lo"):
                                pe.wait_ge(h[name], 2 * i + (n // 4 + 1))
                        if n < NCH - 1:
                            pe.wait_ge(h["h_c"], g + 1)
                            for kk in range(KK):
                                mm3(AX[:, 0, kk * DV:(kk + 1) * DV], Mkh[:, kk, at], Mkl[:, kk, at],
                                    Vh[:, n, :], Vl[:, n, :], True, True)
                            if n == 0:
                                pe.wait_ge(ax_free[1], aux("mlstm", i, 3) + 1)
                            for kk in range(KK):
                                add = AX[:, 1, HALF + 2 * kk:HALF + 2 * kk + 2]
                                mm(add, Mkh[:, kk, at], onesr[:, 0:2], start=True, stop=False)
                                ins = mm(add, Mkl[:, kk, at], onesr[:, 0:2], start=False, stop=True)
                            ins.then_inc(h["h_cu"], 1)
                        pe.wait_ge(h["h_och"], 16 * (g + 1))
                        pe.wait_ge(h["h_hh"], from1(g))
                        for t in range(VT):
                            ins = nc.tensor.transpose(PJ[:, 1, t * P:(t + 1) * P], och[:, t, :], ident[:, :])
                        ins.then_inc(h["h_oT"], 1)
                        pe.wait_ge(h["h_num"], from1(g))
                        mm3(PJ[:, 0, DV:2 * DV], Msh[:, at], Msl[:, at], Vh[:, n, :], Vl[:, n, :], True, True) \
                            .then_inc(h["h_sv"], 1)
                        pe.wait_ge(h["h_clo0"], g + 1)
                        pe.wait_ge(h["h_clo1"], g + 1)
                        pe.wait_ge(h["h_t1"], from1(g))
                        pe.wait_ge(h["h_den"], from1(g))
                        for kk in range(KK):
                            mm3(PJ[:, 0, 0:DV], Mqh[:, kk, at], Mql[:, kk, at], Ch[:, kk, 0:DV],
                                Cl[:, kk, 0:DV], kk == 0, kk == KK - 1)
                        for kk in range(KK):
                            mm3(AX[:, 1, 0:2], Mqh[:, kk, at], Mql[:, kk, at], Ch[:, kk, DV:DV + 2],
                                Cl[:, kk, DV:DV + 2], kk == 0, kk == KK - 1)
                        mm(AX[:, 1, 2:4], Msh[:, at], onesr[:, 0:2], start=True, stop=False)
                        mm(AX[:, 1, 2:4], Msl[:, at], onesr[:, 0:2], start=False, stop=True) \
                            .then_inc(h["h_qc"], 1)
                    if step >= 1:
                        g = NCH * i + (step - 1)
                        pe.wait_ge(h["h_hn"], g + 1)
                        pe.wait_ge(h["h_y1"], from1(g))
                        for t in range(VT):
                            ins = nc.tensor.transpose(PJ[:, 1, HALF + t * P:HALF + (t + 1) * P],
                                                      hh[:, t * P:(t + 1) * P], ident[:, :])
                        ins.then_inc(h["h_hnT"], 1)
                pe.wait_ge(h["h_done"], from1(NCH * i + NCH))
                down("mlstm", i, 4, 8, GXh, GXl, VT, closes_first=False)

            with pe.Fori(0, M_HEADS) as i:
                head(i)
            norm_sums("norm5")

            with pe.Fori(0, R_PAIRS) as i:
                for k in range(3):
                    up("lru", i, k, k, u_wait("norm5") if k == 0 else None)
                pe.wait_ge(l["l_xclo"], from1(3 * i + 3))
                for k in range(2):
                    s = (3 + k) % 2
                    start_unit("lru", i, 3 + k)
                    for t in range(RT):
                        qs = [q for q, (_, b) in enumerate(GATE_TILES) if b == t]
                        p = 3 + 3 * k + t
                        start_tile("lru", i, p)
                        for q in qs:
                            for j in range(2):
                                tok = slice(j * HALF, (j + 1) * HALF)
                                ins = mm3(PJ[:, p % 2, tok], wh[:, s, q * P:(q + 1) * P],
                                          wl[:, s, q * P:(q + 1) * P], XCh[:, GATE_TILES[q][0], tok],
                                          XCl[:, GATE_TILES[q][0], tok], q == qs[0], q == qs[-1],
                                          1 - s if t == 0 and q == qs[0] and j == 0 else None)
                        ins.then_inc(pj_full[p % 2], 1)
                for k in range(3):
                    up("lru", i, 5 + k, 9 + k)
                down("lru", i, 8, 12, G3h, G3l, RT, GREADY["lru"] + 3 * i)
            norm_sums("norm6")
            pe.wait_ge(x_scaled, 16)
            for t in range(8):
                start_tile("write", 0, t)
                for kt in range(KT):
                    ins = nc.tensor.transpose(PJ[:, t % 2, kt * P:(kt + 1) * P], X[:, kt, t * P:(t + 1) * P],
                                              ident[:, :])
                ins.then_inc(pj_full[t % 2], 1)

        @block.scalar
        def _(act):
            raise_starts(act, "act")
            def fn(out, in_, func, scale=1.0, bias=0.0):
                return nc.scalar.activation(out, in_, func, bias=bias, scale=scale)

            def norm(phase):
                first = 8 * NORMS.index(phase)
                for t in range(KT):
                    if phase == "norm4":
                        act.wait_ge(x_scaled, t + 1)
                    elif phase == "norm1":
                        for s in range(2):
                            act.wait_ge(pj_free[s], tile("read", 0, 6) + 1)
                    else:
                        ph, i, p = SOURCE[phase]
                        act.wait_ge(pj_free[t % 2], tile(ph, i, p + t) + 1)
                    if t >= 3:
                        by_pe = t - 2 in PE_SUMS[phase]
                        act.wait_ge(sq_used if by_pe else sq_added, sums_before(phase, t - 1, by_pe))
                    fn((A, B)[t % 2][:, :] if t else C[:, :], X[:, t, :], ACT.Square).then_inc(sq_ready, 1)
                for j in range(2):
                    at = slice(j * HALF, (j + 1) * HALF)
                    act.wait_ge(ax_full[j], aux(phase, 0, j) + 1)
                    fn(C[:, at], AX[:, j, 0:HALF], ACT.Ln, 1.0 / D, eps[:, 0:1]).then_inc(ax_free[j], 1)
                    act.wait_ge(ax_free[j], aux(phase, 0, j) + 1)
                    fn(Dt[:, at], C[:, at], ACT.Exp, -0.5).then_inc(rstd_ready, 1)
                if phase in UREADY:
                    for t in range(KT):
                        act.wait_ge(y_ready, UREADY[phase] + t + 1)
                        fn(Uh[:, t, :], (A, B, C)[t % 3][:, :], ACT.Copy).then_inc(u_rounded, 1)

            for dst, name in ((ident, "ident"), (ones, "ones"), (group64, "group64"), (vec, "vec"),
                              (mbif, "mbif"), (cos, "cos"), (sin, "sin"), (decay, "decay"), (xi, "xi")):
                act.dma_start(dst[tuple(slice(None) for _ in dst.shape)], d[name]).then_inc(consts, 16)
            act.wait_ge(consts, CONSTS)
            act.wait_ge(consts_r, 4)
            for s in range(2):
                act.wait_ge(pj_free[s], tile("read", 0, 6) + 1)
            act.dma_start(x_kept, X[:, :, :]).then_inc(x_spilled, 16)
            norm("norm1")

            act.wait_ge(x_spilled, 16)
            for s in u_ready:
                act.wait_ge(s, 4)
            with act.Fori(0, RET_HEADS) as i:
                for q in range(2):
                    act.wait_ge(pj_full[q], tile("ret", i, q) + 1)
                    if q:
                        act.wait_ge(r["r_qxlo"], i + 1)
                    fn(A[64:128, :], PJ[0:64, q, :], ACT.Copy)
                    fn(A[0:64, :], PJ[64:128, q, :], ACT.Copy).then_inc(r["r_swapped"], 1)
                    act.wait_ge(r["r_rotated"], 2 * i + (q + 1))
                    if q == 0:
                        fn(Qh[:, :], B[:, :], ACT.Copy).then_inc(r["r_qhi"], 1)
                        act.wait_ge(r["r_qx"], i + 1)
                        fn(QXh[:, :], A[:, :], ACT.Copy).then_inc(r["r_qxhi"], 1)
                    else:
                        fn(Kh[:, :], B[:, :], ACT.Copy).then_inc(r["r_khi"], 1)
                act.wait_ge(pj_full[0], tile("ret", i, 2) + 1)
                act.wait_ge(g_ready, GREADY["ret"] + i)
                fn(C[:, :], PJ[:, 0, :], ACT.Copy).then_inc(pj_free[0], 1)
                act.wait_ge(ax_full[0], aux("ret", i, 0) + 1)
                fn(Kth[:, :], AX[:, 0, :], ACT.Copy, v("zeta", i)).then_inc(r["r_kthi"], 1)
                act.wait_ge(pj_full[1], tile("ret", i, 3) + 1)
                fn(Dt[:, :], PJ[:, 1, :], ACT.Silu).then_inc(pj_free[1], 1)
                act.wait_ge(ax_full[1], aux("ret", i, 1) + 1)
                fn(Vth[:, :], AX[:, 1, :], ACT.Copy).then_inc(r["r_vthi"], 1)
                act.wait_ge(ax_free[0], aux("ret", i, 2) + 1)
                fn(SMh[:, :], A[:, :], ACT.Copy).then_inc(r["r_smhi"], 1)
                act.wait_ge(ax_free[1], aux("ret", i, 3) + 1)
                fn(Kh[:, :], B[:, :], ACT.Copy).then_inc(r["r_shi"], 1)
                act.wait_ge(ax_full[0], aux("ret", i, 4) + 1)
                fn(C[:, :], AX[:, 0, :], ACT.Copy)
                act.wait_ge(r["r_smlo"], i + 1)
                fn(A[:, :], AX[:, 0, :], ACT.Square).then_inc(ax_free[0], 1)
                act.wait_ge(ax_full[1], aux("ret", i, 5) + 1)
                act.wait_ge(r["r_slo"], i + 1)
                fn(B[:, :], AX[:, 1, :], ACT.Ln, 1.0 / P, eps[:, 0:1]).then_inc(ax_free[1], 1)
                act.wait_ge(ax_free[1], aux("ret", i, 5) + 1)
                fn(B[:, :], B[:, :], ACT.Exp, -0.5).then_inc(r["r_rstd"], 1)
                act.wait_ge(r["r_y"], i + 1)
                fn(Gh[:, ds(i, 1), :].rearrange("p a s -> p (a s)"), C[:, :], ACT.Copy).then_inc(g_rounded, 1)

            with act.Fori(0, 2) as i:
                for cc in range(2):
                    p = 3 * cc
                    act.wait_ge(pj_full[p % 2], tile("conv", i, p) + 1)
                    act.wait_ge(c["c_y"], from1(2 * i + cc))
                    fn(A[:, :], PJ[:, p % 2, :], ACT.Copy).then_inc(pj_free[p % 2], 1)
                    p += 1
                    act.wait_ge(pj_full[p % 2], tile("conv", i, p) + 1)
                    act.wait_ge(c["c_n"], from1(2 * i + cc))
                    fn(B[:, :], PJ[:, p % 2, :], ACT.Copy).then_inc(pj_free[p % 2], 1)
                    act.wait_ge(c["c_y"], from1(2 * i + (cc + 1)))
                    fn(B[:, :], Dt[:, :], ACT.Square).then_inc(c["c_sq"], 1)
                    act.wait_ge(ax_full[cc], aux("conv", i, cc) + 1)
                    fn(B[:, :], AX[:, cc, :], ACT.Ln, 1.0 / 64, eps[:, 0:1]).then_inc(ax_free[cc], 1)
                    act.wait_ge(ax_free[cc], aux("conv", i, cc) + 1)
                    fn(B[:, :], B[:, :], ACT.Exp, -0.5).then_inc(c["c_rstd"], 1)
                    act.wait_ge(pj_full[1], tile("conv", i, 0))
                    act.wait_ge(c["c_n"], from1(2 * i + (cc + 1)))
                    fn(Gh[:, ds(2 * i + cc, 1), :].rearrange("p a s -> p (a s)"), Dt[:, :], ACT.Copy) \
                        .then_inc(g_rounded, 1)
            norm("norm2")

            with act.Fori(0, FF_BLOCKS) as i:
                def split(k):
                    act.wait_ge(f_sq, 4 * i + (k + 1))
                    fn(Gh[:, k, :], (A, B)[k % 2][:, :], ACT.Copy).then_inc(g_rounded, 1)

                for k in range(4):
                    act.wait_ge(pj_full[k % 2], tile("ffn", i, k) + 1)
                    act.wait_ge(g_ready, 4 * i + (GREADY["ffn"] + k - 1))
                    fn((A, B)[k % 2][:, :], PJ[:, k % 2, :], ACT.Relu).then_inc(pj_free[k % 2], 1)
                    if k == 0:
                        act.wait_ge(pj_full[1], tile("ffn", i, 0))
                    if k >= 1:
                        split(k - 1)
                split(3)
            norm("norm3")
            norm("norm4")

            for k in range(2):
                act.wait_ge(pj_full[k], tile("gate", 0, k) + 1)
                fn(GR[:, k, :], PJ[0:M_HEADS, k, :], ACT.Identity, 1.0, mbif[:, k:k + 1]).then_inc(pj_free[k], 1)
            for k in range(2):
                act.wait_ge(pj_free[k], tile("gate", 0, k) + 1)
            act.dma_start(gate_kept.rearrange("g h s -> h g s"), GR[:, :, :]).then_inc(m["g_stored"], 16)
            act.wait_ge(m["g_stored"], 16)
            act.dma_start(gi[:, :], gate_kept[0].rearrange("h (c t) -> (h c) t", t=CHUNK)).then_inc(m["g_back"], 16)
            act.dma_start(gf[:, :], gate_kept[1].rearrange("h (c t) -> (h c) t", t=CHUNK)).then_inc(m["g_back"], 16)
            act.dma_start(negmask[:, :], d["negmask"]).then_inc(m["g_back"], 16)
            act.wait_ge(m["g_back"], 48)
            fn(ga[:, :], gf[:, :], ACT.Abs).then_inc(m["ga_abs"], 1)
            fn(ltmp[:, 0, :], v("lam", 0, R_TILES), ACT.Abs).then_inc(m["lam_abs"], 1)
            act.wait_ge(m["ga_abs"], 1)
            fn(ga[:, :], ga[:, :], ACT.Exp, -1.0).then_inc(m["ga_exp"], 1)
            act.wait_ge(m["lam_abs"], 1)
            fn(ltmp[:, 0, :], ltmp[:, 0, :], ACT.Exp, -1.0).then_inc(m["lam_exp"], 1)
            act.wait_ge(m["ga_last"], 2)
            for k in range(2):
                act.dma_start(last_kept[k].rearrange("(r a) -> r a", a=1), gcol[:, k:k + 1]).then_inc(m["ga_lastback"], 16)
            act.wait_ge(m["ga_lastback"], 32)
            act.dma_start(sc4[:, 0:2, 0:NCH], last_kept[0:2].rearrange("k (h c) -> h k c", c=NCH)) \
                .then_inc(m["ga_lastback"], 16)
            act.wait_ge(m["ga_m"], 2)
            act.dma_start(last_kept[2].rearrange("(h c) -> h c", c=NCH), sc4[:, 2, 0:NCH]).then_inc(m["ga_mback"], 16)
            act.wait_ge(m["ga_mback"], 16)
            act.dma_start(gcol[:, 2:3], last_kept[2].rearrange("(r a) -> r a", a=1)).then_inc(m["ga_mback"], 16)
            act.wait_ge(m["ga_rows"], 2)
            fn(g5[:, 2, :], g5[:, 1, :], ACT.Exp, 1.0, gcol[:, 2:3]).then_inc(m["ga_exps"], 1)
            fn(g5[:, 3, :], gb[:, :], ACT.Exp, -1.0).then_inc(m["ga_exps"], 1)
            fn(g5[:, 4, :], g5[:, 0, :], ACT.Exp, 1.0, gcol[:, 3:4]).then_inc(m["ga_exps"], 1)
            with act.Fori(0, MT // 2) as i:
                for jj in range(2):
                    j = 2 * i + jj
                    p = 3 * jj
                    s = p % 2
                    act.wait_ge(pj_full[s], tile("inner", i, p) + 1)
                    act.wait_ge(m["st_xm"], from16(32 * i + 16 * jj))
                    act.wait_ge(m["m_conv"], from1(2 * i + jj))
                    fn(A[:, :], PJ[:, s, :], ACT.Copy).then_inc(pj_free[s], 1)
                    act.wait_ge(pj_free[s], tile("inner", i, p) + 1)
                    act.dma_start(xm_kept[ds(j, 1), :, :].rearrange("a p s -> (a p) s"), A[:, :]) \
                        .then_inc(m["st_xm"], 16)
                    act.wait_ge(m["m_conv"], from1(2 * i + (jj + 1)))
                    act.wait_ge(m["st_xc"], from16(32 * i + 16 * jj))
                    act.wait_ge(m["m_zs"], from1(2 * i + jj))
                    fn(Fx[:, :], E[:, :], ACT.Silu).then_inc(m["m_xc"], 1)
                    act.wait_ge(m["m_xc"], from1(2 * i + (jj + 1)))
                    act.dma_start(xc_kept[ds(j, 1), :, :].rearrange("a p s -> (a p) s"), Fx[:, :]) \
                        .then_inc(m["st_xc"], 16)
                    s = 1 - s
                    act.wait_ge(pj_full[s], tile("inner", i, p + 1) + 1)
                    act.wait_ge(m["m_zn"], from1(2 * i + jj))
                    fn(H[:, :], PJ[:, s, :], ACT.Silu).then_inc(pj_free[s], 1)
                    s = 1 - s
                    act.wait_ge(pj_full[s], tile("inner", i, p + 2) + 1)
                    act.wait_ge(m["st_o"], from16(32 * i + 16 * jj))
                    fn(O[:, :], PJ[:, s, :], ACT.Sigmoid).then_inc(pj_free[s], 1)
                    act.wait_ge(pj_free[s], tile("inner", i, p + 2) + 1)
                    act.dma_start(o_kept[ds(j, 1), :, :].rearrange("a p s -> (a p) s"), O[:, :]) \
                        .then_inc(m["st_o"], 16)
                    act.wait_ge(m["m_zs"], from1(2 * i + (jj + 1)))
                    act.dma_start(zs_kept[ds(j, 1), :, :].rearrange("a p s -> (a p) s"), Q[:, :]) \
                        .then_inc(m["st_zs"], 16)
                    act.wait_ge(m["m_zn"], from1(2 * i + (jj + 1)))
                    act.dma_start(zn_kept[ds(j, 1), :, :].rearrange("a p s -> (a p) s"), B[:, :]) \
                        .then_inc(m["st_zn"], 16)

            act.wait_ge(ax_full[0], aux("gate", 0, 0) + 1)
            fn(cols[:, :, :].rearrange("p q r -> p (q r)"), AX[:, 0, 0:5 * ROWS], ACT.Copy).then_inc(ax_free[0], 1)
            act.wait_ge(ax_full[1], aux("gate", 0, 1) + 1)
            fn(dlb[:, :], AX[:, 1, 0:ROWS], ACT.Copy).then_inc(ax_free[1], 1)

            def stage(i, u):
                act.wait_ge(h["h_x%d" % (u % 2)], 64 * i + 16 * (u // 2 + 1))
                fn((XMh, GXh)[u // VT][:, u % VT, :], (A, B)[u % 2][:, :], ACT.Copy).then_inc(h["h_xround"], 1)

            def head(i, last):
                act.wait_ge(pj_full[1], tile("mlstm", i, 0))
                stage(i, 4)
                stage(i, 5)
                for p in range(4):
                    act.wait_ge(pj_full[p % 2], tile("mlstm", i, p) + 1)
                    fn(Vh[:, 2 * p:2 * p + 2, :].rearrange("p a s -> p (a s)"), PJ[:, p % 2, :], ACT.Copy) \
                        .then_inc(h["h_vhi"], 1)
                    if p < 2:
                        stage(i, 6 + p)
                for kk in range(KK):
                    act.wait_ge(pj_full[kk], tile("mlstm", i, 4 + kk) + 1)
                    fn(Mqh[:, kk, :], PJ[:, kk, :], ACT.Copy, DK ** -0.5).then_inc(h["h_qhi"], 1)
                act.wait_ge(ax_free[0], aux("mlstm", i, 0) + 1)
                fn(Dt[:, :], Dt[:, :], ACT.Exp).then_inc(h["h_w"], 1)
                for kk in range(KK):
                    act.wait_ge(pj_full[kk], tile("mlstm", i, 6 + kk) + 1)
                    fn(Mkh[:, kk, :], PJ[:, kk, :], ACT.Copy).then_inc(h["h_khi"], 1)
                for hf in range(2):
                    tok = slice(hf * HALF, (hf + 1) * HALF)
                    if hf == 0:
                        act.wait_ge(h["h_s0"], i + 1)
                    else:
                        act.wait_ge(ax_full[1], aux("mlstm", i, 3) + 1)
                    for kk in range(KK):
                        act.wait_ge(ax_free[1 - kk], aux("mlstm", i, 1 + kk) + 1)
                        fn(Mkh[:, kk, tok], (A, B)[kk][:, tok], ACT.Copy).then_inc(h["h_kt%dhi" % kk], 1)
                    if hf == 0:
                        act.wait_ge(h["h_sw"], i + 1)
                    else:
                        act.wait_ge(ax_free[1], aux("mlstm", i, 3) + 1)
                    fn(Msh[:, tok], Sw[:, tok], ACT.Copy).then_inc(h["h_smhi"], 1)
                for step in range(NCH + 2):
                    if step < NCH:
                        g = NCH * i + step
                        act.wait_ge(h["h_c"], g + 1)
                        act.wait_ge(h["h_qc"], from1(g))
                        fn(Ch[:, :, :], Cf[:, :, :], ACT.Copy).then_inc(h["h_chi"], 1)
                    if 1 <= step <= NCH:
                        act.wait_ge(h["h_st2"], NCH * i + step)
                        fn(mst[:, 2:3], mst[:, 1:2], ACT.Sqrt, 1.0, eps[:, 0:1]).then_inc(h["h_std"], 1)
                    if step < NCH:
                        act.wait_ge(h["h_qc"], from1(g + 1))
                        act.wait_ge(h["h_num"], from1(g))
                        if step == 0:
                            for kk in range(KK):
                                act.wait_ge(h["h_kt%dlo" % kk], 2 * i + 2)
                        fn(t1[:, :], PJ[:, 0, 0:DV], ACT.Copy, hc[:, 2, step:step + 1]).then_inc(h["h_t1"], 1)
                    if step >= 2:
                        n = step - 2
                        act.wait_ge(h["h_y"], from1(NCH * i + (n + 1)))
                        fn(GXh[:, :, n * P:(n + 1) * P], yy[:, :].rearrange("p (t s) -> p t s", t=VT),
                           ACT.Copy).then_inc(h["h_yhi"], 1)
                if not last:
                    for u in range(4):
                        stage(i + 1, u)

            for u in range(4):
                stage(0, u)
            with act.Fori(0, M_HEADS - 1) as i:
                head(i, False)
            head(M_HEADS - 1, True)
            norm("norm5")

            with act.Fori(0, R_PAIRS) as i:
                for t in range(RT):
                    s = t % 2
                    act.wait_ge(pj_full[s], tile("lru", i, t) + 1)
                    act.wait_ge(l["l_xc"], from1(3 * i + t))
                    if t == 0:
                        act.wait_ge(g_ready, 3 * i + GREADY["lru"])
                    fn(A[:, :], PJ[:, s, :], ACT.Copy).then_inc(pj_free[s], 1)
                    act.wait_ge(l["l_xc"], from1(3 * i + (t + 1)))
                    fn(XCh[:, t, :], B[:, :], ACT.Copy).then_inc(l["l_xchi"], 1)
                for t in range(RT):
                    s = (3 + t) % 2
                    act.wait_ge(pj_full[s], tile("lru", i, 3 + t) + 1)
                    fn(R3[:, t, :], PJ[:, s, :], ACT.Sigmoid, 1.0, v("rba", 3 * i + t)).then_inc(pj_free[s], 1)
                for t in range(RT):
                    s = (6 + t) % 2
                    act.wait_ge(pj_full[s], tile("lru", i, 6 + t) + 1)
                    act.wait_ge(l["l_h"], from1(3 * i + t))
                    fn(B[:, :], PJ[:, s, :], ACT.Sigmoid, 1.0, v("rbx", 3 * i + t)).then_inc(pj_free[s], 1)
                    act.wait_ge(l["l_rate"], 3 * i + (t + 1))
                    fn(C[:, :], R3[:, t, :], ACT.Exp)
                    fn(Dt[:, :], R3[:, t, :], ACT.Tanh).then_inc(l["l_th"], 1)
                    act.wait_ge(l["l_e"], 3 * i + (t + 1))
                    fn(Dt[:, :], R3[:, t, :], ACT.Sqrt, -1.0).then_inc(l["l_sqrt"], 1)
                act.wait_ge(pj_full[1], tile("lru", i, 0))
                for t in range(RT):
                    s = (9 + t) % 2
                    act.wait_ge(pj_full[s], tile("lru", i, 9 + t) + 1)
                    act.wait_ge(l["l_x"], 3 * i + 3)
                    act.wait_ge(g_ready, 3 * i + (GREADY["lru"] + t))
                    fn(A[:, :], PJ[:, s, :], ACT.Silu).then_inc(pj_free[s], 1)
                    act.wait_ge(l["l_y"], 3 * i + (t + 1))
                    fn(G3h[:, t, :], A[:, :], ACT.Copy).then_inc(g_rounded, 1)
            norm("norm6")

        @block.vector
        def _(dve):
            raise_starts(dve, "dve")
            V = nc.vector

            def tt(out, a, b, op=ALU.mult):
                return V.tensor_tensor(out, a, b, op)

            def stt(out, a, s, b, op0=ALU.mult, op1=ALU.add):
                return V.scalar_tensor_tensor(out=out, in0=a, scalar=s, in1=b, op0=op0, op1=op1)

            def lo(out, whole, hi):
                return V.tensor_tensor(out, whole, hi.bitcast(F32), ALU.subtract)

            def norm(phase):
                dve.wait_ge(rstd_ready, 2 * NORMS.index(phase) + 2)
                g = GAINS[phase]
                if phase not in UREADY:
                    for t in range(KT):
                        stt(X[:, t, :], X[:, t, :], v(g, t), Dt[:, :], ALU.mult, ALU.mult).then_inc(x_scaled, 1)
                    return
                for t in range(KT):
                    if t >= 3:
                        dve.wait_ge(u_ready[(t - 3) % 2], UREADY[phase] // 2 + (t - 3) // 2 + 1)
                    stt((A, B, C)[t % 3][:, :], X[:, t, :], v(g, t), Dt[:, :], ALU.mult, ALU.mult) \
                        .then_inc(y_ready, 1)
                    if t % 2 == 1:
                        u = t - 1
                        dve.wait_ge(u_rounded, UREADY[phase] + u + 1)
                        lo(Ul[:, u, :], (A, B, C)[u % 3][:, :], Uh[:, u, :]).then_inc(u_ready[0], 1)

            def add_down_tile(phase, i, p0, t):
                s = (p0 + t) % 2
                dve.wait_ge(pj_full[s], tile(phase, i, p0 + t) + 1)
                tt(X[:, t, :], PJ[:, s, :], X[:, t, :], ALU.add).then_inc(pj_free[s], 1)

            def add_down(phase, i, p0):
                for t in range(KT):
                    add_down_tile(phase, i, p0, t)

            V.memset(eps[:, :], EPS).then_inc(consts_r, 1)
            V.memset(zero[:, :], 0.0).then_inc(consts_r, 1)
            dve.wait_ge(consts, CONSTS)
            V.tensor_copy(identr[:, :], ident[:, :]).then_inc(consts_r, 1)
            V.tensor_copy(onesr[:, :], ones[:, 0:4]).then_inc(consts_r, 1)
            for t in range(8):
                dve.wait_ge(pj_full[t % 2], tile("read", 0, t) + 1)
                V.tensor_copy(X[:, :, t * P:(t + 1) * P], PJ[:, t % 2, :].rearrange("p (k s) -> p k s", k=KT)) \
                    .then_inc(pj_free[t % 2], 1)
            norm("norm1")

            dve.wait_ge(x_spilled, 16)
            by_chunk = lambda a: a[:, :].rearrange("p (n s) -> p n s", n=NCH)
            with dve.Fori(0, RET_HEADS) as i:
                for q in range(2):
                    scale = 1.0 if q == 0 else float(P) ** -0.5
                    dve.wait_ge(pj_full[q], tile("ret", i, q) + 1)
                    dve.wait_ge(r["r_swapped"], 2 * i + (q + 1))
                    stt(B[:, :], PJ[:, q, :], scale, cos[:, :], ALU.mult, ALU.mult).then_inc(pj_free[q], 1)
                    stt(A[:, :], A[:, :], scale, sin[:, :], ALU.mult, ALU.mult).then_inc(r["r_sin"], 1)
                    dve.wait_ge(pj_free[q], tile("ret", i, q) + 1)
                    dve.wait_ge(r["r_sin"], 2 * i + (q + 1))
                    tt(B[:, :], B[:, :], A[:, :], ALU.add).then_inc(r["r_rotated"], 1)
                    dve.wait_ge(r["r_rotated"], 2 * i + (q + 1))
                    if q == 0:
                        tt(by_chunk(A), by_chunk(B), xi[:, ds(i, 1), :].broadcast_to([P, NCH, P])) \
                            .then_inc(r["r_qx"], 1)
                        dve.wait_ge(r["r_qhi"], i + 1)
                        lo(Ql[:, :], B[:, :], Qh[:, :]).then_inc(r["r_qlo"], 1)
                        dve.wait_ge(r["r_qxhi"], i + 1)
                        lo(QXl[:, :], A[:, :], QXh[:, :]).then_inc(r["r_qxlo"], 1)
                    else:
                        dve.wait_ge(r["r_khi"], i + 1)
                        lo(Kl[:, :], B[:, :], Kh[:, :]).then_inc(r["r_klo"], 1)
                dve.wait_ge(r["r_kthi"], i + 1)
                stt(Ktl[:, :], AX[:, 0, :], v("zeta", i), Kth[:, :].bitcast(F32), ALU.mult, ALU.subtract) \
                    .then_inc(ax_free[0], 1)
                dve.wait_ge(r["r_vthi"], i + 1)
                lo(Vtl[:, :], AX[:, 1, :], Vth[:, :]).then_inc(ax_free[1], 1)
                dve.wait_ge(ax_full[0], aux("ret", i, 2) + 1)
                tt(by_chunk(A), by_chunk(AX[:, 0, :]), decay[:, ds(i, 1), :].broadcast_to([P, NCH, P])) \
                    .then_inc(ax_free[0], 1)
                V.memset(B[:, 0:P], 0.0).then_inc(r["r_state"], 1)
                dve.wait_ge(ax_full[1], aux("ret", i, 3) + 1)
                for n in range(NCH - 1):
                    dve.wait_ge(r["r_state"], 7 * i + (n + 1))
                    ins = stt(B[:, (n + 1) * P:(n + 2) * P], B[:, n * P:(n + 1) * P], v("chunk_decay", i),
                              AX[:, 1, n * P:(n + 1) * P])
                    if n < NCH - 2:
                        ins.then_inc(r["r_state"], 1)
                    else:
                        ins.then_inc(ax_free[1], 1)
                dve.wait_ge(r["r_smhi"], i + 1)
                lo(SMl[:, :], A[:, :], SMh[:, :]).then_inc(r["r_smlo"], 1)
                dve.wait_ge(r["r_shi"], i + 1)
                lo(Kl[:, :], B[:, :], Kh[:, :]).then_inc(r["r_slo"], 1)
                dve.wait_ge(r["r_rstd"], i + 1)
                stt(C[:, :], C[:, :], v("rng", i), B[:, :], ALU.mult, ALU.mult).then_inc(r["r_y1"], 1)
                dve.wait_ge(r["r_y1"], i + 1)
                dve.wait_ge(pj_free[1], tile("ret", i, 3) + 1)
                tt(C[:, :], C[:, :], Dt[:, :]).then_inc(r["r_y"], 1)
                dve.wait_ge(g_rounded, i + (GREADY["ret"] + 1))
                tt(Gl[:, ds(i, 1), :].rearrange("p a s -> p (a s)"), C[:, :],
                   Gh[:, ds(i, 1), :].rearrange("p a s -> p (a s)").bitcast(F32), ALU.subtract).then_inc(g_ready, 1)
            dve.wait_ge(x_back, 16)
            add_down("ret_down", 0, 0)

            V.memset(Cp[:, 0:8], 0.0).then_inc(c["c_pad"], 1)
            dve.wait_ge(c["c_pad"], 1)
            with dve.Fori(0, 2) as i:
                for cc in range(2):
                    q = 2 * i + cc
                    p = 3 * cc + 2
                    dve.wait_ge(pj_full[p % 2], tile("conv", i, p) + 1)
                    dve.wait_ge(pj_free[(p - 1) % 2], tile("conv", i, p - 1) + 1)
                    tt(Cp[:, 8:8 + S], PJ[:, p % 2, :], B[:, :]).then_inc(pj_free[p % 2], 1)
                    dve.wait_ge(pj_free[p % 2], tile("conv", i, p) + 1)
                    V.tensor_scalar(Dt[:, :], Cp[:, 6:6 + S], v("cnw", q), None, ALU.mult).then_inc(c["c_0"], 1)
                    dve.wait_ge(c["c_0"], 2 * i + (cc + 1))
                    stt(Dt[:, :], Cp[:, 7:7 + S], v("cnw", CONV_TILES + q), Dt[:, :]).then_inc(c["c_1"], 1)
                    dve.wait_ge(c["c_1"], 2 * i + (cc + 1))
                    stt(Dt[:, :], Cp[:, 8:8 + S], v("cnw", 2 * CONV_TILES + q), Dt[:, :]).then_inc(c["c_2"], 1)
                    dve.wait_ge(c["c_2"], 2 * i + (cc + 1))
                    dve.wait_ge(pj_free[(p - 2) % 2], tile("conv", i, p - 2) + 1)
                    tt(Dt[:, :], Dt[:, :], A[:, :]).then_inc(c["c_y"], 1)
                    dve.wait_ge(c["c_rstd"], 2 * i + (cc + 1))
                    stt(Dt[:, :], Dt[:, :], v("cng", q), B[:, :], ALU.mult, ALU.mult).then_inc(c["c_n"], 1)
                    dve.wait_ge(g_rounded, 2 * i + (GREADY["conv"] + cc + 1))
                    tt(Gl[:, ds(q, 1), :].rearrange("p a s -> p (a s)"), Dt[:, :],
                       Gh[:, ds(q, 1), :].rearrange("p a s -> p (a s)").bitcast(F32), ALU.subtract) \
                        .then_inc(g_ready, 1)
            add_down("conv_down", 0, 0)
            norm("norm2")

            with dve.Fori(0, FF_BLOCKS) as i:
                for k in range(5):
                    if k < 4:
                        T = (A, B)[k % 2]
                        dve.wait_ge(pj_free[k % 2], tile("ffn", i, k) + 1)
                        tt(T[:, :], T[:, :], T[:, :]).then_inc(f_sq, 1)
                    if k >= 1:
                        dve.wait_ge(g_rounded, 4 * i + (GREADY["ffn"] + k))
                        lo(Gl[:, k - 1, :], (A, B)[(k - 1) % 2][:, :], Gh[:, k - 1, :]).then_inc(g_ready, 1)
                add_down("ffn", i, 4)
            norm("norm3")
            dve.wait_ge(x_scaled, 8)
            norm("norm4")

            steps = [0]

            def step(ins):
                steps[0] += 1
                ins.then_inc(m["ga_step"], 1)
                dve.wait_ge(m["ga_step"], steps[0])

            def half_log1p(e, z, zz, out):
                step(V.tensor_scalar(z, e, 2.0, None, ALU.add))
                step(V.reciprocal(z, z))
                step(tt(z, e, z))
                step(tt(zz, z, z))
                step(V.tensor_scalar(out, zz, 1.0 / 15, None, ALU.mult))
                for n in (13, 11, 9, 7, 5, 3):
                    step(stt(out, out, 1.0 / n, zz, ALU.add, ALU.mult))
                step(stt(out, out, 1.0, z, ALU.add, ALU.mult))

            dve.wait_ge(m["lam_exp"], 1)
            half_log1p(ltmp[:, 0, :], ltmp[:, 1, :], ltmp[:, 2, :], ltmp[:, 3, :])
            step(V.tensor_scalar(ltmp[:, 1, :], v("lam", 0, R_TILES), -1.0, 0.0, ALU.mult, ALU.max))
            step(stt(ltmp[:, 2, :], ltmp[:, 3, :], 2.0, ltmp[:, 1, :]))
            step(V.tensor_scalar(lra[:, :], ltmp[:, 2, :], -8.0, None, ALU.mult))
            dve.wait_ge(m["ga_exp"], 1)
            half_log1p(ga[:, :], gb[:, :], gc_[:, :], gF[:, :])
            step(V.tensor_scalar(gb[:, :], gf[:, :], 0.0, None, ALU.min))
            step(stt(gc_[:, :], gF[:, :], -2.0, gb[:, :]))
            step(V.memset(gone[:, :], 1.0))
            step(V.memset(gzero[:, :], 0.0))
            step(V.tensor_tensor_scan(gF[:, :], gone[:, :], gc_[:, :], 0.0, ALU.mult, ALU.add))
            step(tt(g5[:, 0, :], gi[:, :], gF[:, :], ALU.subtract))
            step(V.tensor_tensor_scan(gA[:, :], g5[:, 0, :], gzero[:, :], -3.0e38, ALU.max, ALU.add))
            V.tensor_copy(gcol[:, 0:1], gF[:, CHUNK - 1:CHUNK]).then_inc(m["ga_last"], 1)
            V.tensor_copy(gcol[:, 1:2], gA[:, CHUNK - 1:CHUNK]).then_inc(m["ga_last"], 1)
            dve.wait_ge(m["ga_lastback"], 48)
            V.memset(sc4[:, 2, 0:1], 0.0).then_inc(m["ga_m"], 1)
            V.tensor_tensor_scan(sc4[:, 2, 1:NCH + 1], sc4[:, 1, 0:NCH], sc4[:, 0, 0:NCH], 0.0,
                                 ALU.max, ALU.add).then_inc(m["ga_m"], 1)
            dve.wait_ge(m["ga_mback"], 32)
            step(V.tensor_scalar(gM[:, :], gA[:, :], gcol[:, 2:3], None, ALU.max))
            step(tt(gb[:, :], gF[:, :], gM[:, :], ALU.add))
            V.tensor_scalar(gcol[:, 3:4], gM[:, CHUNK - 1:CHUNK], -1.0, None, ALU.mult).then_inc(m["ga_rows"], 1)
            V.tensor_scalar(g5[:, 1, :], gM[:, :], -1.0, None, ALU.mult).then_inc(m["ga_rows"], 1)
            dve.wait_ge(m["ga_exps"], 1)
            V.tensor_scalar(gdiag[:, :], ident[0:ROWS, 0:ROWS], g5[:, 2, CHUNK - 1:CHUNK], None, ALU.mult) \
                .then_inc(m["ga_dl"], 1)
            V.memset(Ap[:, 0:8], 0.0).then_inc(m["m_pad"], 1)
            dve.wait_ge(m["m_pad"], 1)
            with dve.Fori(0, MT // 2) as i:
                for jj in range(2):
                    j = 2 * i + jj
                    p = 3 * jj
                    dve.wait_ge(pj_free[p % 2], tile("inner", i, p) + 1)
                    dve.wait_ge(m["m_xc"], from1(2 * i + jj))
                    V.tensor_scalar(E[:, :], Ap[:, 5:5 + S], v("mcw", j), v("mcb", j), ALU.mult, ALU.add) \
                        .then_inc(m["m_c0"], 1)
                    dve.wait_ge(m["m_c0"], 2 * i + (jj + 1))
                    stt(E[:, :], Ap[:, 6:6 + S], v("mcw", MT + j), E[:, :]).then_inc(m["m_c1"], 1)
                    dve.wait_ge(m["m_c1"], 2 * i + (jj + 1))
                    stt(E[:, :], Ap[:, 7:7 + S], v("mcw", 2 * MT + j), E[:, :]).then_inc(m["m_c2"], 1)
                    dve.wait_ge(m["m_c2"], 2 * i + (jj + 1))
                    stt(E[:, :], Ap[:, 8:8 + S], v("mcw", 3 * MT + j), E[:, :]).then_inc(m["m_conv"], 1)
                    dve.wait_ge(pj_free[(p + 1) % 2], tile("inner", i, p + 1) + 1)
                    dve.wait_ge(m["m_xc"], from1(2 * i + (jj + 1)))
                    dve.wait_ge(m["st_zs"], from16(32 * i + 16 * jj))
                    stt(Q[:, :], Fx[:, :], v("msk", j), H[:, :], ALU.mult, ALU.mult).then_inc(m["m_zs"], 1)
                    dve.wait_ge(m["st_zn"], from16(32 * i + 16 * jj))
                    V.tensor_scalar(B[:, :], H[:, :], v("mnw", j), None, ALU.mult).then_inc(m["m_zn"], 1)

            for s in range(2):
                dve.wait_ge(ax_free[s], aux("gate", 0, s) + 1)

            def stage(i, u):
                dve.wait_ge(h["h_xround"], 8 * i + (u + 1))
                lo((XMl, GXl)[u // VT][:, u % VT, :], (A, B)[u % 2][:, :], (XMh, GXh)[u // VT][:, u % VT, :]) \
                    .then_inc(h["h_xsplit"], 1)

            def head(i, last):
                V.tensor_copy(hc[:, 0:5, :], cols[:, :, ds(NCH * i, NCH)])
                V.tensor_copy(hc[:, 5, :], dlb[:, ds(NCH * i, NCH)]).then_inc(h["h_hc"], 1)
                dve.wait_ge(h["h_hc"], i + 1)
                tt(by_chunk(Dt), ident[:, :].unsqueeze(1).broadcast_to([P, NCH, P]),
                   hc[:, 1, :].unsqueeze(2).broadcast_to([P, NCH, P])).then_inc(h["h_diag"], 1)
                stage(i, 4)
                stage(i, 5)
                for p in range(4):
                    dve.wait_ge(h["h_vhi"], 4 * i + (p + 1))
                    lo(Vl[:, 2 * p:2 * p + 2, :].rearrange("p a s -> p (a s)"), PJ[:, p % 2, :],
                       Vh[:, 2 * p:2 * p + 2, :].rearrange("p a s -> p (a s)")).then_inc(pj_free[p % 2], 1)
                    if p < 2:
                        stage(i, 6 + p)
                for kk in range(KK):
                    dve.wait_ge(h["h_qhi"], 2 * i + (kk + 1))
                    stt(Mql[:, kk, :], PJ[:, kk, :], DK ** -0.5, Mqh[:, kk, :].bitcast(F32), ALU.mult,
                        ALU.subtract).then_inc(pj_free[kk], 1)
                dve.wait_ge(ax_full[0], aux("mlstm", i, 0) + 1)
                tt(by_chunk(Dt), by_chunk(AX[:, 0, :]), hc[:, 0, :].unsqueeze(2).broadcast_to([P, NCH, P]),
                   ALU.add).then_inc(ax_free[0], 1)
                for kk in range(KK):
                    dve.wait_ge(h["h_khi"], 2 * i + (kk + 1))
                    lo(Mkl[:, kk, :], PJ[:, kk, :], Mkh[:, kk, :]).then_inc(pj_free[kk], 1)
                for kk in range(KK):
                    dve.wait_ge(ax_full[1 - kk], aux("mlstm", i, 1 + kk) + 1)
                    tt(by_chunk((A, B)[kk]), by_chunk(AX[:, 1 - kk, :]),
                       hc[:, 4, :].unsqueeze(2).broadcast_to([P, NCH, P])).then_inc(ax_free[1 - kk], 1)
                dve.wait_ge(h["h_w"], i + 1)
                for hf in range(2):
                    tok = slice(hf * HALF, (hf + 1) * HALF)
                    if hf == 0:
                        dve.wait_ge(h["h_s0"], i + 1)
                    else:
                        dve.wait_ge(ax_full[1], aux("mlstm", i, 3) + 1)
                    tt(Sw[:, tok], AX[:, 1, tok], Dt[:, tok]).then_inc((h["h_sw"], ax_free[1])[hf], 1)
                    dve.wait_ge(h["h_kt1hi"], 2 * i + (hf + 1))
                    lo(Mkl[:, 1, tok], B[:, tok], Mkh[:, 1, tok]).then_inc(h["h_kt1lo"], 1)
                    dve.wait_ge(h["h_smhi"], 2 * i + (hf + 1))
                    lo(Msl[:, tok], Sw[:, tok], Msh[:, tok]).then_inc(h["h_smlo"], 1)
                V.memset(Cf[:, :, :], 0.0).then_inc(h["h_c"], 1)
                for step in range(NCH + 2):
                    if 1 <= step < NCH:
                        n = step - 1
                        dve.wait_ge(h["h_cu"], 7 * i + step)
                        dve.wait_ge(h["h_clo0"], NCH * i + step)
                        dve.wait_ge(h["h_clo1"], NCH * i + step)
                        stt(Cf[:, :, 0:DV], Cf[:, :, 0:DV], hc[:, 5, n:n + 1],
                            AX[:, 0, :].rearrange("p (k a) -> p k a", k=KK))
                        stt(Cf[:, :, DV:DV + 2], Cf[:, :, DV:DV + 2], hc[:, 5, n:n + 1],
                            AX[:, 1, HALF:HALF + 4].rearrange("p (k a) -> p k a", k=KK)).then_inc(h["h_c"], 1)
                    if 1 <= step <= NCH:
                        n = step - 1
                        g = NCH * i + n
                        dve.wait_ge(h["h_qc"], from1(g + 1))
                        V.tensor_scalar(dcol[:, 0:1], AX[:, 1, 0:1], hc[:, 2, n:n + 1], AX[:, 1, 2:3], ALU.mult,
                                        ALU.add).then_inc(h["h_den"], 1)
                        dve.wait_ge(h["h_den"], from1(g + 1))
                        V.tensor_scalar(dcol[:, 3:4], dcol[:, 0:1], -1.0, hc[:, 3, n:n + 1], ALU.mult,
                                        ALU.max).then_inc(h["h_d0"], 1)
                        dve.wait_ge(h["h_t1"], from1(g + 1))
                        dve.wait_ge(h["h_sv"], g + 1)
                        tt(num[:, :], PJ[:, 0, DV:2 * DV], t1[:, :], ALU.add).then_inc(h["h_num"], 1)
                        dve.wait_ge(h["h_d0"], g + 1)
                        tt(dcol[:, 1:2], dcol[:, 0:1], dcol[:, 3:4], ALU.max).then_inc(h["h_d1"], 1)
                        dve.wait_ge(h["h_d1"], g + 1)
                        V.reciprocal(dcol[:, 2:3], dcol[:, 1:2]).then_inc(h["h_d2"], 1)
                        dve.wait_ge(h["h_oT"], from1(g + 1))
                        dve.wait_ge(h["h_num"], from1(g + 1))
                        dve.wait_ge(h["h_d2"], g + 1)
                        dve.wait_ge(h["h_hnT"], from1(g))
                        stt(hh[:, :], num[:, :], dcol[:, 2:3], PJ[:, 1, 0:DV], ALU.mult, ALU.mult) \
                            .then_inc(h["h_hh"], 1)
                        dve.wait_ge(h["h_hh"], from1(g + 1))
                        V.bn_stats(bst[:, 0:6], hh[:, :]).then_inc(h["h_st"], 1)
                        dve.wait_ge(h["h_st"], g + 1)
                        V.memset(dcol[:, 7:8], 0.0)
                        V.bn_aggr(mst[:, 0:2], bst[:, 0:6]).then_inc(h["h_st2"], 1)
                    if step < NCH:
                        g = NCH * i + step
                        dve.wait_ge(h["h_chi"], g + 1)
                        lo(Cl[:, 0, :], Cf[:, 0, :], Ch[:, 0, :]).then_inc(h["h_clo0"], 1)
                    if step >= 2:
                        g = NCH * i + (step - 2)
                        dve.wait_ge(h["h_hnT"], from1(g + 1))
                        dve.wait_ge(h["h_znc"], 16 * g + 16)
                        dve.wait_ge(h["h_done"], from1(g))
                        tt(yy[:, :], PJ[:, 1, DV:2 * DV], znc[:, :, :].rearrange("p t s -> p (t s)")) \
                            .then_inc(h["h_y1"], 1)
                    if 1 <= step <= NCH:
                        g = NCH * i + (step - 1)
                        dve.wait_ge(h["h_std"], g + 1)
                        V.reciprocal(mst[:, 3:4], mst[:, 2:3]).then_inc(h["h_rs"], 1)
                        dve.wait_ge(h["h_rs"], g + 1)
                        V.tensor_scalar(hh[:, :], hh[:, :], mst[:, 0:1], mst[:, 3:4], ALU.subtract, ALU.mult) \
                            .then_inc(h["h_hn"], 1)
                for t in range(KT):
                    add_down_tile("mlstm", i, 8, t)
                    if t % 2 == 0 and not last:
                        stage(i + 1, t // 2)

            for u in range(4):
                stage(0, u)
            with dve.Fori(0, M_HEADS - 1) as i:
                head(i, False)
            head(M_HEADS - 1, True)
            norm("norm5")

            V.memset(Ap[:, 0:8], 0.0).then_inc(l["l_pad"], 1)
            dve.wait_ge(l["l_pad"], 1)
            with dve.Fori(0, R_PAIRS) as i:
                for t in range(RT):
                    j = 3 * i + t
                    dve.wait_ge(pj_free[t % 2], tile("lru", i, t) + 1)
                    dve.wait_ge(l["l_xclo"], from1(3 * i + t))
                    V.tensor_scalar(B[:, :], Ap[:, 5:5 + S], v("rcw", j), v("rcb", j), ALU.mult, ALU.add) \
                        .then_inc(l["l_c0"], 1)
                    dve.wait_ge(l["l_c0"], 3 * i + (t + 1))
                    stt(B[:, :], Ap[:, 6:6 + S], v("rcw", R_TILES + j), B[:, :]).then_inc(l["l_c1"], 1)
                    dve.wait_ge(l["l_c1"], 3 * i + (t + 1))
                    stt(B[:, :], Ap[:, 7:7 + S], v("rcw", 2 * R_TILES + j), B[:, :]).then_inc(l["l_c2"], 1)
                    dve.wait_ge(l["l_c2"], 3 * i + (t + 1))
                    stt(B[:, :], Ap[:, 8:8 + S], v("rcw", 3 * R_TILES + j), B[:, :]).then_inc(l["l_xc"], 1)
                    dve.wait_ge(l["l_xchi"], 3 * i + (t + 1))
                    lo(XCl[:, t, :], B[:, :], XCh[:, t, :]).then_inc(l["l_xclo"], 1)
                for t in range(RT):
                    j = 3 * i + t
                    dve.wait_ge(pj_free[(3 + t) % 2], tile("lru", i, 3 + t) + 1)
                    V.tensor_scalar(R3[:, t, :], R3[:, t, :], lra[:, ds(j, 1)], None, ALU.mult) \
                        .then_inc(l["l_rate"], 1)
                for t in range(RT):
                    dve.wait_ge(l["l_ix"], from1(3 * i + t))
                    tt(A[:, :], XCh[:, t, :].bitcast(F32), XCl[:, t, :].bitcast(F32), ALU.add).then_inc(l["l_x"], 1)
                    dve.wait_ge(l["l_x"], 3 * i + (t + 1))
                    dve.wait_ge(pj_free[(6 + t) % 2], tile("lru", i, 6 + t) + 1)
                    tt(B[:, :], B[:, :], A[:, :]).then_inc(l["l_ix"], 1)
                    dve.wait_ge(l["l_th"], 3 * i + (t + 1))
                    tt(R3[:, t, :], C[:, :], C[:, :]).then_inc(l["l_aa"], 1)
                    dve.wait_ge(l["l_aa"], 3 * i + (t + 1))
                    stt(R3[:, t, :], R3[:, t, :], 1.0, Dt[:, :], ALU.add, ALU.mult).then_inc(l["l_e"], 1)
                    dve.wait_ge(l["l_sqrt"], 3 * i + (t + 1))
                    dve.wait_ge(l["l_ix"], from1(3 * i + (t + 1)))
                    tt(B[:, :], B[:, :], Dt[:, :]).then_inc(l["l_bt"], 1)
                    dve.wait_ge(l["l_bt"], 3 * i + (t + 1))
                    V.tensor_tensor_scan(R3[:, t, :], C[:, :], B[:, :], 0.0, ALU.mult, ALU.add) \
                        .then_inc(l["l_h"], 1)
                for t in range(RT):
                    dve.wait_ge(pj_free[(9 + t) % 2], tile("lru", i, 9 + t) + 1)
                    dve.wait_ge(l["l_h"], from1(3 * i + (t + 1)))
                    tt(A[:, :], A[:, :], R3[:, t, :]).then_inc(l["l_y"], 1)
                    dve.wait_ge(g_rounded, 3 * i + (GREADY["lru"] + t + 1))
                    lo(G3l[:, t, :], A[:, :], G3h[:, t, :]).then_inc(g_ready, 1)
                add_down("lru", i, 12)
            norm("norm6")
            for t in range(8):
                T = (B, C)[t % 2]
                dve.wait_ge(pj_full[t % 2], tile("write", 0, t) + 1)
                if t >= 2:
                    dve.wait_ge(out_stored[t % 2], 16 * (t // 2))
                V.tensor_copy(T[:, :], PJ[:, t % 2, :]).then_inc(pj_free[t % 2], 1)


def kernel(**inputs):
    import numpy as np
    import concourse.bacc as bacc
    from concourse.bass_utils import run_bass_kernel_spmd

    arrays = {k: np.asarray(v) for k, v in inputs.items()}
    f32 = np.float32

    def columns(a):
        a = np.asarray(a)
        n = a.shape[-1] // P
        return a.reshape(-1, n, P).transpose(2, 0, 1).reshape(P, -1)

    def gate_weight(w):
        full = np.zeros((R_PAIRS, RT * P, RT * P), f32)
        n = w.shape[-1]
        for b in range(2):
            full[:, b * n:(b + 1) * n, b * n:(b + 1) * n] = w[b::2]
        out = np.zeros((R_PAIRS, P, 8, P), f32)
        for q, (k, m) in enumerate(GATE_TILES):
            out[:, :, q, :] = full[:, k * P:(k + 1) * P, m * P:(m + 1) * P]
        return out.reshape(R_PAIRS, P, 8 * P)

    idx = np.arange(CHUNK, dtype=f32)
    log_gamma = np.log(f32(1.0) - f32(2.0) ** (f32(-5.0) - np.arange(RET_HEADS, dtype=f32))).astype(f32)
    diff = idx[None, :] - idx[:, None]
    decay = np.where(diff[None] >= 0, np.exp(log_gamma[:, None, None] * np.maximum(diff, 0)[None]), 0)
    zeta = np.exp(log_gamma[:, None] * (CHUNK - 1 - idx)[None])
    xi = np.exp(log_gamma[:, None] * (idx + 1)[None])
    half = P // 2
    inv_freq = (f32(1.0) / (f32(10000.0) ** (np.arange(half, dtype=f32) / f32(half)))).astype(f32)
    ang = inv_freq[:, None] * np.arange(S, dtype=f32)[None]
    cos, sin = np.cos(ang), np.sin(ang)
    const = {
        "ident": np.eye(P),
        "ones": np.ones((P, P)),
        "group64": np.kron(np.eye(2), np.ones((64, 64))),
        "cos": np.concatenate([cos, cos]),
        "sin": np.concatenate([-sin, sin]),
        "decay": decay.transpose(1, 0, 2),
        "xi": np.broadcast_to(xi[None], (P, RET_HEADS, P)),
        "negmask": np.where(diff >= 0, 0.0, -1e30),
    }
    vectors = {
        "n1g": arrays["norm1_g"], "n2g": arrays["norm2_g"], "n3g": arrays["final_norm_g"],
        "n4g": arrays["ln_g_2"][0], "n5g": arrays["ln_g_2"][1], "n6g": arrays["final_g_2"],
        "cnw": arrays["conv_w"], "cng": arrays["conv_norm_g"], "rng": arrays["ret_norm_g"],
        "mcw": arrays["m_conv_w_2"][0], "mcb": arrays["m_conv_b_2"][0], "mnw": arrays["m_norm_w_2"][0],
        "msk": arrays["m_skip_2"][0], "rcw": arrays["r_conv_w_2"][0], "rcb": arrays["r_conv_b_2"][0],
        "rba": arrays["r_b_a_2"][0], "rbx": arrays["r_b_x_2"][0], "lam": arrays["r_lam_2"][0],
    }
    packed = {k: columns(a) for k, a in vectors.items()}
    packed["zeta"] = zeta.T
    packed["chunk_decay"] = np.broadcast_to(np.exp(log_gamma * CHUNK)[None], (P, RET_HEADS))
    feeds = {k: np.ascontiguousarray(a, dtype=f32) for k, a in const.items()}
    feeds |= {
        "x": arrays["x"][0], "w_in": arrays["w_in"], "w_out": arrays["w_out"], "w_up": arrays["w_up"],
        "w_down": arrays["w_down"], "m_w_in": arrays["m_w_in_2"][0],
        "m_w_q": arrays["m_w_q_2"][0].reshape(M_INNER, DK), "m_w_k": arrays["m_w_k_2"][0].reshape(M_INNER, DK),
        "m_w_v": arrays["m_w_v_2"][0].reshape(M_INNER, DV), "m_w_out": arrays["m_w_out_2"][0],
        "r_w_in": arrays["r_w_in_2"][0], "r_w_out": arrays["r_w_out_2"][0],
        "gate_a": gate_weight(arrays["r_w_a_2"][0]), "gate_x": gate_weight(arrays["r_w_x_2"][0]),
        "mbif": np.stack([arrays["m_b_i_2"][0], arrays["m_b_f_2"][0]], 1),
        "vec": np.concatenate([packed[k] for k, _ in VEC], 1),
    }
    feeds = {k: np.ascontiguousarray(a) for k, a in feeds.items()}
    nc = bacc.Bacc("TRN2", target_bir_lowering=False, num_devices=1)
    d = {k: nc.dram_tensor(k, a.shape, mybir.dt.from_np(a.dtype), kind="ExternalInput").ap()
         for k, a in feeds.items()}
    d["out"] = nc.dram_tensor("out", (S, D), F32, kind="ExternalOutput").ap()
    build(nc, d)
    got = run_bass_kernel_spmd(nc, [feeds], core_ids=[0])
    return np.asarray(got.results[0]["out"]).reshape(1, S, D)
```

```python
from contextlib import ExitStack

import concourse.bass as bass
from concourse import mybir

F32 = mybir.dt.float32
F32R = mybir.dt.float32r
ACT = mybir.ActivationFunctionType
ALU = mybir.AluOpType
ds = bass.ds

P = 128
D = 1024
S = 1024
KT = D // P
HALF = 512
EPS = 1e-6

RET_HEADS = 4
CONV_TILES = 4
CHUNK = 128
CONSTS = 8 * 16
NCH = S // CHUNK
RET_COL = 1536

FF_BLOCKS = 8

M_HEADS = 4
M_INNER = 2048
MT = M_INNER // P
DV = 512
DK = 256
VT = DV // P
KK = DK // P
ROWS = M_HEADS * NCH

R_WIDTH = 1536
R_TILES = R_WIDTH // P
R_PAIRS = 4
RT = 3
GATE_TILES = [(0, 0), (1, 0), (0, 1), (1, 1), (2, 1), (1, 2), (2, 2)]

PHASES = [
    ("read", 1, 0, 8, 0),
    ("norm1", 1, 0, 0, 2),
    ("ret", RET_HEADS, 4, 4, 6),
    ("ret_down", 1, 4, 8, 0),
    ("conv", 2, 6, 6, 2),
    ("conv_down", 1, 4, 8, 0),
    ("norm2", 1, 0, 0, 2),
    ("ffn", FF_BLOCKS, 8, 12, 0),
    ("norm3", 1, 0, 0, 2),
    ("norm4", 1, 0, 0, 2),
    ("gate", 1, 2, 2, 2),
    ("inner", MT // 2, 6, 6, 0),
    ("mlstm", M_HEADS, 8, 16, 4),
    ("norm5", 1, 0, 0, 2),
    ("lru", R_PAIRS, 12, 20, 0),
    ("norm6", 1, 0, 0, 2),
    ("write", 1, 0, 8, 0),
]


def first_of(column):
    at, out = 0, {}
    for row in PHASES:
        out[row[0]] = at
        at += row[1] * row[column]
    return out, at


UNIT0, UNITS = first_of(2)
PROJ0, _ = first_of(3)
AUX0, _ = first_of(4)
UNITS_OF = {row[0]: row[2] for row in PHASES}
PROJ_OF = {row[0]: row[3] for row in PHASES}
AUX_OF = {row[0]: row[4] for row in PHASES}


def slot_uses(first, per, i, k):
    return first // 2 + (per // 2) * i + k // 2


VEC = [("n1g", KT), ("n2g", KT), ("n3g", KT), ("n4g", KT), ("n5g", KT),
       ("cnw", 3 * CONV_TILES), ("cng", CONV_TILES), ("rng", RET_HEADS), ("zeta", RET_HEADS),
       ("chunk_decay", RET_HEADS), ("mcw", 4 * MT), ("mcb", MT), ("mnw", MT), ("msk", MT),
       ("rcw", 4 * R_TILES), ("rcb", R_TILES), ("rba", R_TILES), ("rbx", R_TILES),
       ("lam", R_TILES)]
VEC_AT = {}
VEC_N = 0
for _name, _n in VEC:
    VEC_AT[_name] = VEC_N
    VEC_N += _n


START1 = {
    "pool": ["w_split0", "w_split1", "h_y", "h_done", "l_ix"],
    "pe": ["w_used0", "h_qc", "h_oT", "h_hnT"],
    "act": ["g_rounded", "h_t1", "h_yhi", "m_xc"],
    "dve": ["g_ready", "c_n", "m_conv", "m_zs", "m_zn", "h_hh", "h_y1", "h_den",
            "h_num", "l_xc", "l_h", "l_xclo"],
}
START16 = {"act": ["st_xm", "st_xc", "st_zn", "st_zs", "st_o"]}


def from1(n):
    return n + 1


def from16(n):
    return n + 16


def build(nc, d):
    ctx = ExitStack()
    with ctx:
        def dram(name, shape):
            return nc.dram_tensor(name, shape, F32, kind="Internal").ap()

        by_name = {}

        def sem(name):
            by_name[name] = ctx.enter_context(nc.semaphore(name))
            return by_name[name]

        def raise_starts(engine, who):
            for name in START1.get(who, []):
                engine.sem_inc(by_name[name], 1)
            for name in START16.get(who, []):
                engine.sem_inc(by_name[name], 16)

        x_kept = dram("x_kept", (P, KT, S))
        xm_kept = dram("xm_kept", (MT, P, S))
        xc_kept = dram("xc_kept", (MT, P, S))
        o_kept = dram("o_kept", (MT, P, S))
        zn_kept = dram("zn_kept", (MT, P, S))
        zs_kept = dram("zs_kept", (MT, P, S))
        gate_kept = dram("gate_kept", (2, M_HEADS, S))
        last_kept = dram("last_kept", (3, ROWS))

        base = nc.sbuf_base
        end = nc.sbuf_usable_end
        top = [(base + 31) // 32 * 32]

        def place(name, shape, dt=F32, at=None):
            size = 4
            for n in shape[1:]:
                size *= n
            size = (size + 31) // 32 * 32
            where = top[0] if at is None else at
            t = nc.alloc_sbuf_tensor_at(name, list(shape), dt, offset=where)
            assert where + size <= end, (name, where + size - end)
            if at is None:
                top[0] += size
            return t, where + size

        def keep(name, shape, dt=F32):
            return place(name, shape, dt)[0]

        X_AT = top[0]
        X = keep("x_res", [P, KT, S])
        X_END = top[0]
        raw = keep("w_raw", [P, 2, 1024])
        wh = keep("w_hi", [P, 2, 1024], F32R)
        wl = keep("w_lo", [P, 2, 1024], F32R)
        ident = keep("ident", [P, P])
        identr = keep("identr", [P, P], F32R)
        ones = keep("ones", [P, P])
        eps = keep("eps", [P, 1])
        zero = keep("zero", [P, 1])
        onesr = keep("onesr", [P, 4], F32R)
        group64 = keep("group64", [P, P])
        mbif = keep("mbif", [2 * M_HEADS, 1])
        vec = keep("vec", [P, VEC_N])
        lra = keep("lru_rate", [P, 2 * R_TILES])
        ltmp = keep("lru_tmp", [P, 4, R_TILES])

        def v(name, k=0, n=1):
            return vec[:, ds(VEC_AT[name] + k, n)]

        Ap = keep("tile_a", [P, 8 + S])
        A = Ap[:, 8:8 + S]
        B = keep("tile_b", [P, S])
        C = keep("tile_c", [P, S])
        Dt = keep("tile_d", [P, S])
        U_AT = top[0]
        Uh = keep("u_hi", [P, KT, S], F32R)
        Ul = keep("u_lo", [P, KT, S], F32R)
        V_AT = top[0]
        Gh = keep("g_hi", [P, VT, S], F32R)
        Gl = keep("g_lo", [P, VT, S], F32R)
        G_END = top[0]

        def area(at, limit):
            cur = [at]

            def put(name, shape, dt=F32):
                t, cur[0] = place(name, shape, dt, at=cur[0])
                assert cur[0] <= limit, (name, cur[0] - limit)
                return t
            return put

        XT = place("tokens", [P, S // P, D], F32, at=U_AT)[0]
        gain6 = place("gain6", [P, D], F32, at=V_AT)[0]
        rcol = place("rstd6", [P, 2, 2 * (S // P)], F32, at=V_AT + 4 * D)[0]

        put = area(X_AT, X_END)
        Qh, Ql = put("q_hi", [P, S], F32R), put("q_lo", [P, S], F32R)
        Kh, Kl = put("k_hi", [P, S], F32R), put("k_lo", [P, S], F32R)
        QXh, QXl = put("qx_hi", [P, S], F32R), put("qx_lo", [P, S], F32R)
        Kth, Ktl = put("kt_hi", [P, S], F32R), put("kt_lo", [P, S], F32R)
        put = area(G_END, end)
        Vth, Vtl = put("vt_hi", [P, S], F32R), put("vt_lo", [P, S], F32R)
        SMh, SMl = put("sm_hi", [P, S], F32R), put("sm_lo", [P, S], F32R)
        cos = put("cos", [P, S])
        sin = put("sin", [P, S])
        decay = put("decay", [P, RET_HEADS, P])
        xi = put("xi", [P, RET_HEADS, P])

        put = area(G_END, end)
        Cp = put("conv_in", [P, 8 + S])

        put = area(V_AT, end)
        E = put("inner_e", [P, S])
        Fx = put("inner_xc", [P, S])
        H = put("inner_z", [P, S])
        Q = put("inner_q", [P, S])
        O = put("inner_o", [P, S])
        GR = put("gate_rows", [2 * M_HEADS, S])

        put = area(U_AT, end)
        GXh = put("m_x_hi", [P, VT, S], F32R)
        GXl = put("m_x_lo", [P, VT, S], F32R)
        Vh = put("m_v_hi", [P, NCH, DV], F32R)
        Vl = put("m_v_lo", [P, NCH, DV], F32R)
        Mqh = put("m_q_hi", [P, KK, S], F32R)
        Mql = put("m_q_lo", [P, KK, S], F32R)
        Mkh = put("m_k_hi", [P, KK, S], F32R)
        Mkl = put("m_k_lo", [P, KK, S], F32R)
        XMh = place("m_xm_hi", [P, VT, S], F32R, at=U_AT + 64 * S)[0]
        XMl = place("m_xm_lo", [P, VT, S], F32R, at=U_AT + 80 * S)[0]
        C_AT = U_AT + 96 * S
        Cf = put("m_c", [P, KK, 514])
        Ch = put("m_c_hi", [P, KK, 514], F32R)
        Cl = put("m_c_lo", [P, KK, 514], F32R)
        negmask = put("negmask", [P, P])
        cols = put("cols", [P, 5, ROWS])
        hc = put("head_cols", [P, 6, NCH])
        dlb = put("dlb", [P, ROWS])
        num = put("m_num", [P, DV])
        dcol = put("m_dcol", [P, 8])
        bst = put("m_bst", [P, 8])
        mst = put("m_mst", [P, 4])
        c_at = [U_AT - 2 * 4 * S, U_AT - 4 * S]
        Msh = place("m_s_hi", [P, S], F32R, at=c_at[0])[0]
        Msl = place("m_s_lo", [P, S], F32R, at=c_at[1])[0]
        ab_at = U_AT - 4 * 4 * S
        t1 = place("m_t1", [P, DV], F32, at=ab_at)[0]
        hh = place("m_hh", [P, DV], F32, at=ab_at + 2048)[0]
        yy = place("m_y", [P, DV], F32, at=ab_at + 4096)[0]
        och = put("m_och", [P, VT, CHUNK])
        znc = put("m_znc", [P, VT, CHUNK])
        zsc = put("m_zsc", [P, VT, CHUNK])
        Sw = place("m_scores", [P, S], F32, at=U_AT)[0]
        put = area(C_AT, C_AT + 3 * 4 * KK * 514)
        gi = put("gi", [ROWS, P])
        gf = put("gf", [ROWS, P])
        ga = put("ga", [ROWS, P])
        gb = put("gb", [ROWS, P])
        gc_ = put("gc", [ROWS, P])
        gF = put("gF", [ROWS, P])
        gA = put("gA", [ROWS, P])
        gM = put("gM", [ROWS, P])
        gone = put("gone", [ROWS, P])
        gzero = put("gzero", [ROWS, P])
        g5 = put("g5", [ROWS, 5, P])
        gcol = put("gcol", [ROWS, 8])
        gdiag = put("gdiag", [ROWS, ROWS])
        sc4 = put("sc4", [M_HEADS, 3, NCH + 1])

        put = area(V_AT, end)
        G3h = put("g3_hi", [P, RT, S], F32R)
        G3l = put("g3_lo", [P, RT, S], F32R)
        XCh = put("xc_hi", [P, RT, S], F32R)
        XCl = put("xc_lo", [P, RT, S], F32R)
        R3 = put("lru_r", [P, RT, S])
        xc_at = V_AT + 2 * 4 * RT * S
        DEC = [C[:, :]] + [place("lru_a%d" % t, [P, S], F32, at=xc_at + 4 * t * S)[0][:, :] for t in range(2)]
        ROOT = [Dt[:, :]] + [place("lru_s%d" % t, [P, S], F32, at=xc_at + 4 * (RT + t) * S)[0][:, :]
                             for t in range(2)]
        Z3 = place("lru_z", [P, RT, S], F32, at=V_AT)[0]
        I3 = place("lru_i", [P, RT, S], F32, at=V_AT + 4 * RT * S)[0]


        PJ = ctx.enter_context(nc.psum_tensor("proj", [P, 2, 1024], F32))
        AX = ctx.enter_context(nc.psum_tensor("aux", [P, 2, 1024], F32))

        consts = sem("consts")
        consts_r = sem("consts_r")
        ident_loaded = sem("ident_loaded")
        w_loaded = [sem("w_loaded0"), sem("w_loaded1")]
        w_rounded = sem("w_rounded")
        w_split = [sem("w_split0"), sem("w_split1")]
        w_used = [sem("w_used0"), sem("w_used1")]
        pj_full = [sem("pj_full0"), sem("pj_full1")]
        pj_free = [sem("pj_free0"), sem("pj_free1")]
        ax_full = [sem("ax_full0"), sem("ax_full1")]
        ax_free = [sem("ax_free0"), sem("ax_free1")]
        xt_loaded = [sem("xt_loaded%d" % t) for t in range(4)]
        x_spilled = sem("x_spilled")
        x_back = [sem("x_back0"), sem("x_back1"), sem("x_back2")]
        out_stored = sem("out_stored")
        gain6_loaded = sem("gain6_loaded")
        r6_root = sem("r6_root")
        r6_ready = sem("r6_ready")
        sq_ready = sem("sq_ready")
        sq_used = sem("sq_used")
        sq_added = sem("sq_added")
        rstd_ready = sem("rstd_ready")
        y_ready = sem("y_ready")
        u_rounded = sem("u_rounded")
        u_ready = [sem("u_ready_dve"), sem("u_ready_pool")]
        g_rounded = sem("g_rounded")
        g_ready = sem("g_ready")
        x_scaled = sem("x_scaled")

        def use(phase, i, k):
            return slot_uses(UNIT0[phase], UNITS_OF[phase], i, k)

        def tile(phase, i, k):
            return slot_uses(PROJ0[phase], PROJ_OF[phase], i, k)

        def aux(phase, i, k):
            return slot_uses(AUX0[phase], AUX_OF[phase], i, k)

        NORMS = ["norm1", "norm2", "norm3", "norm4", "norm5", "norm6"]
        GAINS = dict(norm1="n1g", norm2="n2g", norm3="n3g", norm4="n4g", norm5="n5g")
        SOURCE = dict(norm1=("read", 0, 0), norm2=("conv_down", 0, 0), norm3=("ffn", FF_BLOCKS - 1, 4),
                      norm5=("mlstm", M_HEADS - 1, 8), norm6=("lru", R_PAIRS - 1, 12))
        UREADY = dict(norm1=0, norm2=8, norm4=16, norm5=24)
        PE_SUMS = {p: (1, 3, 5, 7) if p in ("norm1", "norm4") else (7,) for p in NORMS}

        def sums_before(phase, t, by_pe):
            n = 0
            for p in NORMS:
                for u in range(1, 7):
                    if p == phase and u >= t:
                        return n
                    n += (u in PE_SUMS[p]) == by_pe
                if p == phase:
                    return n

        POOL_SPLITS = (1, 3, 5)

        def u_split(phase, t):
            n = UREADY[phase] // KT
            if t in POOL_SPLITS:
                return u_ready[1], 3 * n + t // 2 + 1
            return u_ready[0], 5 * n + (5 if t == 7 else t // 2 + 1)

        GREADY = dict(ret=1, conv=5, ffn=9, lru=41)

        block = ctx.enter_context(nc.Block())

        w_in = d["w_in"].rearrange("(t p) n -> p t n", p=P)
        w_out = d["w_out"].rearrange("(t p) n -> p t n", p=P)
        w_up = d["w_up"].rearrange("(t p) n -> p t n", p=P)
        w_down = d["w_down"].rearrange("(t p) n -> p t n", p=P)
        m_in = d["m_w_in"].rearrange("(t p) n -> p t n", p=P)
        m_q = d["m_w_q"].rearrange("(t p) n -> p t n", p=P)
        m_k = d["m_w_k"].rearrange("(t p) n -> p t n", p=P)
        m_v = d["m_w_v"].rearrange("(t p) n -> p t n", p=P)
        m_out = d["m_w_out"].rearrange("(t p) n -> p t n", p=P)
        r_in = d["r_w_in"].rearrange("(t p) n -> p t n", p=P)
        r_out = d["r_w_out"].rearrange("(t p) n -> p t n", p=P)

        def sems(names):
            return {n: sem(n) for n in names.split()}

        r = sems("r_swapped r_sin r_rotated r_qhi r_qlo r_qx r_qxhi r_qxlo r_khi r_klo "
                 "r_kthi r_vthi r_smhi r_smlo r_state r_shi r_slo r_rstd r_y1 r_y")
        c = sems("c_pad c_taps c_sq c_rstd c_n")
        f_sq = sem("f_sq")
        m = sems("m_pad m_taps m_conv m_xc m_zn m_zs st_xm st_xc st_zn st_zs st_o "
                 "g_stored g_back ga_exp ga_abs ga_step ga_last ga_lastback ga_m ga_mback ga_rows ga_exps "
                 "ga_dl lam_abs lam_exp")
        h = sems("h_x0 h_x1 h_xround h_xsplit h_vhi h_qhi h_khi h_hc h_diag h_w "
                 "h_smhi h_smlo h_c h_chi h_clo0 h_clo1 h_den h_och h_znc h_zsc "
                 "h_s0 h_sw h_kt0hi h_kt1hi h_kt0lo h_kt1lo h_qc h_sv h_cu h_t1 h_num h_dsteps h_oT h_hh h_st "
                 "h_st2 h_std h_rs h_hn h_hnT "
                 "h_y1 h_y h_yhi h_done")
        l = sems("l_pad l_taps l_xc l_xchi l_xclo l_a l_th l_aa l_e l_sqrt l_x l_ix l_bt "
                 "l_h l_y")

        @block.sync
        def _(sp):
            for q in range(4):
                sp.dma_start(XT[:, 2 * q:2 * q + 2, :],
                             d["x"][2 * q * P:(2 * q + 2) * P, :].rearrange("(t p) n -> p t n", p=P)) \
                    .then_inc(xt_loaded[q], 16)

            def load(phase, i, k, src, width):
                n = use(phase, i, k)
                sp.wait_ge(w_split[k % 2], from1(n))
                dst = raw[:, k % 2, :].rearrange("p (t n) -> p t n", n=width)[:, 0:src.shape[1], 0:src.shape[2]]
                sp.dma_start(dst, src).then_inc(w_loaded[k % 2], 16)

            def load_down(phase, i, k0, w, row, tiles):
                for k in range(4):
                    load(phase, i, k0 + k, w[:, ds(row, tiles), k * 256:(k + 1) * 256], 256)

            with sp.Fori(0, RET_HEADS) as i:
                for k in range(4):
                    load("ret", i, k, w_in[:, :, ds(i * P + (RET_COL + k * 512), P)], P)
            last = RET_HEADS - 1
            sp.wait_ge(x_spilled, 16)
            sp.wait_ge(ax_full[0], aux("ret", last, 2) + 1)
            sp.dma_start(X[:, 0:2, :], x_kept[:, 0:2, :]).then_inc(x_back[0], 16)
            sp.wait_ge(ax_full[1], aux("ret", last, 3) + 1)
            sp.dma_start(X[:, 6:8, :], x_kept[:, 6:8, :]).then_inc(x_back[2], 16)
            down_columns = lambda k: w_out[:, 4:8, k * 256:(k + 1) * 256]
            for k in range(2):
                load("ret_down", 0, k, down_columns(k), 256)
            sp.wait_ge(ax_full[0], aux("ret", last, 4) + 1)
            sp.dma_start(X[:, 2:6, :], x_kept[:, 2:6, :]).then_inc(x_back[1], 16)
            for k in range(2, 4):
                load("ret_down", 0, k, down_columns(k), 256)
            with sp.Fori(1, 3) as i:
                for cc in range(2):
                    for k, col in enumerate((512, 1024, 0)):
                        load("conv", i - 1, cc * 3 + k, w_in[:, :, ds(i * 256 + (col + cc * P - 256), P)], P)
            load_down("conv_down", 0, 0, w_out, 0, 4)
            with sp.Fori(0, FF_BLOCKS) as i:
                for k in range(4):
                    load("ffn", i, k, w_up[:, :, ds(i * 512 + k * P, P)], P)
                load_down("ffn", i, 4, w_down, i * 4, 4)
            for k in range(2):
                load("gate", 0, k, m_in[:, 4 * k:4 * k + 4, 3 * M_INNER:3 * M_INNER + 2 * M_HEADS], P)
            with sp.Fori(0, MT // 2) as i:
                for jj in range(2):
                    for k in range(3):
                        load("inner", i, jj * 3 + k, m_in[:, :, ds(i * 256 + (k * M_INNER + jj * P), P)], P)

            def stage_x(i, kept, u0):
                for t in range(VT):
                    u = u0 + t
                    if u >= 2:
                        sp.wait_ge(h["h_xsplit"], 8 * i + (u - 1))
                    sp.dma_start((A, B)[t % 2][:, :], kept[ds(i * VT + t, 1), :, :].rearrange("a p s -> (a p) s")) \
                        .then_inc(h["h_x%d" % (t % 2)], 16)

            def stage_chunk(i, kept, dst, got, gone, n):
                sp.wait_ge(h[gone], from1(NCH * i + n))
                sp.dma_start(dst[:, :, :], kept[ds(i * VT, VT), :, n * CHUNK:(n + 1) * CHUNK]
                             .rearrange("t p s -> p t s")).then_inc(h[got], 16)

            def head(i, last):
                for k in range(2):
                    load("mlstm", i, k, m_v[:, ds(i * VT + 2 * k, 2), :], DV)
                stage_x(i, xc_kept, VT)
                load("mlstm", i, 2, m_q[:, ds(i * VT, VT), :], DK)
                load("mlstm", i, 3, m_k[:, ds(i * VT, VT), :], DK)
                for k in range(2):
                    load("mlstm", i, 4 + k, m_out[:, ds(i * VT, VT), k * 256:(k + 1) * 256], 256)
                for n in range(NCH + 1):
                    if n < NCH:
                        stage_chunk(i, o_kept, och, "h_och", "h_oT", n)
                    if n >= 1:
                        stage_chunk(i, zn_kept, znc, "h_znc", "h_y1", n - 1)
                        stage_chunk(i, zs_kept, zsc, "h_zsc", "h_y", n - 1)
                for k in range(2, 4):
                    load("mlstm", i, 4 + k, m_out[:, ds(i * VT, VT), k * 256:(k + 1) * 256], 256)
                if not last:
                    sp.wait_ge(h["h_done"], from1(NCH * i + NCH))
                    stage_x(i + 1, xm_kept, 0)

            for name in ("st_xm", "st_zn"):
                sp.wait_ge(m[name], from16(16 * MT))
            sp.wait_ge(m["m_conv"], from1(MT))
            stage_x(0, xm_kept, 0)
            for name in ("st_xc", "st_zs", "st_o"):
                sp.wait_ge(m[name], from16(16 * MT))
            with sp.Fori(0, M_HEADS - 1) as i:
                head(i, False)
            head(M_HEADS - 1, True)
            with sp.Fori(0, R_PAIRS) as i:
                for k in range(3):
                    load("lru", i, k, r_in[:, :, ds(i * 384 + k * P, P)], P)
                load("lru", i, 3, r_in[:, :, ds(i * 384 + R_WIDTH, P)], P)
                for k, w in ((4, d["gate_a"]), (5, d["gate_x"])):
                    load("lru", i, k, w[ds(i, 1), :, :].rearrange("a p (t n) -> (a p) t n", n=P), P)
                for k in range(1, 3):
                    load("lru", i, 5 + k, r_in[:, :, ds(i * 384 + (R_WIDTH + k * P), P)], P)
                load_down("lru", i, 8, r_out, i * RT, RT)
            sp.wait_ge(pj_full[1], tile("write", 0, 0))
            sp.dma_start(gain6[:, :], d["gain6"]).then_inc(gain6_loaded, 16)
            for t in range(8):
                sp.wait_ge(pj_free[t % 2], tile("write", 0, t) + 1)
                sp.dma_start(d["out"][t * P:(t + 1) * P, :], XT[:, t, :]).then_inc(out_stored, 16)
            sp.wait_ge(out_stored, 16 * 8)

        @block.gpsimd
        def _(pool):
            raise_starts(pool, "pool")
            pool.wait_ge(consts_r, 4)

            def split_unit(s, n):
                pool.wait_ge(w_loaded[s], 16 * n + 16)
                pool.wait_ge(w_used[s], n + 1)
                nc.gpsimd.tensor_tensor(wh[:, s, :], raw[:, s, :], zero[:, 0:1].broadcast_to([P, 1024]),
                                        ALU.add).then_inc(w_rounded, 1)
                pool.wait_ge(w_rounded, 2 * n + (s + 1))
                nc.gpsimd.tensor_tensor(wl[:, s, :], raw[:, s, :], wh[:, s, :].bitcast(F32),
                                        ALU.subtract).then_inc(w_split[s], 1)

            def norm(phase, unit=None, count=1):
                first = 8 * NORMS.index(phase)
                for t in range(1, 7):
                    if t not in PE_SUMS[phase]:
                        pool.wait_ge(sq_ready, first + t + 1)
                        nc.gpsimd.tensor_tensor(C[:, :], C[:, :], (A, B)[t % 2][:, :], ALU.add) \
                            .then_inc(sq_added, 1)
                        pool.wait_ge(sq_added, sums_before(phase, t + 1, False))
                if unit is not None:
                    for s in range(count):
                        split_unit(s, unit // 2)
                if phase in UREADY:
                    for t in POOL_SPLITS:
                        pool.wait_ge(u_rounded, UREADY[phase] + t + 1)
                        nc.gpsimd.tensor_tensor(Ul[:, t, :], (A, B, C)[t % 3][:, :], Uh[:, t, :].bitcast(F32),
                                                ALU.subtract).then_inc(u_ready[1], 1)

            def split_units(first, after):
                with pool.Fori(0, (after - first) // 2 - 1) as i:
                    split_unit(1, i + first // 2)
                    split_unit(0, i + (first // 2 + 1))
                split_unit(1, after // 2 - 1)

            norm("norm1", 0)
            split_units(0, UNIT0["norm2"])
            norm("norm2", UNIT0["ffn"])
            split_units(UNIT0["ffn"], UNIT0["norm3"])
            norm("norm3")
            norm("norm4", UNIT0["gate"], 2)
            with pool.Fori(UNIT0["inner"] // 2, UNIT0["mlstm"] // 2) as i:
                for s in range(2):
                    split_unit(s, i)
            with pool.Fori(0, M_HEADS) as i:
                for k in range(6):
                    split_unit(k % 2, use("mlstm", i, k))
                for hf in range(2):
                    tok = slice(hf * HALF, (hf + 1) * HALF)
                    pool.wait_ge(h["h_kt0hi"], 2 * i + (hf + 1))
                    nc.gpsimd.tensor_tensor(Mkl[:, 0, tok], A[:, tok], Mkh[:, 0, tok].bitcast(F32),
                                            ALU.subtract).then_inc(h["h_kt0lo"], 1)
                for step in range(NCH + 2):
                    if step < NCH:
                        pool.wait_ge(h["h_chi"], NCH * i + (step + 1))
                        nc.gpsimd.tensor_tensor(Cl[:, 1, :], Cf[:, 1, :], Ch[:, 1, :].bitcast(F32),
                                                ALU.subtract).then_inc(h["h_clo1"], 1)
                    if step < 2:
                        continue
                    n = step - 2
                    g = NCH * i + n
                    pool.wait_ge(h["h_y1"], from1(g + 1))
                    pool.wait_ge(h["h_zsc"], 16 * g + 16)
                    nc.gpsimd.tensor_tensor(yy[:, :], yy[:, :], zsc[:, :, :].rearrange("p t s -> p (t s)"),
                                            ALU.add).then_inc(h["h_y"], 1)
                    pool.wait_ge(h["h_yhi"], from1(g + 1))
                    nc.gpsimd.tensor_tensor(GXl[:, :, n * P:(n + 1) * P],
                                            yy[:, :].rearrange("p (t s) -> p t s", t=VT),
                                            GXh[:, :, n * P:(n + 1) * P].bitcast(F32),
                                            ALU.subtract).then_inc(h["h_done"], 1)
                for k in range(6, 8):
                    split_unit(k % 2, use("mlstm", i, k))
            norm("norm5", UNIT0["lru"])

            def pair(i, last):
                def gate_x(t):
                    pool.wait_ge(l["l_xclo"], from1(3 * i + 3))
                    pool.wait_ge(l["l_ix"], from1(3 * i + t))
                    nc.gpsimd.tensor_tensor(A[:, :], XCh[:, t, :].bitcast(F32), XCl[:, t, :].bitcast(F32),
                                            ALU.add).then_inc(l["l_x"], 1)
                    pool.wait_ge(l["l_x"], 3 * i + (t + 1))
                    pool.wait_ge(pj_free[(7 + t) % 2], tile("lru", i, 7 + t) + 1)
                    nc.gpsimd.tensor_tensor(I3[:, t, :], I3[:, t, :], A[:, :], ALU.mult).then_inc(l["l_ix"], 1)

                for k in range(1, 7):
                    split_unit(k % 2, use("lru", i, k))
                gate_x(0)
                gate_x(1)
                split_unit(1, use("lru", i, 7))
                gate_x(2)
                for k in range(8, 12):
                    split_unit(k % 2, use("lru", i, k))
                if not last:
                    split_unit(0, use("lru", i, 12))

            with pool.Fori(0, R_PAIRS - 1) as i:
                pair(i, False)
            pair(R_PAIRS - 1, True)
            norm("norm6")

        @block.tensor
        def _(pe):
            raise_starts(pe, "pe")
            mm = nc.tensor.matmul

            def mm3(out, lh, ll, rh, rl, start, stop, closes=None):
                first = mm(out, lh, rh, start=start, stop=False)
                if closes is not None:
                    first.then_inc(w_used[closes], 1)
                mm(out, lh, rl, start=False, stop=False)
                return mm(out, ll, rh, start=False, stop=stop)

            def start_unit(phase, i, k):
                pe.wait_ge(w_split[k % 2], from1(use(phase, i, k) + 1))

            def start_tile(phase, i, k):
                pe.wait_ge(pj_free[k % 2], tile(phase, i, k))

            def start_aux(phase, i, k):
                pe.wait_ge(ax_free[k % 2], aux(phase, i, k))

            def project(phase, i, k, p, xh, xl, kts, width, col, waits=None, closes=True, part=None):
                s = k % 2
                part = part or range(kts)
                if 0 in part:
                    start_tile(phase, i, p)
                for kt in part:
                    if waits is not None:
                        pe.wait_ge(*waits(kt))
                    at = kt * width + col
                    for j in range(2):
                        tok = slice(j * HALF, (j + 1) * HALF)
                        ins = mm3(PJ[:, p % 2, tok], wh[:, s, at:at + P], wl[:, s, at:at + P],
                                  xh[:, kt, tok], xl[:, kt, tok], kt == 0, kt == kts - 1,
                                  1 - s if closes and kt == 0 and j == 0 else None)
                if kts - 1 in part:
                    ins.then_inc(pj_full[p % 2], 1)

            def up(phase, i, k, p, waits=None):
                start_unit(phase, i, k)
                project(phase, i, k, p, Uh, Ul, KT, P, 0, waits)

            def down(phase, i, k0, p0, gh, gl, kts, ready=None, closes_first=True):
                s = k0 % 2
                start_unit(phase, i, k0)
                for kt in range(kts):
                    if ready is not None:
                        pe.wait_ge(g_ready, ready + kt + 1)
                    for j in range(2):
                        if kt == 0:
                            start_tile(phase, i, p0 + j)
                        for h2 in range(2):
                            tok = slice(h2 * HALF, (h2 + 1) * HALF)
                            at = kt * 256 + j * P
                            first = closes_first and kt == 0 and j == 0 and h2 == 0
                            ins = mm3(PJ[:, (p0 + j) % 2, tok], wh[:, s, at:at + P], wl[:, s, at:at + P],
                                      gh[:, kt, tok], gl[:, kt, tok], kt == 0, kt == kts - 1,
                                      1 - s if first else None)
                        if kt == kts - 1:
                            ins.then_inc(pj_full[(p0 + j) % 2], 1)
                down_rest(phase, i, k0, p0, gh, gl, kts)

            def down_rest(phase, i, k0, p0, gh, gl, kts):
                for k in range(1, 4):
                    start_unit(phase, i, k0 + k)
                    for j in range(2):
                        project(phase, i, k0 + k, p0 + 2 * k + j, gh, gl, kts, 256, j * P, closes=j == 0)

            def norm_sums(phase, closes=False):
                first = 8 * NORMS.index(phase)
                for j in range(2):
                    start_aux(phase, 0, j)
                own = PE_SUMS[phase]
                for t in own[:-1] + ("C",) + own[-1:]:
                    if t == "C":
                        pe.wait_ge(sq_added, sums_before(phase, 8, False))
                    else:
                        pe.wait_ge(sq_ready, first + t + 1)
                    for j in range(2):
                        ins = mm(AX[:, j, 0:HALF], ones[:, :], (C if t == "C" else B)[:, j * HALF:(j + 1) * HALF],
                                 start=t == (own[:-1] + ("C",))[0], stop=t == 7)
                        if closes and t == (own[:-1] + ("C",))[0] and j == 0:
                            ins.then_inc(w_used[1], 1)
                        if t == 7:
                            ins.then_inc(ax_full[j], 1)
                        elif j == 1 and t != "C":
                            ins.then_inc(sq_used, 1)

            u_wait = lambda phase: (lambda kt: u_split(phase, kt))

            pe.wait_ge(ident_loaded, 16)
            for t in range(8):
                pe.wait_ge(xt_loaded[t // 2], 16)
                start_tile("read", 0, t)
                for kt in range(KT):
                    ins = nc.tensor.transpose(PJ[:, t % 2, kt * P:(kt + 1) * P],
                                              XT[:, t, kt * P:(kt + 1) * P], ident[:, :])
                ins.then_inc(pj_full[t % 2], 1)
            pe.wait_ge(consts, CONSTS)
            pe.wait_ge(consts_r, 4)
            norm_sums("norm1")

            with pe.Fori(0, RET_HEADS) as i:
                up("ret", i, 0, 0, u_wait("norm1"))
                up("ret", i, 1, 1)
                up("ret", i, 2, 2)
                start_aux("ret", i, 0)
                pe.wait_ge(r["r_rotated"], 2 * i + 2)
                for n in range(NCH):
                    at = slice(n * P, (n + 1) * P)
                    ins = nc.tensor.transpose(AX[:, 0, at], B[:, at], ident[:, :])
                ins.then_inc(ax_full[0], 1)
                start_aux("ret", i, 1)
                pe.wait_ge(pj_free[0], tile("ret", i, 2) + 1)
                for n in range(NCH):
                    at = slice(n * P, (n + 1) * P)
                    ins = nc.tensor.transpose(AX[:, 1, at], C[:, at], ident[:, :])
                ins.then_inc(ax_full[1], 1)
                start_unit("ret", i, 3)
                project("ret", i, 3, 3, Uh, Ul, KT, P, 0, part=range(2))
                start_aux("ret", i, 2)
                pe.wait_ge(r["r_qlo"], i + 1)
                pe.wait_ge(r["r_klo"], i + 1)
                for n in range(NCH):
                    at = slice(n * P, (n + 1) * P)
                    ins = mm3(AX[:, 0, at], Kh[:, at], Kl[:, at], Qh[:, at], Ql[:, at], True, True)
                ins.then_inc(ax_full[0], 1)
                start_aux("ret", i, 3)
                pe.wait_ge(ax_free[0], aux("ret", i, 0) + 1)
                for n in range(NCH):
                    at = slice(n * P, (n + 1) * P)
                    ins = mm3(AX[:, 1, at], Kth[:, at], Ktl[:, at], Vth[:, at], Vtl[:, at], True, True)
                ins.then_inc(ax_full[1], 1)
                project("ret", i, 3, 3, Uh, Ul, KT, P, 0, part=range(2, 7))
                start_aux("ret", i, 4)
                pe.wait_ge(r["r_smlo"], i + 1)
                pe.wait_ge(r["r_slo"], i + 1)
                pe.wait_ge(r["r_qxlo"], i + 1)
                for n in range(NCH):
                    at = slice(n * P, (n + 1) * P)
                    mm3(AX[:, 0, at], Vth[:, at], Vtl[:, at], SMh[:, at], SMl[:, at], True, False)
                    ins = mm3(AX[:, 0, at], Kh[:, at], Kl[:, at], QXh[:, at], QXl[:, at], False, True)
                ins.then_inc(ax_full[0], 1)
                project("ret", i, 3, 3, Uh, Ul, KT, P, 0, part=range(7, KT))
                start_aux("ret", i, 5)
                pe.wait_ge(ax_free[0], aux("ret", i, 4) + 1)
                for j in range(2):
                    ins = mm(AX[:, 1, j * HALF:(j + 1) * HALF], ones[:, :], A[:, j * HALF:(j + 1) * HALF],
                             start=True, stop=True)
                ins.then_inc(ax_full[1], 1)
            down("ret_down", 0, 0, 0, Gh, Gl, 4, GREADY["ret"])

            with pe.Fori(0, 2) as i:
                for cc in range(2):
                    for k in range(3):
                        up("conv", i, 3 * cc + k, 3 * cc + k)
                    start_aux("conv", i, cc)
                    pe.wait_ge(c["c_sq"], 2 * i + cc + 1)
                    for j in range(2):
                        ins = mm(AX[:, cc, j * HALF:(j + 1) * HALF], group64[:, :],
                                 B[:, j * HALF:(j + 1) * HALF], start=True, stop=True)
                    ins.then_inc(ax_full[cc], 1)
            down("conv_down", 0, 0, 0, Gh, Gl, 4, GREADY["conv"])
            norm_sums("norm2")

            with pe.Fori(0, FF_BLOCKS) as i:
                for k in range(4):
                    up("ffn", i, k, k, u_wait("norm2") if k == 0 else None)
                down("ffn", i, 4, 4, Gh, Gl, 4, GREADY["ffn"] + 4 * i)
            norm_sums("norm3", closes=True)
            norm_sums("norm4")

            for j in range(2):
                start_tile("gate", 0, j)
            for k in range(2):
                start_unit("gate", 0, k)
                for q in range(4):
                    kt = 4 * k + q
                    pe.wait_ge(*u_wait("norm4")(kt))
                    for j in range(2):
                        tok = slice(j * HALF, (j + 1) * HALF)
                        ins = mm3(PJ[:, j, 0:HALF], wh[:, k, q * P:(q + 1) * P], wl[:, k, q * P:(q + 1) * P],
                                  Uh[:, kt, tok], Ul[:, kt, tok], kt == 0, kt == KT - 1,
                                  0 if k == 1 and q == 0 and j == 0 else None)
                        if kt == KT - 1:
                            ins.then_inc(pj_full[j], 1)
            with pe.Fori(0, MT // 2) as i:
                for k in range(6):
                    up("inner", i, k, k)
            start_aux("gate", 0, 0)
            pe.wait_ge(m["ga_rows"], 2)
            pe.wait_ge(m["ga_exps"], 3)
            for q in range(5):
                ins = nc.tensor.transpose(AX[:, 0, q * ROWS:(q + 1) * ROWS], g5[:, q, :], ident[0:ROWS, 0:ROWS])
            ins.then_inc(ax_full[0], 1)
            start_aux("gate", 0, 1)
            pe.wait_ge(m["ga_dl"], 1)
            mm(AX[:, 1, 0:ROWS], ones[0:ROWS, :], gdiag[:, :], start=True, stop=True).then_inc(ax_full[1], 1)

            def head(i):
                for p0 in (0, 2):
                    for k in range(2):
                        if p0 == 0:
                            start_unit("mlstm", i, k)
                        for p in (p0, p0 + 1):
                            if k == 0:
                                start_tile("mlstm", i, p)
                            for j in range(2):
                                at = slice((2 * p + j) * P, (2 * p + j + 1) * P)
                                for kt in (2 * k, 2 * k + 1):
                                    w = slice((kt % 2) * DV, (kt % 2 + 1) * DV)
                                    if p == 0 and j == 0:
                                        pe.wait_ge(h["h_xsplit"], 8 * i + (kt + 1))
                                    first = p == p0 and j == 0 and kt == 2 * k
                                    closes = {(0, 0): 1, (2, 1): 0}.get((p0, k)) if first else None
                                    ins = mm3(PJ[:, p % 2, j * HALF:(j + 1) * HALF], XMh[:, kt, at],
                                              XMl[:, kt, at], wh[:, k, w], wl[:, k, w],
                                              kt == 0, kt == VT - 1, closes)
                            if k == 1:
                                ins.then_inc(pj_full[p % 2], 1)
                pe.wait_ge(h["h_xsplit"], 8 * i + 8)
                for k in range(2):
                    start_unit("mlstm", i, 2 + k)
                    for j in range(2):
                        project("mlstm", i, 2 + k, 4 + 2 * k + j, GXh, GXl, VT, DK, j * P, closes=j == 0)
                start_aux("mlstm", i, 0)
                pe.wait_ge(h["h_diag"], i + 1)
                for j in range(2):
                    tok = slice(j * HALF, (j + 1) * HALF)
                    mm(AX[:, 0, tok], ones[:, :], Dt[:, tok], start=True, stop=False)
                    ins = mm(AX[:, 0, tok], ident[:, :], negmask[:, :].unsqueeze(1).broadcast_to([P, 4, P]),
                             start=False, stop=True)
                ins.then_inc(ax_full[0], 1)
                for kk in range(KK):
                    pe.wait_ge(ax_free[1 - kk], aux("mlstm", i, 1 + kk))
                    pe.wait_ge(pj_free[kk], tile("mlstm", i, 6 + kk) + 1)
                    for n in range(NCH):
                        at = slice(n * P, (n + 1) * P)
                        ins = mm(AX[:, 1 - kk, at], Mkh[:, kk, at], identr[:, :], start=True, stop=False)
                        if kk == 0 and n == 0:
                            ins.then_inc(w_used[1], 1)
                        ins = mm(AX[:, 1 - kk, at], Mkl[:, kk, at], identr[:, :], start=False, stop=True)
                    ins.then_inc(ax_full[1 - kk], 1)
                start_aux("mlstm", i, 3)
                for n in range(NCH):
                    at = slice(n * P, (n + 1) * P)
                    for kk in range(KK):
                        ins = mm3(AX[:, 1, at], Mkh[:, kk, at], Mkl[:, kk, at], Mqh[:, kk, at], Mql[:, kk, at],
                                  kk == 0, kk == KK - 1)
                    if n == 3:
                        ins.then_inc(h["h_s0"], 1)
                ins.then_inc(ax_full[1], 1)
                for s in range(2):
                    pe.wait_ge(pj_free[s], tile("mlstm", i, 6 + s) + 1)
                    if s == 0:
                        pe.wait_ge(ax_free[0], aux("mlstm", i, 2) + 1)
                for step in range(NCH + 1):
                    if step < NCH:
                        n = step
                        g = NCH * i + n
                        at = slice(n * P, (n + 1) * P)
                        if n % 4 == 0:
                            for name in ("h_smlo", "h_kt0lo", "h_kt1lo"):
                                pe.wait_ge(h[name], 2 * i + (n // 4 + 1))
                        if n < NCH - 1:
                            pe.wait_ge(h["h_c"], g + 1)
                            for kk in range(KK):
                                mm3(AX[:, 0, kk * DV:(kk + 1) * DV], Mkh[:, kk, at], Mkl[:, kk, at],
                                    Vh[:, n, :], Vl[:, n, :], True, True)
                            if n == 0:
                                pe.wait_ge(ax_free[1], aux("mlstm", i, 3) + 1)
                            for kk in range(KK):
                                add = AX[:, 1, HALF + 2 * kk:HALF + 2 * kk + 2]
                                mm(add, Mkh[:, kk, at], onesr[:, 0:2], start=True, stop=False)
                                ins = mm(add, Mkl[:, kk, at], onesr[:, 0:2], start=False, stop=True)
                            ins.then_inc(h["h_cu"], 1)
                        pe.wait_ge(h["h_och"], 16 * (g + 1))
                        pe.wait_ge(h["h_hh"], from1(g))
                        for t in range(VT):
                            ins = nc.tensor.transpose(PJ[:, 1, t * P:(t + 1) * P], och[:, t, :], ident[:, :])
                        ins.then_inc(h["h_oT"], 1)
                        pe.wait_ge(h["h_num"], from1(g))
                        mm3(PJ[:, 0, DV:2 * DV], Msh[:, at], Msl[:, at], Vh[:, n, :], Vl[:, n, :], True, True) \
                            .then_inc(h["h_sv"], 1)
                        pe.wait_ge(h["h_clo0"], g + 1)
                        pe.wait_ge(h["h_clo1"], g + 1)
                        pe.wait_ge(h["h_t1"], from1(g))
                        pe.wait_ge(h["h_den"], from1(g))
                        for kk in range(KK):
                            mm3(PJ[:, 0, 0:DV], Mqh[:, kk, at], Mql[:, kk, at], Ch[:, kk, 0:DV],
                                Cl[:, kk, 0:DV], kk == 0, kk == KK - 1)
                        for kk in range(KK):
                            mm3(AX[:, 1, 0:2], Mqh[:, kk, at], Mql[:, kk, at], Ch[:, kk, DV:DV + 2],
                                Cl[:, kk, DV:DV + 2], kk == 0, kk == KK - 1)
                        mm(AX[:, 1, 2:4], Msh[:, at], onesr[:, 0:2], start=True, stop=False)
                        mm(AX[:, 1, 2:4], Msl[:, at], onesr[:, 0:2], start=False, stop=True) \
                            .then_inc(h["h_qc"], 1)
                    if step >= 1:
                        g = NCH * i + (step - 1)
                        pe.wait_ge(h["h_hn"], g + 1)
                        pe.wait_ge(h["h_y1"], from1(g))
                        for t in range(VT):
                            ins = nc.tensor.transpose(PJ[:, 1, HALF + t * P:HALF + (t + 1) * P],
                                                      hh[:, t * P:(t + 1) * P], ident[:, :])
                        ins.then_inc(h["h_hnT"], 1)
                last = NCH * i + NCH
                start_unit("mlstm", i, 4)
                for h2 in range(2):
                    tok = slice(h2 * HALF, (h2 + 1) * HALF)
                    pe.wait_ge(h["h_done"], from1(last - 4 + 4 * h2))
                    for j in range(2):
                        if h2 == 0:
                            pe.wait_ge(h[("h_t1", "h_hh")[j]], from1(last))
                        for kt in range(VT):
                            at = kt * 256 + j * P
                            ins = mm3(PJ[:, j, tok], wh[:, 0, at:at + P], wl[:, 0, at:at + P],
                                      GXh[:, kt, tok], GXl[:, kt, tok], kt == 0, kt == VT - 1)
                        if h2 == 1:
                            ins.then_inc(pj_full[j], 1)
                down_rest("mlstm", i, 4, 8, GXh, GXl, VT)

            with pe.Fori(0, M_HEADS) as i:
                head(i)
            norm_sums("norm5")

            with pe.Fori(0, R_PAIRS) as i:
                for k in range(3):
                    up("lru", i, k, k, u_wait("norm5") if k == 0 else None)
                up("lru", i, 3, 3)
                pe.wait_ge(l["l_xclo"], from1(3 * i + 3))
                for k in range(2):
                    s = k
                    start_unit("lru", i, 4 + k)
                    for t in range(RT):
                        qs = [q for q, (_, b) in enumerate(GATE_TILES) if b == t]
                        p = 4 + 3 * k + t
                        start_tile("lru", i, p)
                        for q in qs:
                            for j in range(2):
                                tok = slice(j * HALF, (j + 1) * HALF)
                                ins = mm3(PJ[:, p % 2, tok], wh[:, s, q * P:(q + 1) * P],
                                          wl[:, s, q * P:(q + 1) * P], XCh[:, GATE_TILES[q][0], tok],
                                          XCl[:, GATE_TILES[q][0], tok], q == qs[0], q == qs[-1],
                                          1 - s if t == 0 and q == qs[0] and j == 0 else None)
                        ins.then_inc(pj_full[p % 2], 1)
                for k in range(1, 3):
                    up("lru", i, 5 + k, 9 + k)
                down("lru", i, 8, 12, G3h, G3l, RT, GREADY["lru"] + 3 * i)
            def turn(t):
                start_tile("write", 0, t)
                for kt in range(KT):
                    ins = nc.tensor.transpose(PJ[:, t % 2, kt * P:(kt + 1) * P], X[:, kt, t * P:(t + 1) * P],
                                              ident[:, :])
                ins.then_inc(pj_full[t % 2], 1)

            for s in range(2):
                pe.wait_ge(pj_free[s], tile("write", 0, 0))
            for t in range(2):
                turn(t)
            start_aux("norm6", 0, 0)
            pe.wait_ge(sq_added, sums_before("norm6", 8, False))
            pe.wait_ge(sq_ready, 8 * NORMS.index("norm6") + 8)
            for t in range(8):
                tok = slice(t * P, (t + 1) * P)
                mm(AX[:, 0, 2 * t:2 * t + 2], C[:, tok], ones[:, 0:2], start=True, stop=False)
                ins = mm(AX[:, 0, 2 * t:2 * t + 2], B[:, tok], ones[:, 0:2], start=False, stop=True)
            ins.then_inc(ax_full[0], 1)
            for t in range(2, 8):
                turn(t)

        @block.scalar
        def _(act):
            raise_starts(act, "act")
            def fn(out, in_, func, scale=1.0, bias=0.0):
                return nc.scalar.activation(out, in_, func, bias=bias, scale=scale)

            def norm(phase):
                first = 8 * NORMS.index(phase)
                for t in range(KT):
                    if phase == "norm4":
                        act.wait_ge(x_scaled, t + 1)
                    elif phase == "norm1":
                        for s in range(2):
                            act.wait_ge(pj_free[s], tile("read", 0, 6) + 1)
                    else:
                        ph, i, p = SOURCE[phase]
                        act.wait_ge(pj_free[t % 2], tile(ph, i, p + t) + 1)
                    if t >= 3:
                        by_pe = t - 2 in PE_SUMS[phase]
                        act.wait_ge(sq_used if by_pe else sq_added, sums_before(phase, t - 1, by_pe))
                    fn((A, B)[t % 2][:, :] if t else C[:, :], X[:, t, :], ACT.Square).then_inc(sq_ready, 1)
                if phase == "norm6":
                    act.wait_ge(ax_full[0], aux(phase, 0, 0) + 1)
                    act.wait_ge(pj_full[1], tile("write", 0, 0))
                    fn(rcol[:, 0, :], AX[:, 0, 0:2 * (S // P)], ACT.Sqrt, 1.0 / D, eps[:, 0:1]) \
                        .then_inc(r6_root, 1)
                    return
                for j in range(2):
                    at = slice(j * HALF, (j + 1) * HALF)
                    act.wait_ge(ax_full[j], aux(phase, 0, j) + 1)
                    fn(C[:, at], AX[:, j, 0:HALF], ACT.Ln, 1.0 / D, eps[:, 0:1]).then_inc(ax_free[j], 1)
                for j in range(2):
                    at = slice(j * HALF, (j + 1) * HALF)
                    act.wait_ge(ax_free[j], aux(phase, 0, j) + 1)
                    fn(Dt[:, at], C[:, at], ACT.Exp, -0.5).then_inc(rstd_ready, 1)
                if phase in UREADY:
                    for t in range(KT):
                        act.wait_ge(y_ready, UREADY[phase] + t + 1)
                        fn(Uh[:, t, :], (A, B, C)[t % 3][:, :], ACT.Copy).then_inc(u_rounded, 1)

            for dst, name in ((ident, "ident"), (ones, "ones"), (group64, "group64"), (vec, "vec"),
                              (mbif, "mbif"), (cos, "cos"), (sin, "sin"), (decay, "decay"), (xi, "xi")):
                act.dma_start(dst[tuple(slice(None) for _ in dst.shape)], d[name]) \
                    .then_inc(ident_loaded if name == "ident" else consts, 16)
            for s in range(2):
                act.wait_ge(pj_free[s], tile("read", 0, 6) + 1)
            act.dma_start(x_kept, X[:, :, :]).then_inc(x_spilled, 16)
            act.wait_ge(consts, CONSTS)
            act.wait_ge(consts_r, 4)
            norm("norm1")

            act.wait_ge(x_spilled, 16)
            for t in (5, 7):
                act.wait_ge(*u_split("norm1", t))
            with act.Fori(0, RET_HEADS) as i:
                for q in range(2):
                    act.wait_ge(pj_full[q], tile("ret", i, q) + 1)
                    if q:
                        act.wait_ge(r["r_qxlo"], i + 1)
                    fn(A[64:128, :], PJ[0:64, q, :], ACT.Copy)
                    fn(A[0:64, :], PJ[64:128, q, :], ACT.Copy).then_inc(r["r_swapped"], 1)
                    act.wait_ge(r["r_rotated"], 2 * i + (q + 1))
                    if q == 0:
                        fn(Qh[:, :], B[:, :], ACT.Copy).then_inc(r["r_qhi"], 1)
                        act.wait_ge(r["r_qx"], i + 1)
                        fn(QXh[:, :], A[:, :], ACT.Copy).then_inc(r["r_qxhi"], 1)
                    else:
                        fn(Kh[:, :], B[:, :], ACT.Copy).then_inc(r["r_khi"], 1)
                act.wait_ge(pj_full[0], tile("ret", i, 2) + 1)
                act.wait_ge(g_ready, GREADY["ret"] + i)
                fn(C[:, :], PJ[:, 0, :], ACT.Copy).then_inc(pj_free[0], 1)
                act.wait_ge(ax_full[0], aux("ret", i, 0) + 1)
                fn(Kth[:, :], AX[:, 0, :], ACT.Copy, v("zeta", i)).then_inc(r["r_kthi"], 1)
                act.wait_ge(ax_full[1], aux("ret", i, 1) + 1)
                fn(Vth[:, :], AX[:, 1, :], ACT.Copy).then_inc(r["r_vthi"], 1)
                act.wait_ge(ax_free[0], aux("ret", i, 2) + 1)
                fn(SMh[:, :], A[:, :], ACT.Copy).then_inc(r["r_smhi"], 1)
                act.wait_ge(ax_free[1], aux("ret", i, 3) + 1)
                fn(Kh[:, :], B[:, :], ACT.Copy).then_inc(r["r_shi"], 1)
                act.wait_ge(ax_full[0], aux("ret", i, 4) + 1)
                fn(C[:, :], AX[:, 0, :], ACT.Copy)
                act.wait_ge(r["r_smlo"], i + 1)
                fn(A[:, :], AX[:, 0, :], ACT.Square).then_inc(ax_free[0], 1)
                act.wait_ge(pj_full[1], tile("ret", i, 3) + 1)
                fn(Dt[:, :], PJ[:, 1, :], ACT.Silu).then_inc(pj_free[1], 1)
                act.wait_ge(ax_full[1], aux("ret", i, 5) + 1)
                act.wait_ge(r["r_slo"], i + 1)
                fn(B[:, :], AX[:, 1, :], ACT.Ln, 1.0 / P, eps[:, 0:1]).then_inc(ax_free[1], 1)
                act.wait_ge(ax_free[1], aux("ret", i, 5) + 1)
                fn(B[:, :], B[:, :], ACT.Exp, -0.5).then_inc(r["r_rstd"], 1)
                act.wait_ge(r["r_y"], i + 1)
                fn(Gh[:, ds(i, 1), :].rearrange("p a s -> p (a s)"), C[:, :], ACT.Copy).then_inc(g_rounded, 1)

            with act.Fori(0, 2) as i:
                for cc in range(2):
                    p = 3 * cc
                    act.wait_ge(pj_full[p % 2], tile("conv", i, p) + 1)
                    act.wait_ge(c["c_n"], from1(2 * i + cc))
                    fn(B[:, :], PJ[:, p % 2, :], ACT.Copy).then_inc(pj_free[p % 2], 1)
                    p = 3 * cc + 2
                    act.wait_ge(pj_free[p % 2], tile("conv", i, p) + 1)
                    fn(B[:, :], Dt[:, :], ACT.Square).then_inc(c["c_sq"], 1)
                    act.wait_ge(ax_full[cc], aux("conv", i, cc) + 1)
                    fn(B[:, :], AX[:, cc, :], ACT.Ln, 1.0 / 64, eps[:, 0:1]).then_inc(ax_free[cc], 1)
                    act.wait_ge(ax_free[cc], aux("conv", i, cc) + 1)
                    fn(B[:, :], B[:, :], ACT.Exp, -0.5).then_inc(c["c_rstd"], 1)
                    act.wait_ge(pj_full[1], tile("conv", i, 0))
                    act.wait_ge(c["c_n"], from1(2 * i + (cc + 1)))
                    fn(Gh[:, ds(2 * i + cc, 1), :].rearrange("p a s -> p (a s)"), Dt[:, :], ACT.Copy) \
                        .then_inc(g_rounded, 1)
            norm("norm2")

            with act.Fori(0, FF_BLOCKS) as i:
                def split(k):
                    act.wait_ge(f_sq, 4 * i + (k + 1))
                    fn(Gh[:, k, :], (A, B)[k % 2][:, :], ACT.Copy).then_inc(g_rounded, 1)

                for k in range(4):
                    act.wait_ge(pj_full[k % 2], tile("ffn", i, k) + 1)
                    act.wait_ge(g_ready, 4 * i + (GREADY["ffn"] + k - 1))
                    fn((A, B)[k % 2][:, :], PJ[:, k % 2, :], ACT.Relu).then_inc(pj_free[k % 2], 1)
                    if k == 0:
                        act.wait_ge(pj_full[1], tile("ffn", i, 0))
                    if k >= 1:
                        split(k - 1)
                split(3)
            norm("norm3")
            norm("norm4")

            for k in range(2):
                act.wait_ge(pj_full[k], tile("gate", 0, k) + 1)
                fn(GR[:, k * HALF:(k + 1) * HALF], PJ[0:2 * M_HEADS, k, 0:HALF], ACT.Identity, 1.0, mbif[:, :]) \
                    .then_inc(pj_free[k], 1)
            for k in range(2):
                act.wait_ge(pj_free[k], tile("gate", 0, k) + 1)
            act.dma_start(gate_kept.rearrange("g h s -> (g h) s"), GR[:, :]).then_inc(m["g_stored"], 16)
            act.wait_ge(m["g_stored"], 16)
            act.dma_start(gi[:, :], gate_kept[0].rearrange("h (c t) -> (h c) t", t=CHUNK)).then_inc(m["g_back"], 16)
            act.dma_start(gf[:, :], gate_kept[1].rearrange("h (c t) -> (h c) t", t=CHUNK)).then_inc(m["g_back"], 16)
            act.dma_start(negmask[:, :], d["negmask"]).then_inc(m["g_back"], 16)
            act.wait_ge(m["g_back"], 48)
            fn(ga[:, :], gf[:, :], ACT.Abs).then_inc(m["ga_abs"], 1)
            fn(ltmp[:, 0, :], v("lam", 0, R_TILES), ACT.Abs).then_inc(m["lam_abs"], 1)
            act.wait_ge(m["ga_abs"], 1)
            fn(ga[:, :], ga[:, :], ACT.Exp, -1.0).then_inc(m["ga_exp"], 1)
            act.wait_ge(m["lam_abs"], 1)
            fn(ltmp[:, 0, :], ltmp[:, 0, :], ACT.Exp, -1.0).then_inc(m["lam_exp"], 1)
            act.wait_ge(m["ga_last"], 2)
            for k in range(2):
                act.dma_start(last_kept[k].rearrange("(r a) -> r a", a=1), gcol[:, k:k + 1]) \
                    .then_inc(m["ga_lastback"], 16)
            act.wait_ge(m["ga_lastback"], 32)
            act.dma_start(sc4[:, 0:2, 0:NCH], last_kept[0:2].rearrange("k (h c) -> h k c", c=NCH)) \
                .then_inc(m["ga_lastback"], 16)
            with act.Fori(0, MT // 2) as i:
                for jj in range(2):
                    j = 2 * i + jj
                    p = 3 * jj
                    s = p % 2
                    act.wait_ge(pj_full[s], tile("inner", i, p) + 1)
                    act.wait_ge(m["st_xm"], from16(32 * i + 16 * jj))
                    act.wait_ge(m["m_conv"], from1(2 * i + jj))
                    fn(A[:, :], PJ[:, s, :], ACT.Copy).then_inc(pj_free[s], 1)
                    act.wait_ge(pj_free[s], tile("inner", i, p) + 1)
                    act.dma_start(xm_kept[ds(j, 1), :, :].rearrange("a p s -> (a p) s"), A[:, :]) \
                        .then_inc(m["st_xm"], 16)
                    act.wait_ge(m["m_conv"], from1(2 * i + (jj + 1)))
                    act.wait_ge(m["st_xc"], from16(32 * i + 16 * jj))
                    act.wait_ge(m["m_zs"], from1(2 * i + jj))
                    fn(Fx[:, :], E[:, :], ACT.Silu).then_inc(m["m_xc"], 1)
                    act.wait_ge(m["m_xc"], from1(2 * i + (jj + 1)))
                    act.dma_start(xc_kept[ds(j, 1), :, :].rearrange("a p s -> (a p) s"), Fx[:, :]) \
                        .then_inc(m["st_xc"], 16)
                    s = 1 - s
                    act.wait_ge(pj_full[s], tile("inner", i, p + 1) + 1)
                    act.wait_ge(m["m_zn"], from1(2 * i + jj))
                    fn(H[:, :], PJ[:, s, :], ACT.Silu).then_inc(pj_free[s], 1)
                    act.wait_ge(m["m_zs"], from1(2 * i + (jj + 1)))
                    act.dma_start(zs_kept[ds(j, 1), :, :].rearrange("a p s -> (a p) s"), Q[:, :]) \
                        .then_inc(m["st_zs"], 16)
                    act.wait_ge(m["m_zn"], from1(2 * i + (jj + 1)))
                    act.dma_start(zn_kept[ds(j, 1), :, :].rearrange("a p s -> (a p) s"), B[:, :]) \
                        .then_inc(m["st_zn"], 16)
                    s = 1 - s
                    act.wait_ge(pj_full[s], tile("inner", i, p + 2) + 1)
                    act.wait_ge(m["st_o"], from16(32 * i + 16 * jj))
                    fn(O[:, :], PJ[:, s, :], ACT.Sigmoid).then_inc(pj_free[s], 1)
                    act.wait_ge(pj_free[s], tile("inner", i, p + 2) + 1)
                    act.dma_start(o_kept[ds(j, 1), :, :].rearrange("a p s -> (a p) s"), O[:, :]) \
                        .then_inc(m["st_o"], 16)


            def stage(i, u):
                act.wait_ge(h["h_x%d" % (u % 2)], 64 * i + 16 * (u // 2 + 1))
                fn((XMh, GXh)[u // VT][:, u % VT, :], (A, B)[u % 2][:, :], ACT.Copy).then_inc(h["h_xround"], 1)

            def head(i, last):
                act.wait_ge(pj_full[1], tile("mlstm", i, 0))
                stage(i, 4)
                stage(i, 5)
                for p in range(4):
                    act.wait_ge(pj_full[p % 2], tile("mlstm", i, p) + 1)
                    fn(Vh[:, 2 * p:2 * p + 2, :].rearrange("p a s -> p (a s)"), PJ[:, p % 2, :], ACT.Copy) \
                        .then_inc(h["h_vhi"], 1)
                    if p < 2:
                        stage(i, 6 + p)
                for kk in range(KK):
                    act.wait_ge(pj_full[kk], tile("mlstm", i, 4 + kk) + 1)
                    fn(Mqh[:, kk, :], PJ[:, kk, :], ACT.Copy, DK ** -0.5).then_inc(h["h_qhi"], 1)
                for kk in range(KK):
                    act.wait_ge(pj_full[kk], tile("mlstm", i, 6 + kk) + 1)
                    fn(Mkh[:, kk, :], PJ[:, kk, :], ACT.Copy).then_inc(h["h_khi"], 1)
                act.wait_ge(ax_free[0], aux("mlstm", i, 0) + 1)
                fn(Dt[:, :], Dt[:, :], ACT.Exp).then_inc(h["h_w"], 1)
                for hf in range(2):
                    tok = slice(hf * HALF, (hf + 1) * HALF)
                    if hf == 0:
                        act.wait_ge(h["h_s0"], i + 1)
                    else:
                        act.wait_ge(ax_full[1], aux("mlstm", i, 3) + 1)
                    for kk in range(KK):
                        act.wait_ge(ax_free[1 - kk], aux("mlstm", i, 1 + kk) + 1)
                        fn(Mkh[:, kk, tok], (A, B)[kk][:, tok], ACT.Copy).then_inc(h["h_kt%dhi" % kk], 1)
                    if hf == 0:
                        act.wait_ge(h["h_sw"], i + 1)
                    else:
                        act.wait_ge(ax_free[1], aux("mlstm", i, 3) + 1)
                    fn(Msh[:, tok], Sw[:, tok], ACT.Copy).then_inc(h["h_smhi"], 1)
                for step in range(NCH + 2):
                    if step < NCH:
                        g = NCH * i + step
                        act.wait_ge(h["h_c"], g + 1)
                        act.wait_ge(h["h_qc"], from1(g))
                        fn(Ch[:, :, :], Cf[:, :, :], ACT.Copy).then_inc(h["h_chi"], 1)
                    if 1 <= step <= NCH:
                        act.wait_ge(h["h_st2"], NCH * i + step)
                        fn(mst[:, 2:3], mst[:, 1:2], ACT.Sqrt, 1.0, eps[:, 0:1]).then_inc(h["h_std"], 1)
                    if step < NCH:
                        act.wait_ge(h["h_qc"], from1(g + 1))
                        act.wait_ge(h["h_num"], from1(g))
                        if step == 0:
                            for kk in range(KK):
                                act.wait_ge(h["h_kt%dlo" % kk], 2 * i + 2)
                        fn(t1[:, :], PJ[:, 0, 0:DV], ACT.Copy, hc[:, 2, step:step + 1]).then_inc(h["h_t1"], 1)
                    if step >= 2:
                        n = step - 2
                        act.wait_ge(h["h_y"], from1(NCH * i + (n + 1)))
                        fn(GXh[:, :, n * P:(n + 1) * P], yy[:, :].rearrange("p (t s) -> p t s", t=VT),
                           ACT.Copy).then_inc(h["h_yhi"], 1)
                if not last:
                    for u in range(4):
                        stage(i + 1, u)

            act.wait_ge(m["ga_m"], 2)
            act.dma_start(last_kept[2].rearrange("(h c) -> h c", c=NCH), sc4[:, 2, 0:NCH]).then_inc(m["ga_mback"], 16)
            stage(0, 0)
            act.wait_ge(m["ga_mback"], 16)
            act.dma_start(gcol[:, 2:3], last_kept[2].rearrange("(r a) -> r a", a=1)).then_inc(m["ga_mback"], 16)
            for u in range(1, 4):
                stage(0, u)
            act.wait_ge(m["ga_rows"], 2)
            fn(g5[:, 2, :], g5[:, 1, :], ACT.Exp, 1.0, gcol[:, 2:3]).then_inc(m["ga_exps"], 1)
            fn(g5[:, 3, :], gb[:, :], ACT.Exp, -1.0).then_inc(m["ga_exps"], 1)
            fn(g5[:, 4, :], g5[:, 0, :], ACT.Exp, 1.0, gcol[:, 3:4]).then_inc(m["ga_exps"], 1)
            act.wait_ge(ax_full[0], aux("gate", 0, 0) + 1)
            fn(cols[:, :, :].rearrange("p q r -> p (q r)"), AX[:, 0, 0:5 * ROWS], ACT.Copy).then_inc(ax_free[0], 1)
            act.wait_ge(ax_full[1], aux("gate", 0, 1) + 1)
            fn(dlb[:, :], AX[:, 1, 0:ROWS], ACT.Copy).then_inc(ax_free[1], 1)
            with act.Fori(0, M_HEADS - 1) as i:
                head(i, False)
            head(M_HEADS - 1, True)
            norm("norm5")

            with act.Fori(0, R_PAIRS) as i:
                for t in range(RT):
                    s = t % 2
                    act.wait_ge(pj_full[s], tile("lru", i, t) + 1)
                    act.wait_ge(l["l_xc"], from1(3 * i + t))
                    if t == 0:
                        act.wait_ge(l["l_ix"], from1(3 * i))
                        act.wait_ge(g_ready, 3 * i + GREADY["lru"])
                    fn(A[:, :], PJ[:, s, :], ACT.Copy).then_inc(pj_free[s], 1)
                    act.wait_ge(l["l_xc"], from1(3 * i + (t + 1)))
                    fn(XCh[:, t, :], B[:, :], ACT.Copy).then_inc(l["l_xchi"], 1)

                def silu(t, p):
                    act.wait_ge(pj_full[p % 2], tile("lru", i, p) + 1)
                    fn(Z3[:, t, :], PJ[:, p % 2, :], ACT.Silu).then_inc(pj_free[p % 2], 1)

                def powers(t):
                    rate = lambda twice: lra[:, ds(twice * R_TILES + 3 * i + t, 1)]
                    act.wait_ge(pj_free[t % 2], tile("lru", i, 4 + t) + 1)
                    if t == 0:
                        act.wait_ge(l["l_h"], from1(3 * i))
                    else:
                        act.wait_ge(l["l_x"], 3 * i + t)
                    fn(DEC[t], R3[:, t, :], ACT.Exp, rate(0)).then_inc(l["l_a"], 1)
                    fn(ROOT[t], R3[:, t, :], ACT.Tanh, rate(0)).then_inc(l["l_th"], 1)
                    act.wait_ge(l["l_th"], 3 * i + (t + 1))
                    act.wait_ge(l["l_a"], 3 * i + (t + 1))
                    fn(R3[:, t, :], R3[:, t, :], ACT.Exp, rate(1)).then_inc(l["l_aa"], 1)

                act.wait_ge(pj_full[1], tile("lru", i, 0))
                silu(0, 3)
                for q, (dst, bias) in enumerate(((R3, "rba"), (I3, "rbx"))):
                    if q == 1:
                        powers(0)
                    for t in range(RT):
                        p = 4 + 3 * q + t
                        act.wait_ge(pj_full[p % 2], tile("lru", i, p) + 1)
                        fn(dst[:, t, :], PJ[:, p % 2, :], ACT.Sigmoid, 1.0, v(bias, 3 * i + t)) \
                            .then_inc(pj_free[p % 2], 1)

                def root(t):
                    act.wait_ge(l["l_e"], 3 * i + (t + 1))
                    fn(ROOT[t], R3[:, t, :], ACT.Sqrt, -1.0).then_inc(l["l_sqrt"], 1)

                def high(t):
                    act.wait_ge(l["l_y"], 3 * i + (t + 1))
                    fn(G3h[:, t, :], B[:, :], ACT.Copy).then_inc(g_rounded, 1)

                for t in range(1, RT):
                    powers(t)
                for t in range(RT):
                    root(t)
                silu(1, 10)
                high(0)
                silu(2, 11)
                high(1)
                high(2)
            norm("norm6")

        @block.vector
        def _(dve):
            raise_starts(dve, "dve")
            V = nc.vector

            def tt(out, a, b, op=ALU.mult):
                return V.tensor_tensor(out, a, b, op)

            def stt(out, a, s, b, op0=ALU.mult, op1=ALU.add):
                return V.scalar_tensor_tensor(out=out, in0=a, scalar=s, in1=b, op0=op0, op1=op1)

            def lo(out, whole, hi):
                return V.tensor_tensor(out, whole, hi.bitcast(F32), ALU.subtract)

            def norm(phase):
                dve.wait_ge(rstd_ready, 2 * NORMS.index(phase) + 2)
                g = GAINS[phase]
                if phase not in UREADY:
                    for t in range(KT):
                        stt(X[:, t, :], X[:, t, :], v(g, t), Dt[:, :], ALU.mult, ALU.mult).then_inc(x_scaled, 1)
                    return
                for t in range(KT):
                    if t >= 3:
                        dve.wait_ge(*u_split(phase, t - 3))
                    stt((A, B, C)[t % 3][:, :], X[:, t, :], v(g, t), Dt[:, :], ALU.mult, ALU.mult) \
                        .then_inc(y_ready, 1)
                    for u in {1: (0,), 3: (2,), 5: (4,), 7: (6, 7)}.get(t, ()):
                        dve.wait_ge(u_rounded, UREADY[phase] + u + 1)
                        lo(Ul[:, u, :], (A, B, C)[u % 3][:, :], Uh[:, u, :]).then_inc(u_ready[0], 1)

            def add_down_tile(phase, i, p0, t):
                s = (p0 + t) % 2
                dve.wait_ge(pj_full[s], tile(phase, i, p0 + t) + 1)
                tt(X[:, t, :], PJ[:, s, :], X[:, t, :], ALU.add).then_inc(pj_free[s], 1)

            def add_down(phase, i, p0):
                for t in range(KT):
                    add_down_tile(phase, i, p0, t)

            V.memset(eps[:, :], EPS).then_inc(consts_r, 1)
            V.memset(zero[:, :], 0.0).then_inc(consts_r, 1)
            dve.wait_ge(ident_loaded, 16)
            V.tensor_copy(identr[:, :], ident[:, :]).then_inc(consts_r, 1)
            for t in range(8):
                dve.wait_ge(pj_full[t % 2], tile("read", 0, t) + 1)
                V.tensor_copy(X[:, :, t * P:(t + 1) * P], PJ[:, t % 2, :].rearrange("p (k s) -> p k s", k=KT)) \
                    .then_inc(pj_free[t % 2], 1)
            dve.wait_ge(consts, CONSTS)
            V.tensor_copy(onesr[:, :], ones[:, 0:4]).then_inc(consts_r, 1)
            norm("norm1")

            dve.wait_ge(x_spilled, 16)
            by_chunk = lambda a: a[:, :].rearrange("p (n s) -> p n s", n=NCH)
            with dve.Fori(0, RET_HEADS) as i:
                for q in range(2):
                    scale = 1.0 if q == 0 else float(P) ** -0.5
                    dve.wait_ge(pj_full[q], tile("ret", i, q) + 1)
                    dve.wait_ge(r["r_swapped"], 2 * i + (q + 1))
                    stt(B[:, :], PJ[:, q, :], scale, cos[:, :], ALU.mult, ALU.mult).then_inc(pj_free[q], 1)
                    stt(A[:, :], A[:, :], scale, sin[:, :], ALU.mult, ALU.mult).then_inc(r["r_sin"], 1)
                    dve.wait_ge(pj_free[q], tile("ret", i, q) + 1)
                    dve.wait_ge(r["r_sin"], 2 * i + (q + 1))
                    tt(B[:, :], B[:, :], A[:, :], ALU.add).then_inc(r["r_rotated"], 1)
                    dve.wait_ge(r["r_rotated"], 2 * i + (q + 1))
                    if q == 0:
                        tt(by_chunk(A), by_chunk(B), xi[:, ds(i, 1), :].broadcast_to([P, NCH, P])) \
                            .then_inc(r["r_qx"], 1)
                        dve.wait_ge(r["r_qhi"], i + 1)
                        lo(Ql[:, :], B[:, :], Qh[:, :]).then_inc(r["r_qlo"], 1)
                        dve.wait_ge(r["r_qxhi"], i + 1)
                        lo(QXl[:, :], A[:, :], QXh[:, :]).then_inc(r["r_qxlo"], 1)
                    else:
                        dve.wait_ge(r["r_khi"], i + 1)
                        lo(Kl[:, :], B[:, :], Kh[:, :]).then_inc(r["r_klo"], 1)
                dve.wait_ge(r["r_kthi"], i + 1)
                stt(Ktl[:, :], AX[:, 0, :], v("zeta", i), Kth[:, :].bitcast(F32), ALU.mult, ALU.subtract) \
                    .then_inc(ax_free[0], 1)
                dve.wait_ge(r["r_vthi"], i + 1)
                lo(Vtl[:, :], AX[:, 1, :], Vth[:, :]).then_inc(ax_free[1], 1)
                dve.wait_ge(ax_full[0], aux("ret", i, 2) + 1)
                tt(by_chunk(A), by_chunk(AX[:, 0, :]), decay[:, ds(i, 1), :].broadcast_to([P, NCH, P])) \
                    .then_inc(ax_free[0], 1)
                V.memset(B[:, 0:P], 0.0).then_inc(r["r_state"], 1)
                dve.wait_ge(ax_full[1], aux("ret", i, 3) + 1)
                for n in range(NCH - 1):
                    dve.wait_ge(r["r_state"], 7 * i + (n + 1))
                    ins = stt(B[:, (n + 1) * P:(n + 2) * P], B[:, n * P:(n + 1) * P], v("chunk_decay", i),
                              AX[:, 1, n * P:(n + 1) * P])
                    if n < NCH - 2:
                        ins.then_inc(r["r_state"], 1)
                    else:
                        ins.then_inc(ax_free[1], 1)
                dve.wait_ge(r["r_smhi"], i + 1)
                lo(SMl[:, :], A[:, :], SMh[:, :]).then_inc(r["r_smlo"], 1)
                dve.wait_ge(r["r_shi"], i + 1)
                lo(Kl[:, :], B[:, :], Kh[:, :]).then_inc(r["r_slo"], 1)
                dve.wait_ge(r["r_rstd"], i + 1)
                stt(C[:, :], C[:, :], v("rng", i), B[:, :], ALU.mult, ALU.mult).then_inc(r["r_y1"], 1)
                dve.wait_ge(r["r_y1"], i + 1)
                dve.wait_ge(pj_free[1], tile("ret", i, 3) + 1)
                tt(C[:, :], C[:, :], Dt[:, :]).then_inc(r["r_y"], 1)
                dve.wait_ge(g_rounded, i + (GREADY["ret"] + 1))
                tt(Gl[:, ds(i, 1), :].rearrange("p a s -> p (a s)"), C[:, :],
                   Gh[:, ds(i, 1), :].rearrange("p a s -> p (a s)").bitcast(F32), ALU.subtract).then_inc(g_ready, 1)
            for t in range(KT):
                if t in (0, 2, 6):
                    dve.wait_ge(x_back[(t + 2) // 4], 16)
                add_down_tile("ret_down", 0, 0, t)

            V.memset(Cp[:, 0:8], 0.0).then_inc(c["c_pad"], 1)
            dve.wait_ge(c["c_pad"], 1)
            with dve.Fori(0, 2) as i:
                for cc in range(2):
                    q = 2 * i + cc
                    p = 3 * cc + 1
                    dve.wait_ge(pj_full[p % 2], tile("conv", i, p) + 1)
                    dve.wait_ge(pj_free[(p - 1) % 2], tile("conv", i, p - 1) + 1)
                    tt(Cp[:, 8:8 + S], PJ[:, p % 2, :], B[:, :]).then_inc(pj_free[p % 2], 1)
                    dve.wait_ge(pj_free[p % 2], tile("conv", i, p) + 1)
                    V.tensor_scalar(Dt[:, :], Cp[:, 6:6 + S], v("cnw", q), None, ALU.mult).then_inc(c["c_taps"], 1)
                    dve.wait_ge(c["c_taps"], 6 * i + (3 * cc + 1))
                    stt(Dt[:, :], Cp[:, 7:7 + S], v("cnw", CONV_TILES + q), Dt[:, :]).then_inc(c["c_taps"], 1)
                    dve.wait_ge(c["c_taps"], 6 * i + (3 * cc + 2))
                    stt(Dt[:, :], Cp[:, 8:8 + S], v("cnw", 2 * CONV_TILES + q), Dt[:, :]).then_inc(c["c_taps"], 1)
                    dve.wait_ge(c["c_taps"], 6 * i + (3 * cc + 3))
                    p = 3 * cc + 2
                    dve.wait_ge(pj_full[p % 2], tile("conv", i, p) + 1)
                    tt(Dt[:, :], PJ[:, p % 2, :], Dt[:, :]).then_inc(pj_free[p % 2], 1)
                    dve.wait_ge(c["c_rstd"], 2 * i + (cc + 1))
                    dve.wait_ge(pj_free[p % 2], tile("conv", i, p) + 1)
                    stt(Dt[:, :], Dt[:, :], v("cng", q), B[:, :], ALU.mult, ALU.mult).then_inc(c["c_n"], 1)
                    dve.wait_ge(g_rounded, 2 * i + (GREADY["conv"] + cc + 1))
                    tt(Gl[:, ds(q, 1), :].rearrange("p a s -> p (a s)"), Dt[:, :],
                       Gh[:, ds(q, 1), :].rearrange("p a s -> p (a s)").bitcast(F32), ALU.subtract) \
                        .then_inc(g_ready, 1)
            add_down("conv_down", 0, 0)
            norm("norm2")

            with dve.Fori(0, FF_BLOCKS) as i:
                for k in range(5):
                    if k < 4:
                        T = (A, B)[k % 2]
                        dve.wait_ge(pj_free[k % 2], tile("ffn", i, k) + 1)
                        tt(T[:, :], T[:, :], T[:, :]).then_inc(f_sq, 1)
                    if k >= 1:
                        dve.wait_ge(g_rounded, 4 * i + (GREADY["ffn"] + k))
                        lo(Gl[:, k - 1, :], (A, B)[(k - 1) % 2][:, :], Gh[:, k - 1, :]).then_inc(g_ready, 1)
                add_down("ffn", i, 4)
            norm("norm3")
            dve.wait_ge(x_scaled, 8)
            norm("norm4")

            steps = [0]

            def step(ins):
                steps[0] += 1
                ins.then_inc(m["ga_step"], 1)
                dve.wait_ge(m["ga_step"], steps[0])

            def half_log1p(e, z, zz, out):
                step(V.tensor_scalar(z, e, 2.0, None, ALU.add))
                step(V.reciprocal(z, z))
                step(tt(z, e, z))
                step(tt(zz, z, z))
                step(V.tensor_scalar(out, zz, 1.0 / 15, None, ALU.mult))
                for n in (13, 11, 9, 7, 5, 3):
                    step(stt(out, out, 1.0 / n, zz, ALU.add, ALU.mult))
                step(stt(out, out, 1.0, z, ALU.add, ALU.mult))

            dve.wait_ge(m["lam_exp"], 1)
            half_log1p(ltmp[:, 0, :], ltmp[:, 1, :], ltmp[:, 2, :], ltmp[:, 3, :])
            step(V.tensor_scalar(ltmp[:, 1, :], v("lam", 0, R_TILES), -1.0, 0.0, ALU.mult, ALU.max))
            step(stt(ltmp[:, 2, :], ltmp[:, 3, :], 2.0, ltmp[:, 1, :]))
            for twice in range(2):
                step(V.tensor_scalar(lra[:, twice * R_TILES:(twice + 1) * R_TILES], ltmp[:, 2, :],
                                     -8.0 * (twice + 1), None, ALU.mult))
            dve.wait_ge(m["ga_exp"], 1)
            half_log1p(ga[:, :], gb[:, :], gc_[:, :], gF[:, :])
            step(V.tensor_scalar(gb[:, :], gf[:, :], 0.0, None, ALU.min))
            step(stt(gc_[:, :], gF[:, :], -2.0, gb[:, :]))
            step(V.memset(gone[:, :], 1.0))
            step(V.memset(gzero[:, :], 0.0))
            step(V.tensor_tensor_scan(gF[:, :], gone[:, :], gc_[:, :], 0.0, ALU.mult, ALU.add))
            step(tt(g5[:, 0, :], gi[:, :], gF[:, :], ALU.subtract))
            step(V.tensor_tensor_scan(gA[:, :], g5[:, 0, :], gzero[:, :], -3.0e38, ALU.max, ALU.add))
            V.tensor_copy(gcol[:, 0:1], gF[:, CHUNK - 1:CHUNK]).then_inc(m["ga_last"], 1)
            V.tensor_copy(gcol[:, 1:2], gA[:, CHUNK - 1:CHUNK]).then_inc(m["ga_last"], 1)
            V.memset(Ap[:, 0:8], 0.0).then_inc(m["m_pad"], 1)
            dve.wait_ge(m["m_pad"], 1)
            with dve.Fori(0, MT // 2) as i:
                for jj in range(2):
                    j = 2 * i + jj
                    p = 3 * jj
                    dve.wait_ge(pj_free[p % 2], tile("inner", i, p) + 1)
                    dve.wait_ge(m["m_xc"], from1(2 * i + jj))
                    V.tensor_scalar(E[:, :], Ap[:, 5:5 + S], v("mcw", j), v("mcb", j), ALU.mult, ALU.add) \
                        .then_inc(m["m_taps"], 1)
                    dve.wait_ge(m["m_taps"], 6 * i + (3 * jj + 1))
                    stt(E[:, :], Ap[:, 6:6 + S], v("mcw", MT + j), E[:, :]).then_inc(m["m_taps"], 1)
                    dve.wait_ge(m["m_taps"], 6 * i + (3 * jj + 2))
                    stt(E[:, :], Ap[:, 7:7 + S], v("mcw", 2 * MT + j), E[:, :]).then_inc(m["m_taps"], 1)
                    dve.wait_ge(m["m_taps"], 6 * i + (3 * jj + 3))
                    stt(E[:, :], Ap[:, 8:8 + S], v("mcw", 3 * MT + j), E[:, :]).then_inc(m["m_conv"], 1)
                    dve.wait_ge(pj_free[(p + 1) % 2], tile("inner", i, p + 1) + 1)
                    dve.wait_ge(m["m_xc"], from1(2 * i + (jj + 1)))
                    dve.wait_ge(m["st_zs"], from16(32 * i + 16 * jj))
                    stt(Q[:, :], Fx[:, :], v("msk", j), H[:, :], ALU.mult, ALU.mult).then_inc(m["m_zs"], 1)
                    dve.wait_ge(m["st_zn"], from16(32 * i + 16 * jj))
                    V.tensor_scalar(B[:, :], H[:, :], v("mnw", j), None, ALU.mult).then_inc(m["m_zn"], 1)

            def stage(i, u):
                dve.wait_ge(h["h_xround"], 8 * i + (u + 1))
                lo((XMl, GXl)[u // VT][:, u % VT, :], (A, B)[u % 2][:, :], (XMh, GXh)[u // VT][:, u % VT, :]) \
                    .then_inc(h["h_xsplit"], 1)

            def head(i, last):
                V.tensor_copy(hc[:, 0:5, :], cols[:, :, ds(NCH * i, NCH)])
                V.tensor_copy(hc[:, 5, :], dlb[:, ds(NCH * i, NCH)]).then_inc(h["h_hc"], 1)
                dve.wait_ge(h["h_hc"], i + 1)
                tt(by_chunk(Dt), ident[:, :].unsqueeze(1).broadcast_to([P, NCH, P]),
                   hc[:, 1, :].unsqueeze(2).broadcast_to([P, NCH, P])).then_inc(h["h_diag"], 1)
                stage(i, 4)
                stage(i, 5)
                for p in range(4):
                    dve.wait_ge(h["h_vhi"], 4 * i + (p + 1))
                    lo(Vl[:, 2 * p:2 * p + 2, :].rearrange("p a s -> p (a s)"), PJ[:, p % 2, :],
                       Vh[:, 2 * p:2 * p + 2, :].rearrange("p a s -> p (a s)")).then_inc(pj_free[p % 2], 1)
                    if p < 2:
                        stage(i, 6 + p)
                for kk in range(KK):
                    dve.wait_ge(h["h_qhi"], 2 * i + (kk + 1))
                    stt(Mql[:, kk, :], PJ[:, kk, :], DK ** -0.5, Mqh[:, kk, :].bitcast(F32), ALU.mult,
                        ALU.subtract).then_inc(pj_free[kk], 1)
                for kk in range(KK):
                    dve.wait_ge(h["h_khi"], 2 * i + (kk + 1))
                    lo(Mkl[:, kk, :], PJ[:, kk, :], Mkh[:, kk, :]).then_inc(pj_free[kk], 1)
                dve.wait_ge(ax_full[0], aux("mlstm", i, 0) + 1)
                tt(by_chunk(Dt), by_chunk(AX[:, 0, :]), hc[:, 0, :].unsqueeze(2).broadcast_to([P, NCH, P]),
                   ALU.add).then_inc(ax_free[0], 1)
                for kk in range(KK):
                    dve.wait_ge(ax_full[1 - kk], aux("mlstm", i, 1 + kk) + 1)
                    tt(by_chunk((A, B)[kk]), by_chunk(AX[:, 1 - kk, :]),
                       hc[:, 4, :].unsqueeze(2).broadcast_to([P, NCH, P])).then_inc(ax_free[1 - kk], 1)
                dve.wait_ge(h["h_w"], i + 1)
                for hf in range(2):
                    tok = slice(hf * HALF, (hf + 1) * HALF)
                    if hf == 0:
                        dve.wait_ge(h["h_s0"], i + 1)
                    else:
                        dve.wait_ge(ax_full[1], aux("mlstm", i, 3) + 1)
                    tt(Sw[:, tok], AX[:, 1, tok], Dt[:, tok]).then_inc((h["h_sw"], ax_free[1])[hf], 1)
                    dve.wait_ge(h["h_kt1hi"], 2 * i + (hf + 1))
                    lo(Mkl[:, 1, tok], B[:, tok], Mkh[:, 1, tok]).then_inc(h["h_kt1lo"], 1)
                    dve.wait_ge(h["h_smhi"], 2 * i + (hf + 1))
                    lo(Msl[:, tok], Sw[:, tok], Msh[:, tok]).then_inc(h["h_smlo"], 1)
                V.memset(Cf[:, :, :], 0.0).then_inc(h["h_c"], 1)
                for step in range(NCH + 2):
                    if 1 <= step < NCH:
                        n = step - 1
                        dve.wait_ge(h["h_cu"], 7 * i + step)
                        dve.wait_ge(h["h_clo0"], NCH * i + step)
                        dve.wait_ge(h["h_clo1"], NCH * i + step)
                        stt(Cf[:, :, 0:DV], Cf[:, :, 0:DV], hc[:, 5, n:n + 1],
                            AX[:, 0, :].rearrange("p (k a) -> p k a", k=KK))
                        stt(Cf[:, :, DV:DV + 2], Cf[:, :, DV:DV + 2], hc[:, 5, n:n + 1],
                            AX[:, 1, HALF:HALF + 4].rearrange("p (k a) -> p k a", k=KK)).then_inc(h["h_c"], 1)
                    if 1 <= step <= NCH:
                        n = step - 1
                        g = NCH * i + n
                        dve.wait_ge(h["h_qc"], from1(g + 1))
                        V.tensor_scalar(dcol[:, 0:1], AX[:, 1, 0:1], hc[:, 2, n:n + 1], AX[:, 1, 2:3], ALU.mult,
                                        ALU.add).then_inc(h["h_den"], 1)
                        dve.wait_ge(h["h_den"], from1(g + 1))
                        V.tensor_scalar(dcol[:, 3:4], dcol[:, 0:1], -1.0, hc[:, 3, n:n + 1], ALU.mult,
                                        ALU.max).then_inc(h["h_dsteps"], 1)
                        dve.wait_ge(h["h_t1"], from1(g + 1))
                        dve.wait_ge(h["h_sv"], g + 1)
                        tt(num[:, :], PJ[:, 0, DV:2 * DV], t1[:, :], ALU.add).then_inc(h["h_num"], 1)
                        dve.wait_ge(h["h_dsteps"], 3 * g + 1)
                        tt(dcol[:, 1:2], dcol[:, 0:1], dcol[:, 3:4], ALU.max).then_inc(h["h_dsteps"], 1)
                        dve.wait_ge(h["h_dsteps"], 3 * g + 2)
                        V.reciprocal(dcol[:, 2:3], dcol[:, 1:2]).then_inc(h["h_dsteps"], 1)
                        dve.wait_ge(h["h_oT"], from1(g + 1))
                        dve.wait_ge(h["h_num"], from1(g + 1))
                        dve.wait_ge(h["h_dsteps"], 3 * g + 3)
                        dve.wait_ge(h["h_hnT"], from1(g))
                        stt(hh[:, :], num[:, :], dcol[:, 2:3], PJ[:, 1, 0:DV], ALU.mult, ALU.mult) \
                            .then_inc(h["h_hh"], 1)
                        dve.wait_ge(h["h_hh"], from1(g + 1))
                        V.bn_stats(bst[:, 0:6], hh[:, :]).then_inc(h["h_st"], 1)
                        dve.wait_ge(h["h_st"], g + 1)
                        V.memset(dcol[:, 7:8], 0.0)
                        V.bn_aggr(mst[:, 0:2], bst[:, 0:6]).then_inc(h["h_st2"], 1)
                    if step < NCH:
                        g = NCH * i + step
                        dve.wait_ge(h["h_chi"], g + 1)
                        lo(Cl[:, 0, :], Cf[:, 0, :], Ch[:, 0, :]).then_inc(h["h_clo0"], 1)
                    if step >= 2:
                        g = NCH * i + (step - 2)
                        dve.wait_ge(h["h_hnT"], from1(g + 1))
                        dve.wait_ge(h["h_znc"], 16 * g + 16)
                        dve.wait_ge(h["h_done"], from1(g))
                        tt(yy[:, :], PJ[:, 1, DV:2 * DV], znc[:, :, :].rearrange("p t s -> p (t s)")) \
                            .then_inc(h["h_y1"], 1)
                    if 1 <= step <= NCH:
                        g = NCH * i + (step - 1)
                        dve.wait_ge(h["h_std"], g + 1)
                        V.reciprocal(mst[:, 3:4], mst[:, 2:3]).then_inc(h["h_rs"], 1)
                        dve.wait_ge(h["h_rs"], g + 1)
                        V.tensor_scalar(hh[:, :], hh[:, :], mst[:, 0:1], mst[:, 3:4], ALU.subtract, ALU.mult) \
                            .then_inc(h["h_hn"], 1)
                for t in range(KT):
                    add_down_tile("mlstm", i, 8, t)
                    if t % 2 == 0 and not last:
                        stage(i + 1, t // 2)

            dve.wait_ge(m["ga_lastback"], 48)
            V.memset(sc4[:, 2, 0:1], 0.0).then_inc(m["ga_m"], 1)
            V.tensor_tensor_scan(sc4[:, 2, 1:NCH + 1], sc4[:, 1, 0:NCH], sc4[:, 0, 0:NCH], 0.0,
                                 ALU.max, ALU.add).then_inc(m["ga_m"], 1)
            for name in ("st_xc", "st_zs", "st_o"):
                dve.wait_ge(m[name], from16(16 * MT))
            stage(0, 0)
            stage(0, 1)
            dve.wait_ge(m["ga_mback"], 32)
            step(V.tensor_scalar(gM[:, :], gA[:, :], gcol[:, 2:3], None, ALU.max))
            step(tt(gb[:, :], gF[:, :], gM[:, :], ALU.add))
            V.tensor_scalar(gcol[:, 3:4], gM[:, CHUNK - 1:CHUNK], -1.0, None, ALU.mult).then_inc(m["ga_rows"], 1)
            V.tensor_scalar(g5[:, 1, :], gM[:, :], -1.0, None, ALU.mult).then_inc(m["ga_rows"], 1)
            stage(0, 2)
            stage(0, 3)
            dve.wait_ge(m["ga_exps"], 1)
            V.tensor_scalar(gdiag[:, :], ident[0:ROWS, 0:ROWS], g5[:, 2, CHUNK - 1:CHUNK], None, ALU.mult) \
                .then_inc(m["ga_dl"], 1)
            for s in range(2):
                dve.wait_ge(ax_free[s], aux("gate", 0, s) + 1)
            with dve.Fori(0, M_HEADS - 1) as i:
                head(i, False)
            head(M_HEADS - 1, True)
            norm("norm5")

            V.memset(Ap[:, 0:8], 0.0).then_inc(l["l_pad"], 1)
            dve.wait_ge(l["l_pad"], 1)
            with dve.Fori(0, R_PAIRS) as i:
                for t in range(RT):
                    j = 3 * i + t
                    dve.wait_ge(pj_free[t % 2], tile("lru", i, t) + 1)
                    dve.wait_ge(l["l_xclo"], from1(3 * i + t))
                    V.tensor_scalar(B[:, :], Ap[:, 5:5 + S], v("rcw", j), v("rcb", j), ALU.mult, ALU.add) \
                        .then_inc(l["l_taps"], 1)
                    dve.wait_ge(l["l_taps"], 9 * i + (3 * t + 1))
                    stt(B[:, :], Ap[:, 6:6 + S], v("rcw", R_TILES + j), B[:, :]).then_inc(l["l_taps"], 1)
                    dve.wait_ge(l["l_taps"], 9 * i + (3 * t + 2))
                    stt(B[:, :], Ap[:, 7:7 + S], v("rcw", 2 * R_TILES + j), B[:, :]).then_inc(l["l_taps"], 1)
                    dve.wait_ge(l["l_taps"], 9 * i + (3 * t + 3))
                    stt(B[:, :], Ap[:, 8:8 + S], v("rcw", 3 * R_TILES + j), B[:, :]).then_inc(l["l_xc"], 1)
                    dve.wait_ge(l["l_xchi"], 3 * i + (t + 1))
                    lo(XCl[:, t, :], B[:, :], XCh[:, t, :]).then_inc(l["l_xclo"], 1)

                def minus_rest(t):
                    dve.wait_ge(l["l_aa"], 3 * i + (t + 1))
                    stt(R3[:, t, :], R3[:, t, :], 1.0, ROOT[t], ALU.add, ALU.mult).then_inc(l["l_e"], 1)

                def low(t):
                    dve.wait_ge(g_rounded, 3 * i + (GREADY["lru"] + t + 1))
                    lo(G3l[:, t, :], B[:, :], G3h[:, t, :]).then_inc(g_ready, 1)

                for t in range(RT):
                    minus_rest(t)
                for t in range(RT):
                    dve.wait_ge(l["l_sqrt"], 3 * i + (t + 1))
                    dve.wait_ge(l["l_ix"], from1(3 * i + (t + 1)))
                    if t:
                        dve.wait_ge(g_ready, 3 * i + (GREADY["lru"] + t))
                    tt(B[:, :], I3[:, t, :], ROOT[t]).then_inc(l["l_bt"], 1)
                    dve.wait_ge(l["l_bt"], 3 * i + (t + 1))
                    V.tensor_tensor_scan(R3[:, t, :], DEC[t], B[:, :], 0.0, ALU.mult, ALU.add) \
                        .then_inc(l["l_h"], 1)
                    p = (3, 10, 11)[t]
                    dve.wait_ge(l["l_h"], from1(3 * i + (t + 1)))
                    dve.wait_ge(pj_free[p % 2], tile("lru", i, p) + 1)
                    tt(B[:, :], Z3[:, t, :], R3[:, t, :]).then_inc(l["l_y"], 1)
                    low(t)
                add_down("lru", i, 12)
            dve.wait_ge(r6_root, 1)
            V.reciprocal(rcol[:, 1, :], rcol[:, 0, :]).then_inc(r6_ready, 1)
            dve.wait_ge(r6_ready, 1)
            dve.wait_ge(gain6_loaded, 16)
            for t in range(8):
                dve.wait_ge(pj_full[t % 2], tile("write", 0, t) + 1)
                stt(XT[:, t, :], PJ[:, t % 2, :], rcol[:, 1, 2 * t:2 * t + 1], gain6[:, :], ALU.mult, ALU.mult) \
                    .then_inc(pj_free[t % 2], 1)


def kernel(**inputs):
    import numpy as np
    import concourse.bacc as bacc
    from concourse.bass_utils import run_bass_kernel_spmd

    arrays = {k: np.asarray(v) for k, v in inputs.items()}
    f32 = np.float32

    def columns(a):
        a = np.asarray(a)
        n = a.shape[-1] // P
        return a.reshape(-1, n, P).transpose(2, 0, 1).reshape(P, -1)

    def gate_weight(w):
        full = np.zeros((R_PAIRS, RT * P, RT * P), f32)
        n = w.shape[-1]
        for b in range(2):
            full[:, b * n:(b + 1) * n, b * n:(b + 1) * n] = w[b::2]
        out = np.zeros((R_PAIRS, P, 8, P), f32)
        for q, (k, m) in enumerate(GATE_TILES):
            out[:, :, q, :] = full[:, k * P:(k + 1) * P, m * P:(m + 1) * P]
        return out.reshape(R_PAIRS, P, 8 * P)

    idx = np.arange(CHUNK, dtype=f32)
    log_gamma = np.log(f32(1.0) - f32(2.0) ** (f32(-5.0) - np.arange(RET_HEADS, dtype=f32))).astype(f32)
    diff = idx[None, :] - idx[:, None]
    decay = np.where(diff[None] >= 0, np.exp(log_gamma[:, None, None] * np.maximum(diff, 0)[None]), 0)
    zeta = np.exp(log_gamma[:, None] * (CHUNK - 1 - idx)[None])
    xi = np.exp(log_gamma[:, None] * (idx + 1)[None])
    half = P // 2
    inv_freq = (f32(1.0) / (f32(10000.0) ** (np.arange(half, dtype=f32) / f32(half)))).astype(f32)
    ang = inv_freq[:, None] * np.arange(S, dtype=f32)[None]
    cos, sin = np.cos(ang), np.sin(ang)
    const = {
        "ident": np.eye(P),
        "ones": np.ones((P, P)),
        "group64": np.kron(np.eye(2), np.ones((64, 64))),
        "cos": np.concatenate([cos, cos]),
        "sin": np.concatenate([-sin, sin]),
        "decay": decay.transpose(1, 0, 2),
        "xi": np.broadcast_to(xi[None], (P, RET_HEADS, P)),
        "negmask": np.where(diff >= 0, 0.0, -1e30),
    }
    vectors = {
        "n1g": arrays["norm1_g"], "n2g": arrays["norm2_g"], "n3g": arrays["final_norm_g"],
        "n4g": arrays["ln_g_2"][0], "n5g": arrays["ln_g_2"][1], 
        "cnw": arrays["conv_w"], "cng": arrays["conv_norm_g"], "rng": arrays["ret_norm_g"],
        "mcw": arrays["m_conv_w_2"][0], "mcb": arrays["m_conv_b_2"][0], "mnw": arrays["m_norm_w_2"][0],
        "msk": arrays["m_skip_2"][0], "rcw": arrays["r_conv_w_2"][0], "rcb": arrays["r_conv_b_2"][0],
        "rba": arrays["r_b_a_2"][0], "rbx": arrays["r_b_x_2"][0], "lam": arrays["r_lam_2"][0],
    }
    packed = {k: columns(a) for k, a in vectors.items()}
    packed["zeta"] = zeta.T
    packed["chunk_decay"] = np.broadcast_to(np.exp(log_gamma * CHUNK)[None], (P, RET_HEADS))
    feeds = {k: np.ascontiguousarray(a, dtype=f32) for k, a in const.items()}
    feeds |= {
        "x": arrays["x"][0], "gain6": np.broadcast_to(arrays["final_g_2"], (P, D)),
        "w_in": arrays["w_in"], "w_out": arrays["w_out"], "w_up": arrays["w_up"],
        "w_down": arrays["w_down"], "m_w_in": arrays["m_w_in_2"][0],
        "m_w_q": arrays["m_w_q_2"][0].reshape(M_INNER, DK), "m_w_k": arrays["m_w_k_2"][0].reshape(M_INNER, DK),
        "m_w_v": arrays["m_w_v_2"][0].reshape(M_INNER, DV), "m_w_out": arrays["m_w_out_2"][0],
        "r_w_in": arrays["r_w_in_2"][0], "r_w_out": arrays["r_w_out_2"][0],
        "gate_a": gate_weight(arrays["r_w_a_2"][0]), "gate_x": gate_weight(arrays["r_w_x_2"][0]),
        "mbif": np.concatenate([arrays["m_b_i_2"][0], arrays["m_b_f_2"][0]])[:, None],
        "vec": np.concatenate([packed[k] for k, _ in VEC], 1),
    }
    feeds = {k: np.ascontiguousarray(a) for k, a in feeds.items()}
    nc = bacc.Bacc("TRN2", target_bir_lowering=False, num_devices=1)
    d = {k: nc.dram_tensor(k, a.shape, mybir.dt.from_np(a.dtype), kind="ExternalInput").ap()
         for k, a in feeds.items()}
    d["out"] = nc.dram_tensor("out", (S, D), F32, kind="ExternalOutput").ap()
    build(nc, d)
    got = run_bass_kernel_spmd(nc, [feeds], core_ids=[0])
    return np.asarray(got.results[0]["out"]).reshape(1, S, D)
```
